# Optimizing a Trainium2 kernel written in Bass

```python
import math
import jax, jax.numpy as jnp
from jax import lax
import numpy as np

D_MODEL = 1024
BATCH = 1
SEQ = 512
DEPTH = 2

GRID_W = 64
CTX_LEN = 256
N_MIXERS = 3
BLOCK = 128
ROPE_BASE = 10000.0
RMS_EPS = 1e-6
N_MOD = 6

A_HEADS = 8
A_KV_HEADS = 2
A_GROUP = A_HEADS // A_KV_HEADS
A_HEAD_DIM = D_MODEL // A_HEADS
A_WINDOW = 128
A_SCALE = A_HEAD_DIM ** -0.5
A_QKV = (A_HEADS + 2 * A_KV_HEADS) * A_HEAD_DIM

B_WIDTH = D_MODEL
B_BLOCKS = 4
B_BLOCK_W = B_WIDTH // B_BLOCKS
B_CONV_W = 4
B_CONV_PAD_L = (B_CONV_W - 1) // 2
B_LRU_C = 8.0

C_HEADS = 8
C_NOPE = 128
C_ROPE = 64
C_VDIM = 128
C_Q_RANK = D_MODEL // 2
C_KV_RANK = D_MODEL // 4
C_SCALE = (C_NOPE + C_ROPE) ** -0.5
C_IN = C_Q_RANK + C_KV_RANK + C_ROPE

FFN_HIDDEN = ((8 * D_MODEL + 3 * 256 - 1) // (3 * 256)) * 256

kernel_name = 'hybrid_dit_swa_rglru_mla_interleaved'

def rms_norm(x, g):
    xf = x.astype(jnp.float32)
    y = xf * lax.rsqrt(jnp.mean(xf * xf, axis=-1, keepdims=True) + RMS_EPS)
    return (y * g.astype(jnp.float32)).astype(x.dtype)

def modulate(h, shift, scale):
    return h * (1 + scale) + shift

def axial_rope_tables(n_tokens, d_rot):
    n_rows = n_tokens // GRID_W
    row = jnp.repeat(jnp.arange(n_rows), GRID_W).astype(jnp.float32)
    col = jnp.tile(jnp.arange(GRID_W), n_rows).astype(jnp.float32)
    d_axis = d_rot // 2
    inv = 1.0 / (ROPE_BASE ** (jnp.arange(0, d_axis, 2, dtype=jnp.float32) / d_axis))
    ang = jnp.stack([row[:, None] * inv, col[:, None] * inv], axis=1)
    return jnp.cos(ang), jnp.sin(ang)

def apply_axial_rope(x, cos, sin):
    shp = x.shape
    xf = x.astype(jnp.float32).reshape(shp[:-1] + (2, 2, shp[-1] // 4))
    x1 = xf[..., 0, :]
    x2 = xf[..., 1, :]
    c = cos[None, :, None]
    s = sin[None, :, None]
    out = jnp.stack([x1 * c - x2 * s, x2 * c + x1 * s], axis=-2)
    return out.reshape(shp).astype(x.dtype)

def swiglu(h, w_gu, w_down):
    z = h @ w_gu
    return (jax.nn.silu(z[..., :FFN_HIDDEN]) * z[..., FFN_HIDDEN:]) @ w_down

def windowed_gqa(h, hc, w_qkv, sinks, w_o, cos, sin, need_ctx):
    B, T, _ = h.shape
    nb = T // BLOCK
    q_w = A_HEADS * A_HEAD_DIM
    kv_w = A_KV_HEADS * A_HEAD_DIM

    def project(u):
        L = u.shape[1]
        z = u @ w_qkv
        q = z[..., :q_w].reshape(B, L, A_HEADS, A_HEAD_DIM)
        k = z[..., q_w:q_w + kv_w].reshape(B, L, A_KV_HEADS, A_HEAD_DIM)
        v = z[..., q_w + kv_w:].reshape(B, L, A_KV_HEADS, A_HEAD_DIM)
        return q, k, v

    q, k, v = project(h)
    q = apply_axial_rope(q, cos, sin)
    k = apply_axial_rope(k, cos, sin)
    qc, kc, vc = project(hc)
    n_ctx = kc.shape[1]
    sink = sinks.astype(jnp.float32).reshape(A_KV_HEADS, A_GROUP)

    qb = q.reshape(B, nb, BLOCK, A_KV_HEADS, A_GROUP, A_HEAD_DIM)

    def band(t):
        tp = jnp.pad(t, ((0, 0), (BLOCK, BLOCK), (0, 0), (0, 0))).reshape(B, nb + 2, BLOCK, A_KV_HEADS, A_HEAD_DIM)
        return jnp.concatenate([tp[:, :-2], tp[:, 1:-1], tp[:, 2:]], axis=2)

    kw = band(k)
    vw = band(v)
    blk = jnp.arange(nb)[:, None, None]
    qpos = blk * BLOCK + jnp.arange(BLOCK)[None, :, None]
    kpos = (blk - 1) * BLOCK + jnp.arange(3 * BLOCK)[None, None, :]
    valid = (jnp.abs(kpos - qpos) <= A_WINDOW) & (kpos >= 0) & (kpos < T)
    s_win = jnp.einsum('bnqkgd,bnjkd->bnkgqj', qb, kw).astype(jnp.float32) * A_SCALE
    s_win = jnp.where(valid[None, :, None, None], s_win, -jnp.inf)
    s_ctx = jnp.einsum('bnqkgd,bckd->bnkgqc', qb, kc).astype(jnp.float32) * A_SCALE
    s_sink = jnp.broadcast_to(sink[None, None, :, :, None, None], s_ctx.shape[:-1] + (1,))
    p = jax.nn.softmax(jnp.concatenate([s_sink, s_ctx, s_win], axis=-1), axis=-1).astype(v.dtype)
    o = (jnp.einsum('bnkgqc,bckd->bnqkgd', p[..., 1:1 + n_ctx], vc)
         + jnp.einsum('bnkgqj,bnjkd->bnqkgd', p[..., 1 + n_ctx:], vw))
    y = o.reshape(B, T, q_w) @ w_o

    if need_ctx:
        qcg = qc.reshape(B, n_ctx, A_KV_HEADS, A_GROUP, A_HEAD_DIM)
        sc = jnp.einsum('bqkgd,bckd->bkgqc', qcg, kc).astype(jnp.float32) * A_SCALE
        ss = jnp.broadcast_to(sink[None, :, :, None, None], sc.shape[:-1] + (1,))
        pc = jax.nn.softmax(jnp.concatenate([ss, sc], axis=-1), axis=-1)[..., 1:].astype(vc.dtype)
        yc = jnp.einsum('bkgqc,bckd->bqkgd', pc, vc).reshape(B, n_ctx, q_w) @ w_o
    else:
        yc = None
    return y, yc

def centred_depthwise_conv(u, w, b):
    T = u.shape[1]
    up = jnp.pad(u, ((0, 0), (B_CONV_PAD_L, B_CONV_W - 1 - B_CONV_PAD_L), (0, 0)))
    return b + sum(w[k] * up[:, k:k + T] for k in range(B_CONV_W))

def block_diag(u, w):
    ub = u.reshape(u.shape[0], u.shape[1], B_BLOCKS, B_BLOCK_W)
    return jnp.einsum('btnk,nkj->btnj', ub, w).reshape(u.shape)

def rglru_coeffs(u, lam, w_a, b_a, w_x, b_x):
    uf = u.astype(jnp.float32)
    r = jax.nn.sigmoid(block_diag(uf, w_a.astype(jnp.float32)) + b_a.astype(jnp.float32))
    i = jax.nn.sigmoid(block_diag(uf, w_x.astype(jnp.float32)) + b_x.astype(jnp.float32))
    log_a = -B_LRU_C * r * jax.nn.softplus(-lam.astype(jnp.float32))
    a = jnp.exp(log_a)
    b = jnp.sqrt(-jnp.expm1(2.0 * log_a)) * (i * uf)
    return a, b

def linear_scan(a, b, h0, reverse):
    if reverse:
        a = jnp.flip(a, 1)
        b = jnp.flip(b, 1)

    def combine(l, r):
        return (l[0] * r[0], r[0] * l[1] + r[1])

    acc_a, acc_b = lax.associative_scan(combine, (a, b), axis=1)
    h = acc_a * h0[:, None, :] + acc_b
    return jnp.flip(h, 1) if reverse else h

def rglru_block(h, hc, w_in, conv_w, conv_b, lam, w_a, b_a, w_x, b_x, w_out, need_ctx):
    B = h.shape[0]

    def branches(u):
        z = u @ w_in
        return centred_depthwise_conv(z[..., :B_WIDTH], conv_w, conv_b), jax.nn.gelu(z[..., B_WIDTH:])

    xb, gate = branches(h)
    xbc, gatec = branches(hc)
    h_sum = 0.0
    hc_sum = 0.0
    for d, reverse in enumerate((False, True)):
        a_c, b_c = rglru_coeffs(xbc, lam[d], w_a[d], b_a[d], w_x[d], b_x[d])
        hs_c = linear_scan(a_c, b_c, jnp.zeros((B, B_WIDTH), jnp.float32), reverse)
        h0 = hs_c[:, 0] if reverse else hs_c[:, -1]
        a_l, b_l = rglru_coeffs(xb, lam[d], w_a[d], b_a[d], w_x[d], b_x[d])
        h_sum = h_sum + linear_scan(a_l, b_l, h0, reverse)
        if need_ctx:
            hc_sum = hc_sum + hs_c
    y = (h_sum.astype(h.dtype) * gate) @ w_out
    yc = (hc_sum.astype(h.dtype) * gatec) @ w_out if need_ctx else None
    return y, yc

def mla(h, hc, w_in, g_q, g_kv, w_uq, w_ukv, w_out, cos, sin, need_ctx):
    B, T, _ = h.shape
    w_ukv3 = w_ukv.reshape(C_KV_RANK, C_HEADS, C_NOPE + C_VDIM)
    w_uk = w_ukv3[..., :C_NOPE]
    w_uv = w_ukv3[..., C_NOPE:]

    def project(u, rotate):
        L = u.shape[1]
        z = u @ w_in
        cq = rms_norm(z[..., :C_Q_RANK], g_q)
        ckv = rms_norm(z[..., C_Q_RANK:C_Q_RANK + C_KV_RANK], g_kv)
        kr = z[..., C_Q_RANK + C_KV_RANK:].reshape(B, L, 1, C_ROPE)
        q = (cq @ w_uq).reshape(B, L, C_HEADS, C_NOPE + C_ROPE)
        qn, qr = q[..., :C_NOPE], q[..., C_NOPE:]
        if rotate:
            qr = apply_axial_rope(qr, cos, sin)
            kr = apply_axial_rope(kr, cos, sin)
        kn = jnp.einsum('blc,chn->blhn', ckv, w_uk)
        v = jnp.einsum('blc,chv->blhv', ckv, w_uv)
        return qn, qr, kn, kr[:, :, 0], v

    qn, qr, kn, kr, v = project(h, True)
    qnc, qrc, knc, krc, vc = project(hc, False)
    kn_all = jnp.concatenate([knc, kn], axis=1)
    kr_all = jnp.concatenate([krc, kr], axis=1)
    v_all = jnp.concatenate([vc, v], axis=1)

    def attend(qn_b, qr_b, kn_, kr_, v_):
        s = (jnp.einsum('bqhn,bkhn->bhqk', qn_b, kn_)
             + jnp.einsum('bqhr,bkr->bhqk', qr_b, kr_)).astype(jnp.float32) * C_SCALE
        p = jax.nn.softmax(s, axis=-1).astype(v_.dtype)
        return jnp.einsum('bhqk,bkhv->bqhv', p, v_)

    nb = T // BLOCK

    def to_blocks(t):
        return jnp.moveaxis(t.reshape((B, nb, BLOCK) + t.shape[2:]), 1, 0)

    o = lax.map(lambda qs: attend(qs[0], qs[1], kn_all, kr_all, v_all), (to_blocks(qn), to_blocks(qr)))
    o = jnp.moveaxis(o, 0, 1).reshape(B, T, C_HEADS * C_VDIM)
    y = o @ w_out
    if need_ctx:
        yc = attend(qnc, qrc, knc, krc, vc).reshape(B, qnc.shape[1], C_HEADS * C_VDIM) @ w_out
    else:
        yc = None
    return y, yc

def setup_inputs(seed: int = 0) -> dict:
    key = jax.random.key(seed)
    ks = iter(jax.random.split(key, 40))
    f32 = jnp.float32
    n_a = (DEPTH + N_MIXERS - 1) // N_MIXERS
    n_b = (DEPTH + N_MIXERS - 2) // N_MIXERS
    n_c = DEPTH // N_MIXERS

    def nrm(shape, fan_in, gain=1.0):
        return gain * fan_in ** -0.5 * jax.random.normal(next(ks), shape, f32)

    def small(shape, s):
        return s * jax.random.normal(next(ks), shape, f32)

    def gains(shape):
        return 1.0 + 0.05 * jax.random.normal(next(ks), shape, f32)

    x = jax.random.normal(next(ks), (BATCH, SEQ, D_MODEL), f32)
    c = jax.random.normal(next(ks), (BATCH, D_MODEL), f32)
    ctx = jax.random.normal(next(ks), (BATCH, CTX_LEN, D_MODEL), f32)
    c_ctx = jax.random.normal(next(ks), (D_MODEL,), f32)

    ada_w = nrm((DEPTH, D_MODEL, N_MOD * D_MODEL), D_MODEL, 0.5)
    ada_b = small((DEPTH, N_MOD * D_MODEL), 0.02)
    norm_g = gains((DEPTH, 4, D_MODEL))
    ffn_w_gu = nrm((DEPTH, D_MODEL, 2 * FFN_HIDDEN), D_MODEL)
    ffn_w_down = nrm((DEPTH, FFN_HIDDEN, D_MODEL), FFN_HIDDEN)

    a_w_qkv = nrm((n_a, D_MODEL, A_QKV), D_MODEL)
    a_sinks = small((n_a, A_HEADS), 1.0)
    a_w_o = nrm((n_a, A_HEADS * A_HEAD_DIM, D_MODEL), A_HEADS * A_HEAD_DIM)

    b_w_in = nrm((n_b, D_MODEL, 2 * B_WIDTH), D_MODEL)
    b_conv_w = nrm((n_b, B_CONV_W, B_WIDTH), B_CONV_W)
    b_conv_b = small((n_b, B_WIDTH), 0.02)
    a_pow = jax.random.uniform(next(ks), (n_b, 2, B_WIDTH), f32, minval=0.9, maxval=0.999)
    p_lam = a_pow ** (1.0 / B_LRU_C)
    b_lam = jnp.log(p_lam) - jnp.log1p(-p_lam)
    b_w_a = nrm((n_b, 2, B_BLOCKS, B_BLOCK_W, B_BLOCK_W), B_BLOCK_W)
    b_b_a = small((n_b, 2, B_WIDTH), 0.1)
    b_w_x = nrm((n_b, 2, B_BLOCKS, B_BLOCK_W, B_BLOCK_W), B_BLOCK_W)
    b_b_x = small((n_b, 2, B_WIDTH), 0.1)
    b_w_out = nrm((n_b, B_WIDTH, D_MODEL), B_WIDTH)

    c_w_in = nrm((n_c, D_MODEL, C_IN), D_MODEL)
    c_g_q = gains((n_c, C_Q_RANK))
    c_g_kv = gains((n_c, C_KV_RANK))
    c_w_uq = nrm((n_c, C_Q_RANK, C_HEADS * (C_NOPE + C_ROPE)), C_Q_RANK)
    c_w_ukv = nrm((n_c, C_KV_RANK, C_HEADS * (C_NOPE + C_VDIM)), C_KV_RANK)
    c_w_out = nrm((n_c, C_HEADS * C_VDIM, D_MODEL), C_HEADS * C_VDIM)

    return {'x': x, 'c': c, 'ctx': ctx, 'c_ctx': c_ctx,
            'ada_w': ada_w, 'ada_b': ada_b, 'norm_g': norm_g,
            'ffn_w_gu': ffn_w_gu, 'ffn_w_down': ffn_w_down,
            'a_w_qkv': a_w_qkv, 'a_sinks': a_sinks, 'a_w_o': a_w_o,
            'b_w_in': b_w_in, 'b_conv_w': b_conv_w, 'b_conv_b': b_conv_b, 'b_lam': b_lam,
            'b_w_a': b_w_a, 'b_b_a': b_b_a, 'b_w_x': b_w_x, 'b_b_x': b_b_x, 'b_w_out': b_w_out,
            'c_w_in': c_w_in, 'c_g_q': c_g_q, 'c_g_kv': c_g_kv, 'c_w_uq': c_w_uq,
            'c_w_ukv': c_w_ukv, 'c_w_out': c_w_out}

def reference(x, c, ctx, c_ctx, ada_w, ada_b, norm_g, ffn_w_gu, ffn_w_down,
              a_w_qkv, a_sinks, a_w_o,
              b_w_in, b_conv_w, b_conv_b, b_lam, b_w_a, b_b_a, b_w_x, b_b_x, b_w_out,
              c_w_in, c_g_q, c_g_kv, c_w_uq, c_w_ukv, c_w_out):
    n_tok = x.shape[1]
    cos_a, sin_a = axial_rope_tables(n_tok, A_HEAD_DIM)
    cos_c, sin_c = axial_rope_tables(n_tok, C_ROPE)
    s_lat = jax.nn.silu(c)
    s_ctx = jax.nn.silu(c_ctx)[None]
    xc = ctx
    for i in range(DEPTH):
        last = i == DEPTH - 1
        kind, j = i % N_MIXERS, i // N_MIXERS
        m = jnp.split((s_lat @ ada_w[i] + ada_b[i])[:, None, :], N_MOD, axis=-1)
        mc = jnp.split((s_ctx @ ada_w[i] + ada_b[i])[:, None, :], N_MOD, axis=-1)
        g = norm_g[i]
        h = modulate(rms_norm(x, g[0]), m[0], m[1])
        hc = modulate(rms_norm(xc, g[0]), mc[0], mc[1])
        if kind == 0:
            y, yc = windowed_gqa(h, hc, a_w_qkv[j], a_sinks[j], a_w_o[j], cos_a, sin_a, not last)
        elif kind == 1:
            y, yc = rglru_block(h, hc, b_w_in[j], b_conv_w[j], b_conv_b[j], b_lam[j], b_w_a[j], b_b_a[j],
                                b_w_x[j], b_b_x[j], b_w_out[j], not last)
        else:
            y, yc = mla(h, hc, c_w_in[j], c_g_q[j], c_g_kv[j], c_w_uq[j], c_w_ukv[j], c_w_out[j],
                        cos_c, sin_c, not last)
        x = x + m[2] * rms_norm(y, g[1])
        x = x + m[5] * rms_norm(swiglu(modulate(rms_norm(x, g[2]), m[3], m[4]), ffn_w_gu[i], ffn_w_down[i]), g[3])
        if not last:
            xc = xc + mc[2] * rms_norm(yc, g[1])
            xc = xc + mc[5] * rms_norm(swiglu(modulate(rms_norm(xc, g[2]), mc[3], mc[4]), ffn_w_gu[i], ffn_w_down[i]), g[3])
    return x


_drawn_inputs = setup_inputs


def setup_inputs(seed=0):
    import zlib

    import numpy as np

    out = dict(_drawn_inputs(seed))
    spreads = {}
    factors = {'a_sinks': 8.0, 'b_conv_b': 3.936, 'b_b_a': 8.0, 'b_b_x': 7.061}
    for name, (base, spread) in spreads.items():
        noise = np.random.default_rng([zlib.crc32(name.encode()), seed]).standard_normal(out[name].shape)
        drawn = base * np.exp(spread * noise) if base else spread * noise
        out[name] = __import__('jax').numpy.asarray(drawn.astype(out[name].dtype))
    for name, factor in factors.items():
        out[name] = (out[name] * factor).astype(out[name].dtype)
    return out
```

```python
from contextlib import ExitStack

import numpy as np

import concourse.bass as bass
from concourse import mybir

F = mybir.dt.float32
R = mybir.dt.float32r
ALU = mybir.AluOpType
ACT = mybir.ActivationFunctionType
AX = mybir.AxisListType.X

P = 128
D = 1024
KT = D // P
SEQ, CTX = 512, 256
TOK = CTX + SEQ
TT = TOK // P
CT = CTX // P
HID = 2816
HT = HID // P
HEADS, KVH, GROUP = 8, 2, 4
SCALE = float(P) ** -0.5
EPS = 1e-6
CH = 1024
RING = 3
HALF = 512
NEG = -1.0e30
GRID_W, ROPE_BASE = 64, 10000.0
NBLK = 4

C_G, C_CW, C_CB, C_LAM, C_BA, C_BX, NCOL = 0, 32, 64, 72, 88, 104, 120


def plan():
    order = [(("ada", c), 4) for c in range(4)]
    for j in range(12):
        order.append((("qkv", j), 1))
        if j < 8:
            order.append((("ada", 4 + j), 4))
    order += [(("o", j), 1) for j in range(8)]
    order.append((("ffn", 0), 3 * HT))
    order += [(("ada", 12 + c), 4) for c in range(4)]
    for n in range(NBLK):
        order += [(("in", n, j), 1) for j in range(4)]
        for d in range(2):
            order += [(("bd", n, d), 1), (("ada", 16 + 2 * n + d), 4)]
    order += [(("out", j), 1) for j in range(8)]
    order.append((("ffn", 1), 3 * HT))
    at, n = {}, 0
    for key, count in order:
        at[key] = n
        n += count
    return order, at, n


ORDER, AT, CHUNKS = plan()


def landed_table():
    count, got = [0] * RING, []
    for key, number in ORDER:
        for _ in range(number):
            n = len(got)
            count[n % RING] += 32 if key[0] == "bd" else 16
            got.append(count[n % RING])
    return got


LANDED = landed_table()

NORMS = [(0, 0, range(0, TT)), (0, 1, range(0, TT)), (1, 0, range(0, TT)), (1, 1, range(CT, TT))]
UPDATES = [(0, 0, range(0, TT)), (0, 1, range(0, TT)), (1, 0, range(CT, TT)), (1, 1, range(CT, TT))]
NORM_ROW0 = [0, 6, 12, 18]
NORM_GRP = [[(0, 2), (2, 6)], [(0, 2), (2, 6)], [(0, 2), (2, 6)], [(2, 6)]]
NORM_TR0 = [0, 16, 32, 48]
UPD0 = [0, 6, 12, 16]

UNITS = [(t, g, 0, 0) for t in range(CT) for g in range(KVH)]
for t in range(CT, TT):
    w0, w1 = max(t - 1, CT), min(t + 1, TT - 1)
    UNITS += [(t, g, w0, w1 - w0 + 1) for g in range(KVH)]
KTS = [list(range(CT)) + list(range(w0, w0 + nw)) for _, _, w0, nw in UNITS]
PT0 = [sum(len(k) for k in KTS[:u]) for u in range(len(UNITS) + 1)]
NCU = CT * KVH


def trunk(nc, x_in, c_in, ctx_in, cctx_in, ada_w, ada_b, norm_g, w_gu, w_down, w_qkv, sinks, w_o,
          b_w_in, conv_w, conv_b, lam, w_a, b_a, w_x, b_x, b_w_out,
          rope_c, rope_s, win_mask, eye, sel, sel_c, out):
    with ExitStack() as st:
        def sem(name):
            return st.enter_context(nc.semaphore(name))

        def sb(name, shape, dt=F):
            return st.enter_context(nc.sbuf_tensor(name, shape, dt))

        x = sb("x", [P, TT, D])
        hi = sb("hT_hi", [P, KT, TOK], R)
        lo = sb("hT_lo", [P, KT, TOK], R)
        raw = sb("w_raw", [P, RING, CH])
        whi = sb("w_hi", [P, RING, CH], R)
        wlo = sb("w_lo", [P, RING, CH], R)
        gate = sb("gate_rows", [P, 2, 2, D])
        ident = sb("ident", [P, P])
        selb = sb("sel_rows", [5, 2, P])
        selc = sb("sel_cols", [5, 2])
        s4 = sb("silu_parts", [P, KT, P], R)
        silu_c = sb("silu_c", [P, 2, KT])
        stage = sb("stage_rows", [NCOL, P])
        stage_c = sb("stage_c", [16, P])
        cols = sb("cols", [P, NCOL])
        mod = sb("mod_cols", [P, 2, 4, KT, 2])
        modrow = sb("mod_rows", [5, 2, HALF])
        stat = sb("stat", [P, 3, TT])
        ustat = sb("ustat", [P, 3, TT])
        mhalf = sb("minus_half", [P, 1])
        dec = sb("decay", [P, 2, 16])
        sp = sb("sp_work", [P, 5, 16])
        nsink = sb("neg_sinks", [P, HEADS])
        snk = sb("sinks_bc", [P, HEADS])
        smx = sb("row_max", [P, 2, GROUP])
        snm = sb("neg_max", [P, 2, GROUP])
        ssum = sb("row_sum", [P, 2, GROUP])
        ses = sb("sink_exp", [P, 2, GROUP])
        sri = sb("row_inv", [P, 2, GROUP])

        a0 = (nc.sbuf_base + 63) // 64 * 64
        K = 1024

        def ar(name, off, shape, dt=F):
            return nc.alloc_sbuf_tensor_at(name, shape, dt, offset=a0 + off)

        y = ar("y", 0, [P, TT, D])
        hrow = ar("h_rows", 24 * K, [P, TT, D])
        ntmp = ar("norm_tmp", 48 * K, [P, 2, HALF])
        junk = ar("square_out", 62 * K, [P, D])
        qT = ar("qT", 0, [P, HEADS, TOK])
        kT = ar("kT", 24 * K, [P, KVH, TOK])
        V = ar("V", 30 * K, [P, TT, 2 * P])
        qraw = ar("q_raw", 36 * K, [P, TT, HALF])
        qrot = ar("q_rot", 48 * K, [P, TT - CT, HALF])
        rc = ar("rope_cos", 56 * K, [P, TT - CT, P])
        rs = ar("rope_sin", 58 * K, [P, TT - CT, P])
        rtmp = ar("rope_tmp", 60 * K, [P, 2, HALF])
        S = ar("scores", 36 * K, [P, 2, GROUP, 5 * P])
        PT = ar("probsT", 56 * K, [P, 5, GROUP * P])
        mask = ar("mask", 66 * K, [P, 3 * P])
        ahi = ar("act_hi", 24 * K, [P, 2, 2, TOK], R)
        alo = ar("act_lo", 36 * K, [P, 2, 2, TOK], R)
        sg = ar("act", 48 * K, [P, 2, TOK])
        u = ar("conv_out", 0, [P, 2, TOK])
        uhi = ar("conv_hi", 6 * K, [P, 2, TOK], R)
        ulo = ar("conv_lo", 12 * K, [P, 2, TOK], R)
        hsum = ar("h_sum", 18 * K, [P, 2, SEQ])
        z = ar("z", 24 * K, [P, KT, SEQ])
        rr = ar("gate_r", 40 * K, [P, 2, TOK])
        ii = ar("gate_i", 46 * K, [P, 2, TOK])
        aa = ar("lru_a", 52 * K, [P, 2, TOK])
        a2 = ar("lru_a2", 58 * K, [P, TOK])
        gl = ar("gelu", 61 * K, [P, 2, SEQ])
        assert a0 + 68 * K <= nc.sbuf_usable_end

        ps = st.enter_context(nc.psum_tensor("ps", [P, 8, HALF], F))

        raw_landed = [sem(f"raw_landed{i}") for i in range(RING)]
        x_landed = [sem(f"x_landed{i}") for i in range(TT)]
        c_landed, cols_landed, rope_landed = sem("c_landed"), sem("cols_landed"), sem("rope_landed")
        gate_landed = [sem("gates0_landed"), sem("mixer_gate1_landed"), sem("ffn_gate1_landed")]
        sel_landed, att_landed = sem("sel_landed"), sem("att_landed")
        bias_landed = [sem("bias_landed0"), sem("bias_landed1")]
        w_hi, w_lo, w_used = sem("w_hi_ready"), sem("w_lo_ready"), sem("w_used")
        zeroed, start_tr, silu_done, s4_done, cols_done = (
            sem("zeroed"), sem("start_tr"), sem("silu_done"), sem("s4_done"), sem("cols_done"))
        sp_act, sp_dve = sem("sp_act"), sem("sp_dve")
        row_moved, ada_out, ada_done, ada_step = sem("row_moved"), sem("ada_out"), sem("ada_done"), sem("ada_step")
        n_ssq, n_mean, n_rstd, n_row = sem("n_ssq"), sem("n_mean"), sem("n_rstd"), sem("n_row")
        n_tr, n_hi, n_tmp, n_lo = sem("n_tr"), sem("n_hi"), sem("n_tmp"), sem("n_lo")
        u_ssq, u_mean, u_rstd, u_scaled, x_added = (
            sem("u_ssq"), sem("u_mean"), sem("u_rstd"), sem("u_scaled"), sem("x_added"))
        qkv_moved, rope_mul, rope_done, qk_tr, qk_moved = (
            sem("qkv_moved"), sem("rope_mul"), sem("rope_done"), sem("qk_tr"), sem("qk_moved"))
        s_mm, s_ctx, s_win, s_max, s_neg, s_exp, s_den, s_inv, s_prob = (
            sem("s_mm"), sem("s_ctx"), sem("s_win"), sem("s_max"), sem("s_neg"), sem("s_exp"),
            sem("s_den"), sem("s_inv"), sem("s_prob"))
        p_tr, p_moved, pv_mm, o_hi, o_lo = sem("p_tr"), sem("p_moved"), sem("pv_mm"), sem("o_hi"), sem("o_lo")
        y_moved = sem("y_moved")
        silu_r, prod_r, ahi_r, alo_r, down_mm, down_add = [], [], [], [], [], []
        for i in range(2):
            silu_r.append(sem(f"silu_ready{i}"))
            prod_r.append(sem(f"prod_ready{i}"))
            ahi_r.append(sem(f"act_hi_ready{i}"))
            alo_r.append(sem(f"act_lo_ready{i}"))
            down_mm.append(sem(f"down_mm{i}"))
            down_add.append(sem(f"down_added{i}"))
        in_act, conv, u_hi, u_lo = sem("in_act"), sem("conv"), sem("u_hi"), sem("u_lo")
        bd_mm, sig, decay_exp, tanh_r, a_sq, iu_r, v_r, sqrt_r, b_r, scan_r, h_r, z_r, z_hi, z_lo = (
            sem("bd_mm"), sem("sigmoid"), sem("decay_exp"), sem("tanh_r"), sem("a_sq"), sem("iu_r"),
            sem("v_r"), sem("sqrt_r"), sem("b_r"), sem("scan_r"), sem("h_r"), sem("z_r"),
            sem("z_hi"), sem("z_lo"))
        out_sent = sem("out_sent")

        def landed_value(n, v=0):
            return LANDED[n] + v * (16 * 12 // RING)

        def gu_src(li, q, up):
            s = w_gu[li].rearrange("(k p) n -> p k n", p=P)
            return s[:, :, bass.ts(q + (HT if up else 0), P)]

        def down_src(li, q):
            return w_down[li][bass.ts(q, P), :]

        block = st.enter_context(nc.Block())

        @block.sync
        def _(eng):
            def load(n, src, dst=None, v=0):
                if n >= RING:
                    eng.wait_ge(w_lo, n - RING + 1 + v * 12)
                to = raw[:, n % RING, :] if dst is None else dst(raw[:, n % RING, :])
                eng.dma_start(to, src).then_inc(raw_landed[n % RING], 16)

            def two_by(dst):
                return dst.rearrange("p (k n) -> p k n", k=2)

            def load_cols512(n, w, j, cc):
                load(n, w[2 * j * P:(2 * j + 2) * P, cc * HALF:(cc + 1) * HALF].rearrange("(k p) n -> p k n", p=P), two_by)

            def eight_by(dst):
                return dst.rearrange("p (k n) -> p k n", k=KT)

            def load_ada(a):
                li, c = a // 12, a % 12
                if a >= 2:
                    eng.wait_ge(ada_out, a - 1)
                eng.dma_start(modrow[4:5, a % 2, :], ada_b[li:li + 1, c * HALF:(c + 1) * HALF]).then_inc(bias_landed[a % 2], 16)
                for j in range(4):
                    load_cols512(AT["ada", a] + j, ada_w[li], j, c)

            def load_gate_gain(li, m, v):
                g = norm_g[li, 2 * m + 1:2 * m + 2, :].to_broadcast((P, D))
                eng.dma_start(gate[:, m, v, :], g).then_inc(gate_landed[li + li * m], 16)

            def load_ffn(li):
                b = AT["ffn", li]

                def gu(n, q, v=0):
                    for t in range(2):
                        load(n + 2 * t, gu_src(li, q + t, False), eight_by, v)
                        load(n + 2 * t + 1, gu_src(li, q + t, True), eight_by, v)

                def down(n, q, v=0):
                    for t in range(2):
                        load(n + t, down_src(li, q + t), None, v)

                gu(b, 0)
                with eng.Fori(0, 5) as v:
                    for s in range(2):
                        gu(b + 4 + 6 * s, 4 * v + 2 + 2 * s, v)
                        down(b + 8 + 6 * s, 4 * v + 2 * s, v)
                down(b + 64, HT - 2)

            eng.dma_start(stage_c[0:8, :], c_in.rearrange("a (t p) -> (a t) p", p=P)).then_inc(c_landed, 16)
            eng.dma_start(stage_c[8:16, :], cctx_in.rearrange("(t p) -> t p", p=P)).then_inc(c_landed, 16)
            eng.dma_start(ident[:, :], eye).then_inc(c_landed, 16)
            eng.dma_start(selb[:, :, :], sel).then_inc(sel_landed, 16)
            eng.dma_start(selc[:, :], sel_c).then_inc(sel_landed, 16)
            gate_loads = [(0, m, v) for m in range(2) for v in range(2)]
            for key, count in ORDER:
                n = AT[key]
                if key[0] == "ada":
                    a = key[1]
                    if a == 4:
                        for g in gate_loads:
                            load_gate_gain(*g)
                    if a in (16, 22):
                        eng.wait_ge(x_added, UPD0[2])
                        load_gate_gain(1, (a - 16) // 6, 0)
                    load_ada(a)
                elif key[0] == "qkv":
                    load_cols512(n, w_qkv[0], key[1] % 4, key[1] // 4)
                    if key[1] == 0:
                        eng.dma_start(rc[:, :, :], rope_c).then_inc(rope_landed, 16)
                        eng.dma_start(rs[:, :, :], rope_s).then_inc(rope_landed, 16)
                        eng.dma_start(mask[:, :], win_mask).then_inc(att_landed, 16)
                        eng.dma_start(snk[:, :], sinks[0:1, :].to_broadcast((P, HEADS))).then_inc(att_landed, 16)
                elif key[0] == "o":
                    load_cols512(n, w_o[0], key[1] % 4, key[1] // 4)
                elif key[0] == "out":
                    load_cols512(n, b_w_out[0], key[1] % 4, key[1] // 4)
                elif key[0] == "in":
                    _, b, j = key
                    m = 2 * b + j if j < 2 else KT + 2 * b + j - 2
                    load(n, b_w_in[0].rearrange("(k p) n -> p k n", p=P)[:, :, m * P:(m + 1) * P], eight_by)
                elif key[0] == "bd":
                    _, b, d = key
                    eng.wait_ge(w_lo, n - RING + 1)
                    slot = raw[:, n % RING, :].rearrange("p (g k n) -> p g k n", g=2, k=2)
                    for g, w in enumerate((w_a, w_x)):
                        eng.dma_start(slot[:, g], w[0, d, b].rearrange("(k p) n -> p k n", p=P)).then_inc(raw_landed[n % RING], 16)
                else:
                    load_ffn(key[1])
            for i, t in enumerate(range(CT, TT)):
                eng.wait_ge(x_added, UPD0[3] + i + 1)
                eng.dma_start(out[0, (t - CT) * P:(t - CT + 1) * P, :], x[:, t, :]).then_inc(out_sent, 16)
            eng.wait_ge(out_sent, 16 * (TT - CT))

        @block.scalar
        def _(eng):
            done = [0]
            last_square = []

            def split(n, v=0):
                eng.wait_ge(raw_landed[n % RING], landed_value(n, v))
                if n >= RING:
                    eng.wait_ge(w_used, n - RING + 1 + v * 12)
                eng.activation(whi[:, n % RING, :], raw[:, n % RING, :], ACT.Copy).then_inc(w_hi, 1)

            def splits_to(end):
                while done[0] < min(end, CHUNKS):
                    split(done[0])
                    done[0] += 1

            def ada_row(a):
                n = AT["ada", a] + 3
                splits_to(n + 3)
                eng.wait_ge(w_used, n + 1)
                if a >= 2:
                    eng.wait_ge(ada_out, a - 1)
                eng.activation(modrow[0:4, a % 2, :], ps[0:4, 6, :], ACT.Copy).then_inc(row_moved, 1)

            def square(src, dst, signal, number):
                if last_square:
                    eng.wait_ge(*last_square[-1])
                eng.activation(junk[:, :], src, ACT.Square, accum_out=dst).then_inc(signal, 1)
                last_square.append((signal, number + 1))

            def norm_square(k, i):
                t = NORMS[k][2][i]
                if k == 0:
                    eng.wait_ge(x_landed[t], 16)
                else:
                    eng.wait_ge(x_added, UPD0[k - 1] + i + 1)
                square(x[:, t, :], stat[:, 0, t:t + 1], n_ssq, NORM_ROW0[k] + i)

            def update_square(k, i, ready):
                t = UPDATES[k][2][i]
                ready(i)
                square(y[:, t, :], ustat[:, 0, t:t + 1], u_ssq, UPD0[k] + i)

            def norm_hi(k):
                seq = NORM_TR0[k]
                for t0, t1 in NORM_GRP[k]:
                    for ct in range(KT):
                        eng.wait_ge(n_tmp, seq + 1)
                        eng.activation(hi[:, ct, t0 * P:t1 * P], ntmp[:, seq % 2, 0:(t1 - t0) * P], ACT.Copy).then_inc(n_hi, 1)
                        seq += 1

            def update_norm(ku, kn, ready, between=lambda i: None):
                n = len(UPDATES[ku][2])
                for i in range(n + 4):
                    if i < n:
                        update_square(ku, i, ready)
                    if kn is not None and 0 <= i - 2 < n:
                        norm_square(kn, i - 2)
                    between(i)

            def ffn(li):
                b = AT["ffn", li]
                hw = 384 if li == 0 else HALF
                w = TOK if li == 0 else SEQ

                def gated(n0, q, t, v):
                    eng.wait_ge(w_used, n0 + 2 + 2 * t + v * 12)
                    if not isinstance(q, int) or q >= 2:
                        eng.wait_ge(alo_r[li], q - 1)
                    if li == 0:
                        g, o = ps[:, 4 * t:4 * t + 2, 0:hw], sg[:, t, 0:w].rearrange("p (h w) -> p h w", h=2)
                    else:
                        g, o = ps[:, 4 * t, 0:hw], sg[:, t, 0:w]
                    eng.activation(o, g, ACT.Silu).then_inc(silu_r[li], 1)
                    eng.wait_ge(prod_r[li], q + 1)

                def gated_hi(q, t, par):
                    eng.activation(ahi[:, par, t, 0:w], sg[:, t, 0:w], ACT.Copy).then_inc(ahi_r[li], 1)

                def step(n0, i, par, v):
                    for k in range(1, 5):
                        split(n0 + k, v)
                    gated(n0, 2 * i, 0, v)
                    gated_hi(2 * i, 0, par)
                    split(n0 + 5, v)
                    split(n0 + 6, v)
                    gated(n0, 2 * i + 1, 1, v)
                    gated_hi(2 * i + 1, 1, par)

                splits_to(b + 5)
                gated(b, 0, 0, 0)
                gated_hi(0, 0, 0)
                gated(b, 1, 1, 0)
                gated_hi(1, 1, 0)
                with eng.Fori(0, 5) as v:
                    for s in range(2):
                        step(b + 4 + 6 * s, 1 + s + 2 * v, (1 + s) % 2, v)
                done[0] = b + 65
                splits_to(b + 66)

            for t in range(TT):
                src = ctx_in[0, t * P:(t + 1) * P, :] if t < CT else x_in[0, (t - CT) * P:(t - CT + 1) * P, :]
                eng.dma_start(x[:, t, :], src).then_inc(x_landed[t], 16)
            pieces = [(C_G + 8 * (2 * li + wh), norm_g[li, 2 * wh:2 * wh + 1, :], 8) for li in range(2) for wh in range(2)]
            pieces += [(C_CW, conv_w[0], 32), (C_CB, conv_b, 8), (C_LAM, lam[0], 16), (C_BA, b_a[0], 16), (C_BX, b_x[0], 16)]
            for row, src, n in pieces:
                eng.dma_start(stage[row:row + n, :], src.rearrange("a (t p) -> (a t) p", p=P)).then_inc(cols_landed, 16)
            eng.wait_ge(start_tr, 1)
            eng.activation(silu_c[:, :, :], ps[:, 7, 0:16].rearrange("p (v k) -> p v k", v=2), ACT.Silu).then_inc(silu_done, 1)
            splits_to(3)
            eng.wait_ge(sp_dve, 2)
            eng.activation(sp[:, 1, :], sp[:, 0, :], ACT.Exp, scale=-1.0).then_inc(sp_act, 1)
            for a in range(2):
                ada_row(a)
            for i in range(TT):
                norm_square(0, i)
            for a in range(2, 4):
                ada_row(a)
            norm_hi(0)

            def qkv_move(cc):
                n = AT["qkv", 4 * cc + 3]
                splits_to(n + 3)
                eng.wait_ge(w_used, n + 1)
                if cc:
                    eng.wait_ge(qk_tr, 6 * cc)
                    eng.wait_ge(rope_mul, 12 * cc)
                for t in range(TT):
                    w = HALF if cc < 2 else 2 * P
                    eng.activation(qraw[:, t, 0:w], ps[:, t, 0:w], ACT.Copy).then_inc(qkv_moved, 1)
                    if cc == 2:
                        eng.activation(V[:, t, :], ps[:, t, w:HALF], ACT.Copy).then_inc(qkv_moved, 1)

            def qk_move(cc):
                nh = 4 if cc < 2 else 2
                for t in range(TT):
                    s = 6 * cc + t
                    eng.wait_ge(qk_tr, s + 1)
                    dst = qT[:, 4 * cc:4 * cc + 4, t * P:(t + 1) * P] if cc < 2 else kT[:, :, t * P:(t + 1) * P]
                    src = ps[:, 6 + s % 2, 0:nh * P].rearrange("p (h q) -> p h q", h=nh)
                    eng.activation(dst, src, ACT.Copy).then_inc(qk_moved, 1)

            for j in range(12):
                if j % 4 == 3:
                    qkv_move(j // 4)
                if j < 8:
                    ada_row(4 + j)
                if j in (5, 9):
                    qk_move((j - 5) // 4)
            splits_to(AT["o", 0] + 3)
            qk_move(2)

            def ctx_move(u, p):
                eng.wait_ge(s_mm, 2 * u + p + 1)
                if u >= 2:
                    eng.wait_ge(p_tr, PT0[u - 1])
                eng.activation(S[:, u % 2, 2 * p:2 * p + 2, 0:CTX],
                               ps[:, 3 * p, :].rearrange("p (h k) -> p h k", h=2), ACT.Copy).then_inc(s_ctx, 1)

            ctx_move(0, 0)
            ctx_move(0, 1)
            for un, (t, g, w0, nw) in enumerate(UNITS):
                b, nk = un % 2, CTX + nw * P
                eng.wait_ge(s_neg, 2 * (un + 1))
                for h in range(GROUP):
                    eng.activation(S[:, b, h, 0:nk], S[:, b, h, 0:nk], ACT.Exp, bias=snm[:, b, h:h + 1],
                                   scale=SCALE, accum_out=ssum[:, b, h:h + 1]).then_inc(s_exp, 1)
                eng.activation(ses[:, b, :], ses[:, b, :], ACT.Exp).then_inc(s_exp, 1)
                for i in range(len(KTS[un])):
                    eng.wait_ge(p_tr, PT0[un] + i + 1)
                    if un:
                        eng.wait_ge(pv_mm, PT0[un])
                    eng.activation(PT[:, i, :], ps[:, 6, :], ACT.Copy).then_inc(p_moved, 1)
                    if i < 2 and un + 1 < len(UNITS):
                        ctx_move(un + 1, i)
                eng.wait_ge(pv_mm, PT0[un + 1])
                eng.activation(hi[:, 4 * g:4 * g + 4, t * P:(t + 1) * P],
                               ps[:, 7, :].rearrange("p (h q) -> p h q", h=4), ACT.Copy).then_inc(o_hi, 1)

            for half in range(2):
                n = AT["o", 4 * half + 3]
                splits_to(n + 3)
                eng.wait_ge(w_used, n + 1)
                for i in range(TT):
                    o = 6 * half + i
                    eng.activation(y[:, i, half * HALF:(half + 1) * HALF], ps[:, o % 8, :], ACT.Copy).then_inc(y_moved, 1)

            update_norm(0, 1, lambda i: eng.wait_ge(y_moved, 6 + i + 1))
            splits_to(AT["ffn", 0] + 3)
            norm_hi(1)
            ffn(0)

            def ada_between(i):
                if i in (1, 3, 5, 7):
                    ada_row(12 + i // 2)

            update_norm(1, 2, lambda i: eng.wait_ge(down_add[0], 12 * (HT // 2 - 1) + 2 * i + 3), ada_between)
            norm_hi(2)

            for n in range(NBLK):
                for j in range(2):
                    c, q = AT["in", n, j], 2 * n + j
                    splits_to(c + 3)
                    eng.wait_ge(w_used, c + 1)
                    if n:
                        eng.wait_ge(iu_r, 4 * n)
                        eng.wait_ge(u_lo, 2 * n)
                    w1, cb = cols[:, C_CW + 8 + q:C_CW + 9 + q], cols[:, C_CB + q:C_CB + q + 1]
                    eng.activation(u[:, j, 0:CTX], ps[:, 2 * j, 0:CTX], ACT.Identity, bias=cb, scale=w1).then_inc(in_act, 1)
                    eng.activation(u[:, j, CTX:TOK], ps[:, 2 * j + 1, :], ACT.Identity, bias=cb, scale=w1).then_inc(in_act, 1)
                for j in range(2):
                    eng.wait_ge(conv, 6 * (2 * n + j + 1))
                    if n:
                        eng.wait_ge(w_used, AT["bd", n - 1, 1] + 1)
                    eng.activation(uhi[:, j, :], u[:, j, :], ACT.Copy).then_inc(u_hi, 1)
                for j in range(2):
                    c = AT["in", n, 2 + j]
                    splits_to(c + 3)
                    eng.wait_ge(w_used, c + 1)
                    if n:
                        eng.wait_ge(z_r, 2 * n)
                    eng.activation(gl[:, j, :], ps[:, j, :], ACT.Gelu_apprx_tanh).then_inc(in_act, 1)
                for d in range(2):
                    c, e = AT["bd", n, d], 2 * n + d
                    splits_to(c + 3)
                    for m in range(2):
                        for g, (dst, col) in enumerate(((rr, C_BA), (ii, C_BX))):
                            s = 2 * m + g
                            if s < 3:
                                eng.wait_ge(bd_mm, 3 * e + s + 1)
                            else:
                                eng.wait_ge(w_used, c + 1)
                            if e:
                                eng.wait_ge(scan_r, 4 * e)
                                eng.wait_ge(h_r, 2 * n)
                            bias = cols[:, col + 8 * d + 2 * n + m:col + 8 * d + 2 * n + m + 1]
                            eng.activation(dst[:, m, :].rearrange("p (h w) -> p h w", h=2), ps[:, 2 + 2 * g:4 + 2 * g, 0:384],
                                           ACT.Sigmoid, bias=bias).then_inc(sig, 1)
                    for m in range(2):
                        k = 8 * d + 2 * n + m
                        eng.wait_ge(sig, 4 * e + 2 * m + 1)
                        eng.activation(aa[:, m, :], rr[:, m, :], ACT.Exp, scale=dec[:, 0, k:k + 1]).then_inc(decay_exp, 1)
                        eng.wait_ge(decay_exp, 2 * e + m + 1)
                        eng.activation(rr[:, m, :], rr[:, m, :], ACT.Tanh, scale=dec[:, 1, k:k + 1]).then_inc(tanh_r, 1)
                    ada_row(16 + e)
                    for m in range(2):
                        eng.wait_ge(v_r, 2 * e + m + 1)
                        eng.activation(rr[:, m, :], rr[:, m, :], ACT.Sqrt).then_inc(sqrt_r, 1)
            splits_to(AT["out", 0] + 3)
            for ct in range(KT):
                eng.wait_ge(z_r, ct + 1)
                eng.activation(hi[:, ct, CTX:TOK], z[:, ct, :], ACT.Copy).then_inc(z_hi, 1)
            for half in range(2):
                n = AT["out", 4 * half + 3]
                splits_to(n + 3)
                eng.wait_ge(w_used, n + 1)
                for i in range(4):
                    eng.activation(y[:, CT + i, half * HALF:(half + 1) * HALF], ps[:, 4 * half + i, :], ACT.Copy).then_inc(y_moved, 1)
            update_norm(2, 3, lambda i: eng.wait_ge(y_moved, 12 + 4 + i + 1))
            splits_to(AT["ffn", 1] + 3)
            norm_hi(3)
            ffn(1)
            update_norm(3, None, lambda i: eng.wait_ge(down_add[1], 8 * (HT // 2 - 1) + 2 * i + 3))

        @block.vector
        def _(eng):
            done = [0]

            def split(n, v=0):
                eng.wait_ge(w_hi, n + 1 + v * 12)
                s = n % RING
                eng.tensor_tensor(wlo[:, s, :], raw[:, s, :], whi[:, s, :].bitcast(F), ALU.subtract).then_inc(w_lo, 1)

            def splits_to(end):
                while done[0] < min(end, CHUNKS):
                    split(done[0])
                    done[0] += 1

            def ada_finish(a):
                li, c = a // 12, a % 12
                m, half = c // 2, c % 2
                splits_to(AT["ada", a] + 6)
                eng.wait_ge(ada_out, a + 1)
                if m in (2, 5):
                    gm = m // 3
                    eng.wait_ge(gate_landed[li + li * gm], 64 if li == 0 else 16)
                    for v in range(2 if li == 0 else 1):
                        g = gate[:, gm, v, half * HALF:(half + 1) * HALF]
                        ins = eng.tensor_tensor(g, ps[:, 7 - v, :], g, ALU.mult)
                    ins.then_inc(ada_done, 1)
                    return
                idx = m if m < 2 else m - 1
                for v in range(2):
                    src = ps[:, 7, 0:8].rearrange("p (t v) -> p v t", v=2)[:, v, :]
                    dst = mod[:, li, idx, 4 * half:4 * half + 4, v]
                    if idx % 2 == 0:
                        ins = eng.tensor_copy(dst, src)
                    else:
                        g0 = C_G + 8 * (2 * li + idx // 2) + 4 * half
                        ins = eng.scalar_tensor_tensor(dst, src, 1.0, cols[:, g0:g0 + 4], ALU.add, ALU.mult)
                ins.then_inc(ada_done, 1)

            def mean(t, src, ssq, number, signal):
                eng.wait_ge(ssq, number + 1)
                eng.tensor_scalar(src[:, 1, t:t + 1], src[:, 0, t:t + 1], 1.0 / D, EPS, ALU.mult, ALU.add).then_inc(signal, 1)

            def norm_row(k, i):
                t = NORMS[k][2][i]
                eng.wait_ge(n_rstd, NORM_ROW0[k] + i + 1)
                eng.tensor_scalar(hrow[:, t, :], x[:, t, :], stat[:, 2, t:t + 1], None, ALU.mult).then_inc(n_row, 1)

            def update_scale(k, i):
                li, m, tiles = UPDATES[k]
                t = tiles[i]
                eng.wait_ge(u_rstd, UPD0[k] + i + 1)
                eng.scalar_tensor_tensor(y[:, t, :], y[:, t, :], ustat[:, 2, t:t + 1],
                                         gate[:, m, 1 if t < CT else 0, :], ALU.mult, ALU.mult).then_inc(u_scaled, 1)

            def update_norm(ku, kn, between=lambda i: None):
                li, m, tiles = UPDATES[ku]
                n = len(tiles)
                eng.wait_ge(ada_done, 12 * li + (6 if m == 0 else 12))
                for i in range(n + 4):
                    if i < n:
                        mean(tiles[i], ustat, u_ssq, UPD0[ku] + i, u_mean)
                    if 0 <= i - 1 < n:
                        update_scale(ku, i - 1)
                    if kn is not None and 0 <= i - 2 < n:
                        mean(tiles[i - 2], stat, n_ssq, NORM_ROW0[kn] + i - 2, n_mean)
                    if kn is not None and 0 <= i - 3 < n:
                        norm_row(kn, i - 3)
                    between(i)

            def norm_lo(k):
                li, which, _ = NORMS[k]
                eng.wait_ge(ada_done, 12 * li + (4 if which == 0 else 10))
                seq = NORM_TR0[k]
                todo = [(t0, t1, ct) for t0, t1 in NORM_GRP[k] for ct in range(KT)]

                def finish(s, t0, t1, ct):
                    eng.wait_ge(n_hi, s + 1)
                    eng.wait_ge(n_tmp, s + 1)
                    w = (t1 - t0) * P
                    eng.tensor_tensor(lo[:, ct, t0 * P:t1 * P], ntmp[:, s % 2, 0:w],
                                      hi[:, ct, t0 * P:t1 * P].bitcast(F), ALU.subtract).then_inc(n_lo, 1)

                for i, (t0, t1, ct) in enumerate(todo):
                    v, s = (1 if t0 == 0 else 0), seq + i
                    eng.wait_ge(n_tr, s + 1)
                    if s >= 2:
                        eng.wait_ge(n_lo, s - 1)
                    eng.tensor_scalar(ntmp[:, s % 2, 0:(t1 - t0) * P], ps[:, s % 4, 0:(t1 - t0) * P],
                                      mod[:, li, 2 * which + 1, ct, v:v + 1], mod[:, li, 2 * which, ct, v:v + 1],
                                      ALU.mult, ALU.add).then_inc(n_tmp, 1)
                    if i:
                        finish(s - 1, *todo[i - 1])
                finish(seq + len(todo) - 1, *todo[-1])

            def ffn(li):
                b = AT["ffn", li]
                hw = 384 if li == 0 else HALF
                w = TOK if li == 0 else SEQ
                tiles = UPDATES[2 * li + 1][2]
                nd = 2 * len(tiles)

                def product(q, t, par):
                    eng.wait_ge(silu_r[li], q + 1)
                    if li == 0:
                        s, up = sg[:, t, 0:w].rearrange("p (h w) -> p h w", h=2), ps[:, 4 * t + 2:4 * t + 4, 0:hw]
                    else:
                        s, up = sg[:, t, 0:w], ps[:, 4 * t + 2, 0:hw]
                    eng.tensor_tensor(s, s, up, ALU.mult).then_inc(prod_r[li], 1)
                    eng.wait_ge(ahi_r[li], q + 1)
                    eng.tensor_tensor(alo[:, par, t, 0:w], sg[:, t, 0:w], ahi[:, par, t, 0:w].bitcast(F),
                                      ALU.subtract).then_inc(alo_r[li], 1)

                def down_adds(j, last_chunk, v):
                    for o in range(nd):
                        if o < nd - 1:
                            eng.wait_ge(down_mm[li], (nd - 1) * j + o + 1)
                        else:
                            eng.wait_ge(w_used, last_chunk + 1 + v * 12)
                        to = y[:, tiles[o // 2], (o % 2) * HALF:(o % 2 + 1) * HALF]
                        eng.tensor_tensor(to, ps[:, o % 4, :], to, ALU.add).then_inc(down_add[li], 1)

                def step(n0, i, par, v):
                    for k in range(1, 5):
                        split(n0 + k, v)
                    product(2 * i, 0, par)
                    split(n0 + 5, v)
                    split(n0 + 6, v)
                    product(2 * i + 1, 1, par)
                    down_adds(i - 1, n0 + 5, v)

                splits_to(b + 5)
                product(0, 0, 0)
                product(1, 1, 0)
                eng.wait_ge(down_add[li], 1)
                with eng.Fori(0, 5) as v:
                    for s in range(2):
                        step(b + 4 + 6 * s, 1 + s + 2 * v, (1 + s) % 2, v)
                done[0] = b + 65
                splits_to(b + 66)
                down_adds(HT // 2 - 1, b + 65, 0)

            eng.wait_ge(silu_done, 1)
            eng.wait_ge(zeroed, 1)
            sv = silu_c[:, :, :].rearrange("p v k -> p k v")
            eng.tensor_copy(s4[:, :, 0:4:2], sv).then_inc(s4_done, 1)
            eng.wait_ge(s4_done, 1)
            eng.tensor_tensor(s4[:, :, 1:4:2], sv, s4[:, :, 0:4:2].bitcast(F), ALU.subtract).then_inc(s4_done, 1)
            splits_to(3)
            eng.wait_ge(start_tr, 2)
            eng.tensor_copy(cols[:, :], ps[:, 6, 0:NCOL]).then_inc(cols_done, 1)
            eng.wait_ge(cols_done, 1)
            step_no = [0]

            def chain(ins):
                step_no[0] += 1
                ins.then_inc(sp_dve, 1)
                eng.wait_ge(sp_dve, step_no[0])

            lamc = cols[:, C_LAM:C_LAM + 16]
            chain(eng.tensor_scalar(sp[:, 0, :], lamc, -1.0, None, ALU.mult))
            chain(eng.tensor_tensor(sp[:, 0, :], sp[:, 0, :], lamc, ALU.max))
            for a in range(2):
                ada_finish(a)
            eng.wait_ge(sp_act, 1)
            chain(eng.tensor_scalar(sp[:, 2, :], sp[:, 1, :], 2.0, None, ALU.add))
            chain(eng.reciprocal(sp[:, 2, :], sp[:, 2, :]))
            chain(eng.tensor_tensor(sp[:, 1, :], sp[:, 1, :], sp[:, 2, :], ALU.mult))
            chain(eng.tensor_tensor(sp[:, 2, :], sp[:, 1, :], sp[:, 1, :], ALU.mult))
            chain(eng.tensor_scalar(sp[:, 3, :], sp[:, 2, :], 2.0 / 17, 2.0 / 15, ALU.mult, ALU.add))
            for k in range(13, 0, -2):
                chain(eng.tensor_tensor(sp[:, 3, :], sp[:, 3, :], sp[:, 2, :], ALU.mult))
                chain(eng.tensor_scalar(sp[:, 3, :], sp[:, 3, :], 2.0 / k, None, ALU.add))
            chain(eng.tensor_tensor(sp[:, 3, :], sp[:, 3, :], sp[:, 1, :], ALU.mult))
            chain(eng.tensor_scalar(sp[:, 4, :], lamc, -1.0, 0.0, ALU.mult, ALU.max))
            chain(eng.tensor_tensor(sp[:, 4, :], sp[:, 4, :], sp[:, 3, :], ALU.add))
            chain(eng.tensor_scalar(dec[:, 0, :], sp[:, 4, :], -8.0, None, ALU.mult))
            chain(eng.tensor_scalar(dec[:, 1, :], sp[:, 4, :], 8.0, None, ALU.mult))

            for i in range(TT):
                mean(i, stat, n_ssq, i, n_mean)
                if i:
                    norm_row(0, i - 1)
            norm_row(0, TT - 1)
            for a in range(2, 4):
                ada_finish(a)
            norm_lo(0)

            def rope(cc):
                nh = 4 if cc < 2 else 2
                w = nh * P
                eng.wait_ge(rope_landed, 32)
                for i in range(TT - CT):
                    r = 4 * cc + i
                    eng.wait_ge(qkv_moved, (6 * cc + CT + i + 1) if cc < 2 else 12 + 2 * (CT + i) + 1)
                    if cc:
                        eng.wait_ge(qk_tr, 6 * cc)
                    if r >= 2:
                        eng.wait_ge(rope_done, r - 1)
                    src = qraw[:, CT + i, 0:w]
                    c = rc[:, i, :].rearrange("p (o w) -> p o w", o=1).to_broadcast((P, nh, P))
                    eng.tensor_tensor(qrot[:, i, 0:w].rearrange("p (h w) -> p h w", h=nh),
                                      src.rearrange("p (h w) -> p h w", h=nh), c, ALU.mult).then_inc(rope_mul, 1)
                    sv5 = src.rearrange("p (h a s w) -> p s h a w", h=nh, a=2, s=2)
                    tv5 = rtmp[:, r % 2, 0:w].rearrange("p (h a s w) -> p s h a w", h=nh, a=2, s=2)
                    rv = rs[:, i, :].rearrange("p (a s w) -> p s a w", a=2, s=2)
                    for s in range(2):
                        sn = rv[:, s].rearrange("p (o a) w -> p o a w", o=1).to_broadcast((P, nh, 2, 32))
                        eng.tensor_tensor(tv5[:, s], sv5[:, 1 - s], sn, ALU.mult).then_inc(rope_mul, 1)

            for j in range(12):
                splits_to(AT["qkv", j] + 3)
                if j % 4 == 3:
                    rope(j // 4)
                if j < 8:
                    ada_finish(4 + j)
            splits_to(AT["o", 0] + 3)

            eng.wait_ge(att_landed, 32)
            eng.tensor_scalar(nsink[:, :], snk[:, :], -1.0, None, ALU.mult).then_inc(s_den, 1)
            eng.wait_ge(s_den, 1)

            def window_move(u, p):
                t, g, w0, nw = UNITS[u]
                if not nw:
                    return
                eng.wait_ge(s_mm, 2 * u + p + 1)
                if u >= 2:
                    eng.wait_ge(p_tr, PT0[u - 1])
                off = (w0 - t + 1) * P
                mk = mask[:, off:off + nw * P].rearrange("p (o w) -> p o w", o=1).to_broadcast((P, 2, nw * P))
                eng.tensor_tensor(S[:, u % 2, 2 * p:2 * p + 2, CTX:CTX + nw * P],
                                  ps[:, 3 * p + 1:3 * p + 3, 0:nw * P], mk, ALU.add).then_inc(s_win, 1)

            def maxima(u):
                t, g, w0, nw = UNITS[u]
                b = u % 2
                eng.wait_ge(s_ctx, 2 * (u + 1))
                if nw:
                    eng.wait_ge(s_win, 2 * (u - NCU + 1))
                eng.tensor_reduce(smx[:, b, :], S[:, b, :, 0:CTX + nw * P], AX, ALU.max).then_inc(s_max, 1)
                eng.wait_ge(s_max, u + 1)
                eng.scalar_tensor_tensor(snm[:, b, :], smx[:, b, :], -SCALE, nsink[:, 4 * g:4 * g + 4],
                                         ALU.mult, ALU.min).then_inc(s_neg, 1)
                eng.wait_ge(s_neg, 2 * u + 1)
                eng.tensor_tensor(ses[:, b, :], snk[:, 4 * g:4 * g + 4], snm[:, b, :], ALU.add).then_inc(s_neg, 1)

            maxima(0)
            for un, (t, g, w0, nw) in enumerate(UNITS):
                b, nk = un % 2, CTX + nw * P
                eng.wait_ge(s_exp, 5 * (un + 1))
                eng.tensor_tensor(ssum[:, b, :], ssum[:, b, :], ses[:, b, :], ALU.add).then_inc(s_den, 1)
                eng.wait_ge(s_den, un + 2)
                eng.reciprocal(sri[:, b, :], ssum[:, b, :]).then_inc(s_inv, 1)
                eng.wait_ge(s_inv, un + 1)
                for h in range(GROUP):
                    eng.tensor_scalar(S[:, b, h, 0:nk], S[:, b, h, 0:nk], sri[:, b, h:h + 1], None, ALU.mult).then_inc(s_prob, 1)
                if un + 1 < len(UNITS):
                    window_move(un + 1, 0)
                    window_move(un + 1, 1)
                    maxima(un + 1)
                eng.wait_ge(o_hi, un + 1)
                dst = slice(4 * g, 4 * g + 4), slice(t * P, (t + 1) * P)
                eng.tensor_tensor(lo[:, dst[0], dst[1]], ps[:, 7, :].rearrange("p (h q) -> p h q", h=4),
                                  hi[:, dst[0], dst[1]].bitcast(F), ALU.subtract).then_inc(o_lo, 1)

            for half in range(2):
                splits_to(AT["o", 4 * half + 3] + 3)
            update_norm(0, 1)
            splits_to(AT["ffn", 0] + 3)
            norm_lo(1)
            ffn(0)

            def ada_between(i):
                if i in (1, 3, 5, 7):
                    ada_finish(12 + i // 2)

            update_norm(1, 2, ada_between)
            norm_lo(2)

            def taps(n, j):
                q = 2 * n + j
                k0 = 12 * n + 6 * j
                step = 0
                for k, dt in ((0, -1), (2, 1), (3, 2)):
                    wk = cols[:, C_CW + 8 * k + q:C_CW + 8 * k + q + 1]
                    for s, (t0, t1, src) in enumerate(((0, CTX, ps[:, 2 * j, 0:CTX]), (CTX, TOK, ps[:, 2 * j + 1, :]))):
                        w = t1 - t0
                        a, e = max(0, -dt), w - max(0, dt)
                        if step < 2:
                            eng.wait_ge(in_act, 6 * n + 2 * j + s + 1)
                        else:
                            eng.wait_ge(conv, k0 + step - 1)
                        eng.scalar_tensor_tensor(u[:, j, t0 + a:t0 + e], src[:, a + dt:e + dt], wk,
                                                 u[:, j, t0 + a:t0 + e], ALU.mult, ALU.add).then_inc(conv, 1)
                        step += 1

            for n in range(NBLK):
                for j in range(2):
                    splits_to(AT["in", n, j] + 3)
                    taps(n, j)
                splits_to(AT["in", n, 2] + 3)
                for j in range(2):
                    eng.wait_ge(u_hi, 2 * n + j + 1)
                    eng.tensor_tensor(ulo[:, j, :], u[:, j, :], uhi[:, j, :].bitcast(F), ALU.subtract).then_inc(u_lo, 1)
                splits_to(AT["in", n, 3] + 3)
                for d in range(2):
                    e = 2 * n + d
                    splits_to(AT["bd", n, d] + 3)
                    for m in range(2):
                        eng.wait_ge(a_sq, 2 * e + m + 1)
                        eng.wait_ge(tanh_r, 2 * e + m + 1)
                        eng.scalar_tensor_tensor(rr[:, m, :], a2[:, :], 1.0, rr[:, m, :], ALU.add, ALU.mult).then_inc(v_r, 1)
                    ada_finish(16 + e)
                    for m in range(2):
                        s = 2 * e + m
                        eng.wait_ge(sqrt_r, s + 1)
                        eng.wait_ge(iu_r, s + 1)
                        eng.tensor_tensor(rr[:, m, :], rr[:, m, :], ii[:, m, :], ALU.mult).then_inc(b_r, 1)
                        eng.wait_ge(b_r, s + 1)
                        if d == 0:
                            eng.tensor_tensor_scan(ii[:, m, 0:CTX], aa[:, m, 0:CTX], rr[:, m, 0:CTX], 0.0,
                                                   ALU.mult, ALU.add).then_inc(scan_r, 1)
                            eng.wait_ge(scan_r, 2 * s + 1)
                            if n:
                                eng.wait_ge(z_r, 2 * n)
                            eng.tensor_tensor_scan(hsum[:, m, :], aa[:, m, CTX:TOK], rr[:, m, CTX:TOK],
                                                   ii[:, m, CTX - 1:CTX], ALU.mult, ALU.add).then_inc(scan_r, 1)
                        else:
                            eng.tensor_tensor_scan(ii[:, m, 0:CTX][:, ::-1], aa[:, m, 0:CTX][:, ::-1],
                                                   rr[:, m, 0:CTX][:, ::-1], 0.0, ALU.mult, ALU.add).then_inc(scan_r, 1)
                            eng.wait_ge(scan_r, 2 * s + 1)
                            eng.tensor_tensor_scan(ii[:, m, CTX:TOK][:, ::-1], aa[:, m, CTX:TOK][:, ::-1],
                                                   rr[:, m, CTX:TOK][:, ::-1], ii[:, m, 0:1],
                                                   ALU.mult, ALU.add).then_inc(scan_r, 1)
            splits_to(AT["out", 0] + 3)
            for ct in range(KT):
                eng.wait_ge(z_hi, ct + 1)
                eng.tensor_tensor(lo[:, ct, CTX:TOK], z[:, ct, :], hi[:, ct, CTX:TOK].bitcast(F), ALU.subtract).then_inc(z_lo, 1)
            for half in range(2):
                splits_to(AT["out", 4 * half + 3] + 3)
            update_norm(2, 3)
            splits_to(AT["ffn", 1] + 3)
            norm_lo(3)
            ffn(1)
            update_norm(3, None)

        @block.gpsimd
        def _(eng):
            def rstd(src, t, means, number, signal):
                eng.wait_ge(means, number + 1)
                eng.tensor_tensor(src[:, 2, t:t + 1], src[:, 1, t:t + 1], mhalf[:, :], ALU.pow).then_inc(signal, 1)

            def update_norm(ku, kn):
                li, m, tiles = UPDATES[ku]
                n = len(tiles)
                for i in range(n + 4):
                    if i < n:
                        rstd(ustat, tiles[i], u_mean, UPD0[ku] + i, u_rstd)
                    if 0 <= i - 1 < n:
                        t = tiles[i - 1]
                        eng.wait_ge(u_scaled, UPD0[ku] + i)
                        eng.tensor_tensor(x[:, t, :], x[:, t, :], y[:, t, :], ALU.add).then_inc(x_added, 1)
                    if kn is not None and 0 <= i - 2 < n:
                        rstd(stat, tiles[i - 2], n_mean, NORM_ROW0[kn] + i - 2, n_rstd)

            eng.memset(s4[:, :, :].bitcast(F), 0.0).then_inc(zeroed, 1)
            eng.memset(mhalf[:, :], -0.5).then_inc(zeroed, 1)
            eng.wait_ge(zeroed, 2)
            for i in range(TT):
                rstd(stat, i, n_mean, i, n_rstd)
            for cc in range(3):
                w = HALF if cc < 2 else 2 * P
                for i in range(TT - CT):
                    r = 4 * cc + i
                    eng.wait_ge(rope_mul, 3 * (r + 1))
                    eng.tensor_tensor(qrot[:, i, 0:w], qrot[:, i, 0:w], rtmp[:, r % 2, 0:w], ALU.add).then_inc(rope_done, 1)
            update_norm(0, 1)
            eng.wait_ge(x_added, UPD0[1])
            eng.memset(y[:, :, :], 0.0).then_inc(down_add[0], 1)
            update_norm(1, 2)
            for n in range(NBLK):
                for d in range(2):
                    e = 2 * n + d
                    for m in range(2):
                        s = 2 * e + m
                        eng.wait_ge(decay_exp, s + 1)
                        if s:
                            eng.wait_ge(v_r, s)
                        eng.tensor_tensor(a2[:, :], aa[:, m, :], aa[:, m, :], ALU.mult).then_inc(a_sq, 1)
                        eng.wait_ge(sig, 4 * e + 2 * m + 2)
                        eng.tensor_tensor(ii[:, m, :], ii[:, m, :], u[:, m, :], ALU.mult).then_inc(iu_r, 1)
                for m in range(2):
                    eng.wait_ge(scan_r, 8 * n + 4 + 2 * m + 2)
                    eng.tensor_tensor(hsum[:, m, :], hsum[:, m, :], ii[:, m, CTX:TOK], ALU.add).then_inc(h_r, 1)
                    eng.wait_ge(h_r, 2 * n + m + 1)
                    eng.wait_ge(in_act, 6 * n + 5 + m)
                    eng.tensor_tensor(z[:, 2 * n + m, :], hsum[:, m, :], gl[:, m, :], ALU.mult).then_inc(z_r, 1)
            update_norm(2, 3)
            eng.wait_ge(x_added, UPD0[3])
            eng.memset(y[:, CT:TT, :], 0.0).then_inc(down_add[1], 1)
            update_norm(3, None)

        @block.tensor
        def _(eng):
            def mm3(to, a_hi, a_lo, b_hi, b_lo, start, stop):
                eng.matmul(to, a_hi, b_hi, start=start, stop=False)
                eng.matmul(to, a_hi, b_lo, start=False, stop=False)
                return eng.matmul(to, a_lo, b_hi, start=False, stop=stop)

            def ready(n, v=0):
                eng.wait_ge(w_lo, n + 1 + v * 12)

            def ada(a, banks_free=lambda: None):
                li, c = a // 12, a % 12
                banks_free()
                if a:
                    eng.wait_ge(ada_done, a)
                for j in range(4):
                    n = AT["ada", a] + j
                    ready(n)
                    for kk in range(2):
                        k = 2 * j + kk
                        for part in (whi, wlo):
                            ins = eng.matmul(ps[:, 6, :], s4[:, k, :], part[:, n % RING, kk * HALF:(kk + 1) * HALF],
                                             start=(k == 0 and part is whi), stop=(k == KT - 1 and part is wlo))
                    ins.then_inc(w_used, 1)
                eng.wait_ge(row_moved, a + 1)
                eng.wait_ge(bias_landed[a % 2], 16 * (a // 2 + 1))
                if c // 2 in (2, 5):
                    for v in range(2 if li == 0 else 1):
                        ins = eng.matmul(ps[:, 7 - v, :], selb[:, v, :], modrow[:, a % 2, :], start=True, stop=True)
                else:
                    for t in range(4):
                        ins = eng.matmul(ps[:, 7, 2 * t:2 * t + 2], modrow[:, a % 2, t * P:(t + 1) * P], selc[:, :],
                                         start=True, stop=True)
                ins.then_inc(ada_out, 1)

            def norm_transposes(k):
                rows, seq = NORM_ROW0[k], NORM_TR0[k]
                for t0, t1 in NORM_GRP[k]:
                    rows += t1 - t0
                    eng.wait_ge(n_row, rows)
                    for ct in range(KT):
                        if seq >= 4:
                            eng.wait_ge(n_tmp, seq - 3)
                        for t in range(t0, t1):
                            ins = eng.transpose(ps[:, seq % 4, (t - t0) * P:(t - t0 + 1) * P],
                                                hrow[:, t, ct * P:(ct + 1) * P], ident[:, :])
                        ins.then_inc(n_tr, 1)
                        seq += 1
                eng.wait_ge(n_hi, seq)
                eng.wait_ge(n_lo, seq)

            def token_major(name, tiles, acc, bank):
                for j in acc:
                    n = AT[name, j]
                    ready(n)
                    for kk in range(2):
                        k = 2 * (j % 4) + kk
                        for i, t in enumerate(tiles):
                            bank_no = bank(j, i)
                            h_hi, h_lo = hi[:, k, t * P:(t + 1) * P], lo[:, k, t * P:(t + 1) * P]
                            w = slice(kk * HALF, (kk + 1) * HALF)
                            if k == 0:
                                yield j, i
                            ins = mm3(ps[:, bank_no, :], h_hi, h_lo, whi[:, n % RING, w], wlo[:, n % RING, w],
                                      k == 0, k == KT - 1)
                    ins.then_inc(w_used, 1)

            def channel_major(n, parts, col0=0, v=0, kts=range(KT), src=None):
                src_hi, src_lo = src if src else (hi, lo)
                for i, k in enumerate(kts):
                    w_h = whi[:, n % RING, col0 + i * P:col0 + (i + 1) * P]
                    w_l = wlo[:, n % RING, col0 + i * P:col0 + (i + 1) * P]
                    for to, tok in parts:
                        ins = mm3(to, w_h, w_l, src_hi[:, k, tok], src_lo[:, k, tok], i == 0, i == len(kts) - 1)
                return ins

            def ffn(li):
                b = AT["ffn", li]
                tiles = UPDATES[2 * li + 1][2]
                nd = 2 * len(tiles)
                cuts = [(0, 384), (384, 768)] if li == 0 else [(CTX, TOK)]

                def up(n0, i, t, v, first):
                    for s in range(2):
                        n = n0 + 2 * t + s
                        ready(n, v)
                        if s == 0 and not first:
                            if t == 0:
                                eng.wait_ge(down_add[li], nd * (i - 1) + 1)
                                eng.wait_ge(prod_r[li], 2 * i - 1)
                            else:
                                eng.wait_ge(prod_r[li], 2 * i)
                        parts = [(ps[:, 4 * t + 2 * s + k, 0:c1 - c0], slice(c0, c1)) for k, (c0, c1) in enumerate(cuts)]
                        channel_major(n, parts).then_inc(w_used, 1)

                def down(n, j, par, v):
                    ready(n + 1, v)
                    eng.wait_ge(alo_r[li], 2 * j + 2)
                    if not isinstance(j, int) or j < HT // 2 - 1:
                        eng.wait_ge(prod_r[li], 2 * j + 3)
                    for o in range(nd):
                        if o >= 4:
                            eng.wait_ge(down_add[li], nd * j + o - 2)
                        tk = slice((o // 2) * P, (o // 2 + 1) * P)
                        w = slice((o % 2) * HALF, (o % 2 + 1) * HALF)
                        for t in range(2):
                            s = (n + t) % RING
                            ins = mm3(ps[:, o % 4, :], ahi[:, par, t, tk], alo[:, par, t, tk], whi[:, s, w], wlo[:, s, w],
                                      t == 0, t == 1)
                            if o == nd - 1:
                                ins.then_inc(w_used, 1)
                        if o < nd - 1:
                            ins.then_inc(down_mm[li], 1)

                for t in range(2):
                    up(b, 0, t, 0, True)
                with eng.Fori(0, 5) as v:
                    for s in range(2):
                        n0, i = b + 4 + 6 * s, 1 + s + 2 * v
                        for t in range(2):
                            up(n0, i, t, v, False)
                        down(n0 + 4, s + 2 * v, s, v)
                eng.wait_ge(down_add[li], nd * (HT // 2 - 1) + 1)
                down(b + 64, HT // 2 - 1, 0, 0)

            eng.wait_ge(c_landed, 48)
            eng.transpose(ps[:, 7, 0:16], stage_c[:, :], ident[0:16, 0:16]).then_inc(start_tr, 1)
            eng.wait_ge(cols_landed, 16 * 9)
            eng.transpose(ps[:, 6, 0:NCOL], stage[:, :], ident[0:NCOL, 0:NCOL]).then_inc(start_tr, 1)
            eng.wait_ge(s4_done, 2)
            eng.wait_ge(sel_landed, 32)
            eng.wait_ge(cols_done, 1)
            for a in range(4):
                ada(a)
            norm_transposes(0)

            def qk_transposes(cc):
                nh = 4 if cc < 2 else 2
                eng.wait_ge(ada_done, min(12, 4 + (4 * cc + 6)))
                for t in range(TT):
                    s = 6 * cc + t
                    if t < CT:
                        eng.wait_ge(qkv_moved, 6 * cc + t + 1 if cc < 2 else 12 + 2 * t + 1)
                        src = qraw[:, t, :]
                    else:
                        eng.wait_ge(rope_done, 4 * cc + t - CT + 1)
                        src = qrot[:, t - CT, :]
                    if s >= 2:
                        eng.wait_ge(qk_moved, s - 1)
                    for h in range(nh):
                        ins = eng.transpose(ps[:, 6 + s % 2, h * P:(h + 1) * P], src[:, h * P:(h + 1) * P], ident[:, :])
                    ins.then_inc(qk_tr, 1)

            for j in range(12):
                for jj, i in token_major("qkv", range(TT), [j], lambda j, i: i):
                    if jj >= 4:
                        eng.wait_ge(qkv_moved, 6 * (jj // 4 - 1) + i + 1)
                if j < 8:
                    ada(4 + j, (lambda: eng.wait_ge(qk_moved, 6)) if j >= 6 else (lambda: None))
                if j in (5, 9):
                    qk_transposes((j - 5) // 4)
            qk_transposes(2)

            eng.wait_ge(qkv_moved, 24)
            eng.wait_ge(qk_moved, 18)

            def scores(u, p):
                t, g, w0, nw = UNITS[u]
                if u:
                    eng.wait_ge(s_ctx, 2 * (u - 1) + p + 1)
                    if u - 1 >= NCU:
                        eng.wait_ge(s_win, 2 * (u - 1 - NCU) + p + 1)
                for h2 in range(2):
                    q = qT[:, 4 * g + 2 * p + h2, t * P:(t + 1) * P]
                    ins = eng.matmul(ps[:, 3 * p, h2 * CTX:(h2 + 1) * CTX], q, kT[:, g, 0:CTX], start=True, stop=True)
                    if nw:
                        ins = eng.matmul(ps[:, 3 * p + 1 + h2, 0:nw * P], q, kT[:, g, w0 * P:(w0 + nw) * P],
                                         start=True, stop=True)
                ins.then_inc(s_mm, 1)

            scores(0, 0)
            scores(0, 1)
            for un, (t, g, w0, nw) in enumerate(UNITS):
                kts = KTS[un]

                def values(i):
                    eng.wait_ge(p_moved, PT0[un] + i + 1)
                    if i == 0 and un:
                        eng.wait_ge(o_hi, un)
                        eng.wait_ge(o_lo, un)
                    eng.matmul(ps[:, 7, :], V[:, kts[i], g * P:(g + 1) * P], PT[:, i, :],
                               start=(i == 0), stop=(i == len(kts) - 1)).then_inc(pv_mm, 1)

                eng.wait_ge(s_prob, 4 * (un + 1))
                for i in range(len(kts)):
                    if PT0[un] + i:
                        eng.wait_ge(p_moved, PT0[un] + i)
                    for h in range(GROUP):
                        ins = eng.transpose(ps[:, 6, h * P:(h + 1) * P], S[:, un % 2, h, i * P:(i + 1) * P], ident[:, :])
                    ins.then_inc(p_tr, 1)
                    if i < 2 and un + 1 < len(UNITS):
                        scores(un + 1, i)
                    if i:
                        values(i - 1)
                values(len(kts) - 1)

            eng.wait_ge(o_hi, len(UNITS))
            eng.wait_ge(o_lo, len(UNITS))
            for jj, i in token_major("o", range(TT), range(8), lambda j, i: (6 * (j // 4) + i) % 8):
                if jj >= 4 and i >= 2:
                    eng.wait_ge(y_moved, i - 1)
            norm_transposes(1)
            ffn(0)
            for a in range(12, 16):
                ada(a)
            norm_transposes(2)

            for n in range(NBLK):
                for j in range(4):
                    c = AT["in", n, j]
                    ready(c)
                    p = j % 2
                    if j == 0 and n:
                        eng.wait_ge(in_act, 6 * n)
                    if j == 1 and n:
                        eng.wait_ge(sig, 8 * n)
                    if j >= 2:
                        eng.wait_ge(conv, 12 * n + 6)
                    parts = [(ps[:, 2 * j, 0:CTX], slice(0, CTX))] if j < 2 else []
                    parts += [(ps[:, 2 * j + 1 if j < 2 else p, :], slice(CTX, TOK))]
                    channel_major(c, parts).then_inc(w_used, 1)
                eng.wait_ge(u_lo, 2 * n + 2)
                for d in range(2):
                    c, e = AT["bd", n, d], 2 * n + d
                    ready(c)
                    for m in range(2):
                        for g in range(2):
                            s = 4 * e + 2 * m + g
                            if s >= 2:
                                eng.wait_ge(sig, s - 1)
                            for k in range(2):
                                at_w = (2 * g + k) * 2 * P + m * P
                                w_h, w_l = whi[:, c % RING, at_w:at_w + P], wlo[:, c % RING, at_w:at_w + P]
                                for to, tok in ((ps[:, 2 + 2 * g, 0:384], slice(0, 384)),
                                                (ps[:, 3 + 2 * g, 0:384], slice(384, 768))):
                                    ins = mm3(to, w_h, w_l, uhi[:, k, tok], ulo[:, k, tok], k == 0, k == 1)
                            ins.then_inc(bd_mm if 2 * m + g < 3 else w_used, 1)
                    ada(16 + e)
            eng.wait_ge(z_lo, KT)
            eng.wait_ge(sig, 4 * 2 * NBLK)
            eng.wait_ge(ada_done, 24)
            for jj, i in token_major("out", range(CT, TT), range(8), lambda j, i: 4 * (j // 4) + i):
                pass
            norm_transposes(3)
            ffn(1)


_TRUNK_INS = ["x", "c", "ctx", "c_ctx", "ada_w", "ada_b", "norm_g", "ffn_w_gu", "ffn_w_down", "a_w_qkv", "a_sinks",
              "a_w_o", "b_w_in", "b_conv_w", "b_conv_b", "b_lam", "b_w_a", "b_b_a", "b_w_x", "b_b_x", "b_w_out"]


def shape_constants():
    pos = np.arange(SEQ)
    inv = (1.0 / (np.float32(ROPE_BASE) ** (np.arange(0, 64, 2, dtype=np.float32) / np.float32(64)))).astype(np.float32)
    ang = np.stack([(pos // GRID_W).astype(np.float32)[:, None] * inv, (pos % GRID_W).astype(np.float32)[:, None] * inv], 1)
    cos, sin = np.cos(ang), np.sin(ang)
    c = np.stack([cos, cos], 2).reshape(SEQ // P, P, P).transpose(1, 0, 2)
    s = np.stack([-sin, sin], 2).reshape(SEQ // P, P, P).transpose(1, 0, 2)
    i, j = np.arange(P)[:, None], np.arange(3 * P)[None, :]
    mask = np.where(np.abs(j - P - i) <= P, 0.0, NEG)
    sel = np.zeros((5, 2, P))
    sel[[0, 1, 4], 0] = 1.0
    sel[[2, 3, 4], 1] = 1.0
    made = {"rope_c": c, "rope_s": s, "win_mask": mask, "eye": np.eye(P), "sel": sel, "sel_c": sel[:, :, 0]}
    return {k: np.ascontiguousarray(v, dtype=np.float32) for k, v in made.items()}


def kernel(**inputs):
    import concourse.bacc as bacc
    from concourse.bass_utils import run_bass_kernel_spmd

    nc = bacc.Bacc("TRN2", target_bir_lowering=False, num_devices=1)
    arrays, args = {}, []
    for name in _TRUNK_INS:
        arrays[f"in_{name}"] = np.ascontiguousarray(inputs[name])
    arrays.update({f"const_{k}": v for k, v in shape_constants().items()})
    for name, a in arrays.items():
        args.append(nc.dram_tensor(name, a.shape, mybir.dt.from_np(a.dtype), kind="ExternalInput").ap())
    args.append(nc.dram_tensor("out_latents", (1, SEQ, D), F, kind="ExternalOutput").ap())
    trunk(nc, *args)
    r = run_bass_kernel_spmd(nc, [arrays], core_ids=[0])
    return r.results[0]["out_latents"]
```

```python
from contextlib import ExitStack

import numpy as np

import concourse.bass as bass
from concourse import mybir

F = mybir.dt.float32
R = mybir.dt.float32r
ALU = mybir.AluOpType
ACT = mybir.ActivationFunctionType
AX = mybir.AxisListType.X

P = 128
D = 1024
KT = D // P
SEQ, CTX = 512, 256
TOK = CTX + SEQ
TT = TOK // P
CT = CTX // P
HID = 2816
HT = HID // P
HEADS, KVH, GROUP = 8, 2, 4
SCALE = float(P) ** -0.5
EPS = 1e-6
CH = 1024
RING = 3
HALF = 512
NEG = -1.0e30
GRID_W, ROPE_BASE = 64, 10000.0
NBLK = 4

C_G, C_CW, C_CB, C_LAM, C_BA, C_BX, NCOL = 0, 32, 64, 72, 88, 104, 120


QKV_ADA = {0: (4,), 2: (5,), 4: (6,), 6: (7,), 8: (8,)}
UNIT_ADA = {0: 9, 2: 10, 4: 11}
O_ADA = {1: (12,), 3: (13,), 5: (14,), 6: (15,)}
IN_ADA = {1: 16, 3: 17}
OUT_ORDER = [(0, 0), (0, 1), (0, 2), (1, 0), (1, 1), (1, 2), (0, 3), (1, 3)]


def plan():
    order = [(("ada", c), 4) for c in range(4)]
    for j in range(12):
        order.append((("qkv", j), 1))
        order += [(("ada", a), 4) for a in QKV_ADA.get(j, ())]
    order += [(("ada", a), 4) for a in UNIT_ADA.values()]
    for j in range(8):
        order.append((("o", j), 1))
        order += [(("ada", a), 4) for a in O_ADA.get(j, ())]
    order.append((("ffn", 0), 3 * HT))
    for n in range(NBLK):
        for j in range(4):
            order.append((("in", n, j), 1))
            if j in IN_ADA:
                order.append((("ada", IN_ADA[j] + 2 * n), 4))
        order += [(("bd", n, d), 1) for d in range(2)]
    order += [(("out", j), 1) for j in range(8)]
    order.append((("ffn", 1), 3 * HT))
    at, n = {}, 0
    for key, count in order:
        at[key] = n
        n += count
    return order, at, n


ORDER, AT, CHUNKS = plan()


def landed_table():
    count, got = [0] * RING, []
    for key, number in ORDER:
        for _ in range(number):
            n = len(got)
            count[n % RING] += 32 if key[0] == "bd" else 16
            got.append(count[n % RING])
    return got


LANDED = landed_table()

NORMS = [(0, 0, range(0, TT)), (0, 1, range(0, TT)), (1, 0, range(0, TT)), (1, 1, range(CT, TT))]
UPDATES = [(0, 0, range(0, TT)), (0, 1, range(0, TT)), (1, 0, range(CT, TT)), (1, 1, range(CT, TT))]
NORM_ROW0 = [0, 6, 12, 18]
NORM_GRP = [[(0, 2), (2, 6)], [(0, 2), (2, 6)], [(0, 2), (2, 6)], [(2, 6)]]
NORM_TR0 = [0, 16, 32, 48]
UPD0 = [0, 6, 12, 16]

UNITS = []
for t in range(TT):
    w0 = 0 if t < CT else max(t - 1, CT)
    nw = 0 if t < CT else min(t + 1, TT - 1) - w0 + 1
    UNITS += [(t, h // GROUP, h, w0, nw) for h in range(0, HEADS, 2)]
NU = len(UNITS)
NCU = CT * HEADS // 2
GRPS = []
for _, _, _, w0, nw in UNITS:
    kts = list(range(CT)) + list(range(w0, w0 + nw))
    GRPS.append([kts[k:k + 2] for k in range(0, len(kts), 2)])
GR0 = [sum(len(k) for k in GRPS[:u]) for u in range(NU + 1)]
SR, PR = 4, 5


def ada_banks(a):
    if a < 4:
        return 6 - a % 2, 7
    return (1, 2) if a in UNIT_ADA.values() else (6, 7)


ZEROED = 4


def trunk(nc, x_in, c_in, ctx_in, cctx_in, ada_w, ada_b, norm_g, w_gu, w_down, w_qkv, sinks, w_o,
          b_w_in, conv_w, conv_b, lam, w_a, b_a, w_x, b_x, b_w_out,
          rope_c, rope_s, win_mask, eye, sel, sel_c, out):
    with ExitStack() as st:
        def sem(name):
            return st.enter_context(nc.semaphore(name))

        def sb(name, shape, dt=F):
            return st.enter_context(nc.sbuf_tensor(name, shape, dt))

        hi = sb("hT_hi", [P, KT, TOK], R)
        lo = sb("hT_lo", [P, KT, TOK], R)
        raw = sb("w_raw", [P, RING, CH])
        whi = sb("w_hi", [P, RING, CH], R)
        wlo = sb("w_lo", [P, RING, CH], R)
        ident = sb("ident", [P, P])
        selb = sb("sel_rows", [5, 2, P])
        selc = sb("sel_cols", [5, 2])
        s4 = sb("silu_parts", [P, KT, P], R)
        silu_c = sb("silu_c", [P, 2, KT])
        stage = sb("stage_rows", [NCOL, P])
        stage_c = sb("stage_c", [16, P])
        cols = sb("cols", [P, NCOL])
        mod = sb("mod_cols", [P, 2, 4, KT, 2])
        modrow = sb("mod_rows", [5, 2, HALF])
        stat = sb("stat", [P, 3, TT])
        ustat = sb("ustat", [P, 3, TT])
        mhalf = sb("minus_half", [P, 1])
        dec = sb("decay", [P, 2, 16])
        sp = sb("sp_work", [P, 5, 16])
        nsink = sb("neg_sinks", [P, HEADS])
        snk = sb("sinks_bc", [P, HEADS])
        smx = sb("row_max", [P, SR, 2])
        snm = sb("neg_max", [P, SR, 2])
        ssum = sb("row_sum", [P, SR, 2])
        ses = sb("sink_exp", [P, SR, 2])
        sri = sb("row_inv", [P, SR, 2])

        K = 1024
        g0 = (nc.sbuf_base + 63) // 64 * 64
        a0 = g0 + 40 * K

        def ar(name, off, shape, dt=F):
            return nc.alloc_sbuf_tensor_at(name, shape, dt, offset=a0 + off)

        gate = ar("gate_rows", -40 * K, [P, 2, 2, D])
        x = ar("x", -24 * K, [P, TT, D])
        y = ar("y", 0, [P, TT, D])
        hrow = ar("h_rows", 24 * K, [P, TT, D])
        ntmp = ar("norm_tmp", 48 * K, [P, 4, HALF])
        junk = ar("square_out", 62 * K, [P, D])
        qT = ar("qT", 0, [P, HEADS, TOK])
        kT = ar("kT", 24 * K, [P, KVH, TOK])
        V = ar("V", 30 * K, [P, TT, 2 * P])
        qraw = ar("q_raw", 36 * K, [P, TT, HALF])
        qrot = ar("q_rot", 48 * K, [P, TT - CT, HALF])
        rc = ar("rope_cos", 56 * K, [P, TT - CT, P])
        rs = ar("rope_sin", 58 * K, [P, TT - CT, P])
        rtmp = ar("rope_tmp", 60 * K, [P, 2, HALF])
        S = ar("scores", 36 * K, [P, SR, 2, 5 * P])
        PT = ar("probsT", 56 * K, [P, PR, HALF])
        mask = ar("mask", 66 * K, [P, 3 * P])
        ahi = ar("act_hi", 24 * K, [P, 2, 2, TOK], R)
        alo = ar("act_lo", 36 * K, [P, 2, 2, TOK], R)
        sg = ar("act", 48 * K, [P, 2, TOK])
        u = ar("conv_out", 0, [P, 2, TOK])
        uhi = ar("conv_hi", 6 * K, [P, 2, TOK], R)
        ulo = ar("conv_lo", 12 * K, [P, 2, TOK], R)
        hsum = ar("h_sum", 18 * K, [P, 2, SEQ])
        z = ar("z", 24 * K, [P, KT, SEQ])
        rr = [ar("gate_r0", 40 * K, [P, 2, TOK]), ar("gate_r1", -32 * K, [P, 2, TOK])]
        ii = [ar("gate_i0", 46 * K, [P, 2, TOK]), ar("gate_i1", -26 * K, [P, 2, TOK])]
        aa = [ar("lru_a0", 52 * K, [P, 2, TOK]), ar("lru_a1", 58 * K, [P, 2, TOK])]
        a2 = [ar("lru_sq0", 64 * K, [P, TOK]), ar("lru_sq1", -20 * K, [P, TOK])]
        assert a0 + 68 * K <= nc.sbuf_usable_end

        ps = st.enter_context(nc.psum_tensor("ps", [P, 8, HALF], F))

        raw_landed = [sem(f"raw_landed{i}") for i in range(RING)]
        x_landed = [sem(f"x_landed{i}") for i in range(TT)]
        c_landed, cols_landed, rope_landed = sem("c_landed"), sem("cols_landed"), sem("rope_landed")
        gate_landed = [sem("gates0_landed"), sem("mixer_gate1_landed"), sem("ffn_gate1_landed")]
        sel_landed, att_landed = sem("sel_landed"), sem("att_landed")
        bias_landed = [sem("bias_landed0"), sem("bias_landed1")]
        w_hi, w_lo, w_used = sem("w_hi_ready"), sem("w_lo_ready"), sem("w_used")
        zeroed, start_tr, silu_done, s4_done, cols_done = (
            sem("zeroed"), sem("start_tr"), sem("silu_done"), sem("s4_done"), sem("cols_done"))
        sp_act, sp_dve = sem("sp_act"), sem("sp_dve")
        row_moved, ada_out, ada_done, ada_step = sem("row_moved"), sem("ada_out"), sem("ada_done"), sem("ada_step")
        n_ssq, n_mean, n_rstd, n_row = sem("n_ssq"), sem("n_mean"), sem("n_rstd"), sem("n_row")
        n_tr, n_hi, n_tmp, n_lo = sem("n_tr"), sem("n_hi"), sem("n_tmp"), sem("n_lo")
        u_ssq, u_mean, u_rstd, u_scaled, x_even, x_odd = (
            sem("u_ssq"), sem("u_mean"), sem("u_rstd"), sem("u_scaled"), sem("x_even_added"), sem("x_odd_added"))
        qkv_moved, rope_mul, rope_done, qk_tr, qk_moved = (
            sem("qkv_moved"), sem("rope_mul"), sem("rope_done"), sem("qk_tr"), sem("qk_moved"))
        s_mm, s_ctx, s_win, s_max, s_neg, s_exp, s_den, s_inv, s_prob = (
            sem("s_mm"), sem("s_ctx"), sem("s_win"), sem("s_max"), sem("s_neg"), sem("s_exp"),
            sem("s_den"), sem("s_inv"), sem("s_prob"))
        p_tr, p_moved, pv_mm, o_hi, o_lo = sem("p_tr"), sem("p_moved"), sem("pv_mm"), sem("o_hi"), sem("o_lo")
        y_moved = sem("y_moved")
        silu_r, prod_r, ahi_r, alo_r, down_mm, down_add = [], [], [], [], [], []
        for i in range(2):
            silu_r.append(sem(f"silu_ready{i}"))
            prod_r.append(sem(f"prod_ready{i}"))
            ahi_r.append(sem(f"act_hi_ready{i}"))
            alo_r.append(sem(f"act_lo_ready{i}"))
            down_mm.append(sem(f"down_mm{i}"))
            down_add.append(sem(f"down_added{i}"))
        in_act, conv, u_hi, u_lo = sem("in_act"), sem("conv"), sem("u_hi"), sem("u_lo")
        bd_mm, sig, decay_exp, tanh_r, a_sq, iu_r, v_r, sqrt_r, b_r, scan_r, h_r, z_r, z_hi, z_lo = (
            sem("bd_mm"), sem("sigmoid"), sem("decay_exp"), sem("tanh_r"), sem("a_sq"), sem("iu_r"),
            sem("v_r"), sem("sqrt_r"), sem("b_r"), sem("scan_r"), sem("h_r"), sem("z_r"),
            sem("z_hi"), sem("z_lo"))
        out_sent = sem("out_sent")

        def wait_x(eng, k, i):
            eng.wait_ge(x_even if i % 2 == 0 else x_odd, UPD0[k] // 2 + i // 2 + 1)

        def landed_value(n, v=0):
            return LANDED[n] + v * (16 * 12 // RING)

        def gu_src(li, q, up):
            s = w_gu[li].rearrange("(k p) n -> p k n", p=P)
            return s[:, :, bass.ts(q + (HT if up else 0), P)]

        def down_src(li, q):
            return w_down[li][bass.ts(q, P), :]

        block = st.enter_context(nc.Block())

        @block.sync
        def _(eng):
            def load(n, src, dst=None, v=0):
                if n >= RING:
                    eng.wait_ge(w_lo, n - RING + 1 + v * 12)
                to = raw[:, n % RING, :] if dst is None else dst(raw[:, n % RING, :])
                eng.dma_start(to, src).then_inc(raw_landed[n % RING], 16)

            def two_by(dst):
                return dst.rearrange("p (k n) -> p k n", k=2)

            def load_cols512(n, w, j, cc):
                load(n, w[2 * j * P:(2 * j + 2) * P, cc * HALF:(cc + 1) * HALF].rearrange("(k p) n -> p k n", p=P), two_by)

            def eight_by(dst):
                return dst.rearrange("p (k n) -> p k n", k=KT)

            def load_ada(a):
                li, c = a // 12, a % 12
                if a >= 2:
                    eng.wait_ge(ada_out, a - 1)
                eng.dma_start(modrow[4:5, a % 2, :], ada_b[li:li + 1, c * HALF:(c + 1) * HALF]).then_inc(bias_landed[a % 2], 16)
                for j in range(4):
                    load_cols512(AT["ada", a] + j, ada_w[li], j, c)

            def load_gate_gain(li, m, v):
                g = norm_g[li, 2 * m + 1:2 * m + 2, :].to_broadcast((P, D))
                eng.dma_start(gate[:, v, m, :], g).then_inc(gate_landed[li + li * m], 16)

            def load_ffn(li):
                b = AT["ffn", li]

                def gu(n, q, v=0):
                    for t in range(2):
                        load(n + 2 * t, gu_src(li, q + t, False), eight_by, v)
                        load(n + 2 * t + 1, gu_src(li, q + t, True), eight_by, v)

                def down(n, q, v=0):
                    for t in range(2):
                        load(n + t, down_src(li, q + t), None, v)

                gu(b, 0)
                with eng.Fori(0, 5) as v:
                    for s in range(2):
                        gu(b + 4 + 6 * s, 4 * v + 2 + 2 * s, v)
                        down(b + 8 + 6 * s, 4 * v + 2 * s, v)
                down(b + 64, HT - 2)

            eng.dma_start(stage_c[0:8, :], c_in.rearrange("a (t p) -> (a t) p", p=P)).then_inc(c_landed, 16)
            eng.dma_start(stage_c[8:16, :], cctx_in.rearrange("(t p) -> t p", p=P)).then_inc(c_landed, 16)
            eng.dma_start(ident[:, :], eye).then_inc(c_landed, 16)
            eng.dma_start(selb[:, :, :], sel).then_inc(sel_landed, 16)
            eng.dma_start(selc[:, :], sel_c).then_inc(sel_landed, 16)
            gate_loads = [(0, m, v) for m in range(2) for v in range(2)]
            for key, count in ORDER:
                n = AT[key]
                if key[0] == "ada":
                    a = key[1]
                    if a == 4:
                        for g in gate_loads:
                            load_gate_gain(*g)
                    if a in (16, 22):
                        eng.wait_ge(x_even, UPD0[2] // 2)
                        eng.wait_ge(x_odd, UPD0[2] // 2)
                        load_gate_gain(1, (a - 16) // 6, 0)
                    load_ada(a)
                elif key[0] == "qkv":
                    load_cols512(n, w_qkv[0], key[1] % 4, key[1] // 4)
                    if key[1] == 0:
                        eng.dma_start(rc[:, :, :], rope_c).then_inc(rope_landed, 16)
                        eng.dma_start(rs[:, :, :], rope_s).then_inc(rope_landed, 16)
                        eng.dma_start(mask[:, :], win_mask).then_inc(att_landed, 16)
                        eng.dma_start(snk[:, :], sinks[0:1, :].to_broadcast((P, HEADS))).then_inc(att_landed, 16)
                elif key[0] == "o":
                    load_cols512(n, w_o[0], key[1] % 4, key[1] // 4)
                elif key[0] == "out":
                    load_cols512(n, b_w_out[0], OUT_ORDER[key[1]][1], OUT_ORDER[key[1]][0])
                elif key[0] == "in":
                    _, b, j = key
                    m = 2 * b + j if j < 2 else KT + 2 * b + j - 2
                    load(n, b_w_in[0].rearrange("(k p) n -> p k n", p=P)[:, :, m * P:(m + 1) * P], eight_by)
                elif key[0] == "bd":
                    _, b, d = key
                    eng.wait_ge(w_lo, n - RING + 1)
                    slot = raw[:, n % RING, :].rearrange("p (g k n) -> p g k n", g=2, k=2)
                    for g, w in enumerate((w_a, w_x)):
                        eng.dma_start(slot[:, g], w[0, d, b].rearrange("(k p) n -> p k n", p=P)).then_inc(raw_landed[n % RING], 16)
                else:
                    load_ffn(key[1])
            for i, t in enumerate(range(CT, TT)):
                wait_x(eng, 3, i)
                eng.dma_start(out[0, (t - CT) * P:(t - CT + 1) * P, :], x[:, t, :]).then_inc(out_sent, 16)
            eng.wait_ge(out_sent, 16 * (TT - CT))

        @block.scalar
        def _(eng):
            done = [0]
            last_square = []

            def split(n, v=0):
                eng.wait_ge(raw_landed[n % RING], landed_value(n, v))
                if n >= RING:
                    eng.wait_ge(w_used, n - RING + 1 + v * 12)
                eng.activation(whi[:, n % RING, :], raw[:, n % RING, :], ACT.Copy).then_inc(w_hi, 1)

            def splits_to(end):
                while done[0] < min(end, CHUNKS):
                    split(done[0])
                    done[0] += 1

            def ada_row(a):
                n = AT["ada", a] + 3
                splits_to(n + 3)
                eng.wait_ge(w_used, n + 1)
                if a >= 2:
                    eng.wait_ge(ada_out, a - 1)
                eng.activation(modrow[0:4, a % 2, :], ps[0:4, ada_banks(a)[0], :], ACT.Copy).then_inc(row_moved, 1)

            def square(src, dst, signal, number):
                if last_square:
                    eng.wait_ge(*last_square[-1])
                eng.activation(junk[:, :], src, ACT.Square, accum_out=dst).then_inc(signal, 1)
                last_square.append((signal, number + 1))

            def norm_square(k, i):
                t = NORMS[k][2][i]
                if k == 0:
                    eng.wait_ge(x_landed[t], 16)
                else:
                    wait_x(eng, k - 1, i)
                square(x[:, t, :], stat[:, 0, t:t + 1], n_ssq, NORM_ROW0[k] + i)

            def norm_row(k, i):
                t = NORMS[k][2][i]
                eng.wait_ge(n_rstd, NORM_ROW0[k] + i + 1)
                if k == 2 and i == 0:
                    eng.wait_ge(w_used, AT["ffn", 0] + 3 * HT)
                eng.activation(hrow[:, t, :], x[:, t, :], ACT.Copy, scale=stat[:, 2, t:t + 1]).then_inc(n_row, 1)

            def update_square(k, i, ready):
                t = UPDATES[k][2][i]
                ready(i)
                square(y[:, t, :], ustat[:, 0, t:t + 1], u_ssq, UPD0[k] + i)

            def norm_affine(k):
                li, which, _ = NORMS[k]
                eng.wait_ge(ada_done, 12 * li + (4 if which == 0 else 10))
                seq = NORM_TR0[k]
                for t0, t1 in NORM_GRP[k]:
                    v = 1 if t0 == 0 else 0
                    for ct in range(KT):
                        eng.wait_ge(n_tr, seq + 1)
                        if seq >= 4:
                            eng.wait_ge(n_lo, seq - 3)
                        eng.activation(ntmp[:, seq % 4, 0:(t1 - t0) * P], ps[:, seq % 8, 0:(t1 - t0) * P], ACT.Identity,
                                       bias=mod[:, li, 2 * which, ct, v:v + 1],
                                       scale=mod[:, li, 2 * which + 1, ct, v:v + 1]).then_inc(n_tmp, 1)
                        seq += 1

            def update_norm(ku, kn, ready):
                n = len(UPDATES[ku][2])
                for i in range(n + 4):
                    if i < n:
                        update_square(ku, i, ready)
                    if kn is not None and 0 <= i - 2 < n:
                        norm_square(kn, i - 2)
                    if kn is not None and 0 <= i - 3 < n:
                        norm_row(kn, i - 3)

            def ffn(li):
                b = AT["ffn", li]
                hw = 384 if li == 0 else HALF
                w = TOK if li == 0 else SEQ

                def gated(n0, q, t, v):
                    eng.wait_ge(w_used, n0 + 2 + 2 * t + v * 12)
                    if not isinstance(q, int) or q >= 2:
                        eng.wait_ge(alo_r[li], q - 1)
                    if li == 0:
                        g, o = ps[:, 4 * t:4 * t + 2, 0:hw], sg[:, t, 0:w].rearrange("p (h w) -> p h w", h=2)
                    else:
                        g, o = ps[:, 4 * t, 0:hw], sg[:, t, 0:w]
                    eng.activation(o, g, ACT.Silu).then_inc(silu_r[li], 1)
                    eng.wait_ge(prod_r[li], q + 1)

                def gated_hi(q, t, par):
                    eng.activation(ahi[:, par, t, 0:w], sg[:, t, 0:w], ACT.Copy).then_inc(ahi_r[li], 1)

                def step(n0, i, par, v):
                    for k in range(1, 5):
                        split(n0 + k, v)
                    gated(n0, 2 * i, 0, v)
                    gated_hi(2 * i, 0, par)
                    split(n0 + 5, v)
                    split(n0 + 6, v)
                    gated(n0, 2 * i + 1, 1, v)
                    gated_hi(2 * i + 1, 1, par)

                splits_to(b + 5)
                gated(b, 0, 0, 0)
                gated_hi(0, 0, 0)
                gated(b, 1, 1, 0)
                gated_hi(1, 1, 0)
                with eng.Fori(0, 5) as v:
                    for s in range(2):
                        step(b + 4 + 6 * s, 1 + s + 2 * v, (1 + s) % 2, v)
                done[0] = b + 65
                splits_to(b + 66)

            pieces = [(C_G + 8 * (2 * li + wh), norm_g[li, 2 * wh:2 * wh + 1, :], 8) for li in range(2) for wh in range(2)]
            pieces += [(C_CW, conv_w[0], 32), (C_CB, conv_b, 8), (C_LAM, lam[0], 16), (C_BA, b_a[0], 16), (C_BX, b_x[0], 16)]
            for row, src, n in pieces:
                eng.dma_start(stage[row:row + n, :], src.rearrange("a (t p) -> (a t) p", p=P)).then_inc(cols_landed, 16)
            for t in range(TT):
                src = ctx_in[0, t * P:(t + 1) * P, :] if t < CT else x_in[0, (t - CT) * P:(t - CT + 1) * P, :]
                eng.dma_start(x[:, t, :], src).then_inc(x_landed[t], 16)
            eng.wait_ge(start_tr, 1)
            eng.activation(silu_c[:, :, :], ps[:, 7, 0:16].rearrange("p (v k) -> p v k", v=2), ACT.Silu).then_inc(silu_done, 1)
            splits_to(3)
            for a in range(4):
                ada_row(a)
                if a < 3:
                    norm_square(0, 2 * a)
                    norm_square(0, 2 * a + 1)
                if a:
                    norm_row(0, 2 * a - 2)
                    norm_row(0, 2 * a - 1)
            norm_affine(0)

            def qkv_move(cc):
                n = AT["qkv", 4 * cc + 3]
                splits_to(n + 3)
                eng.wait_ge(w_used, n + 1)
                if cc:
                    eng.wait_ge(qk_tr, 6 * cc)
                    eng.wait_ge(rope_mul, 12 * cc)
                for t in range(TT):
                    w = HALF if cc < 2 else 2 * P
                    eng.activation(qraw[:, t, 0:w], ps[:, t, 0:w], ACT.Copy).then_inc(qkv_moved, 1)
                    if cc == 2:
                        eng.activation(V[:, t, :], ps[:, t, w:HALF], ACT.Copy).then_inc(qkv_moved, 1)

            def qk_move(cc):
                nh = 4 if cc < 2 else 2
                for t in range(TT):
                    s = 6 * cc + t
                    eng.wait_ge(qk_tr, s + 1)
                    dst = qT[:, 4 * cc:4 * cc + 4, t * P:(t + 1) * P] if cc < 2 else kT[:, :, t * P:(t + 1) * P]
                    src = ps[:, 6 + s % 2, 0:nh * P].rearrange("p (h q) -> p h q", h=nh)
                    eng.activation(dst, src, ACT.Copy).then_inc(qk_moved, 1)

            for j in range(12):
                if j % 4 == 3:
                    qkv_move(j // 4)
                for a in QKV_ADA.get(j, ()):
                    ada_row(a)
                if j in (5, 9):
                    qk_move((j - 5) // 4)
            splits_to(AT["qkv", 11] + 4)
            qk_move(2)
            eng.wait_ge(sp_dve, 2)
            eng.activation(sp[:, 1, :], sp[:, 0, :], ACT.Exp, scale=-1.0).then_inc(sp_act, 1)

            def ctx_move(u):
                eng.wait_ge(s_mm, u + 1)
                if u >= SR:
                    eng.wait_ge(p_tr, GR0[u - SR + 1])
                eng.activation(S[:, u % SR, :, 0:CTX], ps[:, 3 * (u % 2), :].rearrange("p (h k) -> p h k", h=2),
                               ACT.Copy).then_inc(s_ctx, 1)

            def exps(u):
                t, g, h0, w0, nw = UNITS[u]
                b, nk = u % SR, CTX + nw * P
                eng.wait_ge(s_neg, 2 * (u + 1))
                for h in range(2):
                    eng.activation(S[:, b, h, 0:nk], S[:, b, h, 0:nk], ACT.Exp, bias=snm[:, b, h:h + 1],
                                   scale=SCALE, accum_out=ssum[:, b, h:h + 1]).then_inc(s_exp, 1)
                eng.activation(ses[:, b, :], ses[:, b, :], ACT.Exp).then_inc(s_exp, 1)

            def probs_move(u, i):
                q, w = GR0[u] + i, 2 * P * len(GRPS[u][i])
                eng.wait_ge(p_tr, q + 1)
                if q >= PR:
                    eng.wait_ge(pv_mm, q - PR + 1)
                eng.activation(PT[:, q % PR, 0:w], ps[:, 6, 0:w], ACT.Copy).then_inc(p_moved, 1)

            ctx_move(0)
            ctx_move(1)
            exps(0)
            for un, (t, g, h0, w0, nw) in enumerate(UNITS):
                if un + 1 < NU:
                    exps(un + 1)
                probs_move(un, 0)
                if un + 2 < NU:
                    ctx_move(un + 2)
                for i in range(1, len(GRPS[un])):
                    probs_move(un, i)
                eng.wait_ge(pv_mm, GR0[un + 1])
                eng.activation(hi[:, h0:h0 + 2, t * P:(t + 1) * P],
                               ps[:, 7, 0:2 * P].rearrange("p (h q) -> p h q", h=2), ACT.Copy).then_inc(o_hi, 1)
                if un in UNIT_ADA:
                    ada_row(UNIT_ADA[un])
            splits_to(AT["o", 0] + 3)

            for j in range(8):
                n = AT["o", j]
                splits_to(n + 3)
                if j % 4 == 3:
                    eng.wait_ge(w_used, n + 1)
                    half = j // 4
                    for i in range(TT):
                        eng.activation(y[:, i, half * HALF:(half + 1) * HALF], ps[:, i, :], ACT.Copy).then_inc(y_moved, 1)
                for a in O_ADA.get(j, ()):
                    ada_row(a)

            update_norm(0, 1, lambda i: eng.wait_ge(y_moved, 6 + i + 1))
            splits_to(AT["ffn", 0] + 3)
            norm_affine(1)
            ffn(0)

            update_norm(1, 2, lambda i: eng.wait_ge(down_add[0], 12 * (HT // 2 - 1) + 2 * i + 2 + ZEROED))
            splits_to(AT["in", 0, 0] + 3)
            norm_affine(2)

            def z_hi_parts(tiles):
                for ct in tiles:
                    eng.wait_ge(z_r, ct + 1)
                    eng.activation(hi[:, ct, CTX:TOK], z[:, ct, :], ACT.Copy).then_inc(z_hi, 1)

            for n in range(NBLK):
                nxt = AT["in", n + 1, 0] if n + 1 < NBLK else AT["out", 0]
                for j in range(2):
                    c, q, k = AT["in", n, j], 2 * n + j, 2 - 2 * j
                    splits_to(c + 3)
                    eng.wait_ge(w_used, c + 1)
                    if n:
                        eng.wait_ge(iu_r, 4 * n)
                        eng.wait_ge(u_lo, 2 * n)
                    w1, cb = cols[:, C_CW + 8 + q:C_CW + 9 + q], cols[:, C_CB + q:C_CB + q + 1]
                    eng.activation(u[:, j, 0:CTX], ps[:, k, 0:CTX], ACT.Identity, bias=cb, scale=w1).then_inc(in_act, 1)
                    eng.activation(u[:, j, CTX:TOK], ps[:, k + 1, :], ACT.Identity, bias=cb, scale=w1).then_inc(in_act, 1)
                ada_row(16 + 2 * n)
                for j in range(2):
                    eng.wait_ge(conv, 6 * (2 * n + j + 1))
                    if n:
                        eng.wait_ge(w_used, AT["bd", n - 1, 1] + 1)
                    eng.activation(uhi[:, j, :], u[:, j, :], ACT.Copy).then_inc(u_hi, 1)
                    c = AT["in", n, 2 + j]
                    splits_to(c + 3)
                    eng.wait_ge(w_used, c + 1)
                    eng.activation(z[:, 2 * n + j, :], ps[:, 4 + j, :], ACT.Gelu_apprx_tanh).then_inc(in_act, 1)
                if n == NBLK - 1:
                    z_hi_parts(range(KT - 2))
                ada_row(17 + 2 * n)
                for d in range(2):
                    c, e = AT["bd", n, d], 2 * n + d
                    splits_to(c + 3)
                    if n:
                        eng.wait_ge(scan_r, 4 * (e - 1))
                        if d:
                            eng.wait_ge(h_r, 2 * n)
                    for m in range(2):
                        for g, (dst, col) in enumerate(((rr, C_BA), (ii, C_BX))):
                            s = 2 * m + g
                            if s < 3:
                                eng.wait_ge(bd_mm, 3 * e + s + 1)
                            else:
                                eng.wait_ge(w_used, c + 1)
                            bias = cols[:, col + 8 * d + 2 * n + m:col + 8 * d + 2 * n + m + 1]
                            eng.activation(dst[d][:, m, :].rearrange("p (h w) -> p h w", h=2),
                                           ps[:, 4 * g:4 * g + 2, 0:384], ACT.Sigmoid, bias=bias).then_inc(sig, 1)
                for e in (2 * n, 2 * n + 1):
                    for m in range(2):
                        d = e % 2
                        k = 8 * d + 2 * n + m
                        eng.wait_ge(sig, 4 * e + 2 * m + 1)
                        eng.activation(aa[d][:, m, :], rr[d][:, m, :], ACT.Exp, scale=dec[:, 0, k:k + 1]).then_inc(decay_exp, 1)
                        eng.wait_ge(decay_exp, 2 * e + m + 1)
                        eng.activation(rr[d][:, m, :], rr[d][:, m, :], ACT.Tanh, scale=dec[:, 1, k:k + 1]).then_inc(tanh_r, 1)
                    splits_to(nxt + 2 + e % 2)
                for e in (2 * n, 2 * n + 1):
                    for m in range(2):
                        eng.wait_ge(v_r, 2 * e + m + 1)
                        eng.activation(rr[e % 2][:, m, :], rr[e % 2][:, m, :], ACT.Sqrt).then_inc(sqrt_r, 1)
                    splits_to(nxt + 4)
            for j in range(8):
                n = AT["out", j]
                splits_to(n + 3)
                if j == 3:
                    z_hi_parts(range(KT - 2, KT))
                if OUT_ORDER[j][1] == 3:
                    half = OUT_ORDER[j][0]
                    eng.wait_ge(w_used, n + 1)
                    for i in range(4):
                        eng.activation(y[:, CT + i, half * HALF:(half + 1) * HALF], ps[:, 4 * half + i, :], ACT.Copy).then_inc(y_moved, 1)
            update_norm(2, 3, lambda i: eng.wait_ge(y_moved, 12 + 4 + i + 1))
            splits_to(AT["ffn", 1] + 3)
            norm_affine(3)
            ffn(1)
            update_norm(3, None, lambda i: eng.wait_ge(down_add[1], 8 * (HT // 2 - 1) + 2 * i + 2 + ZEROED))

        @block.vector
        def _(eng):
            done = [0]

            def split(n, v=0):
                eng.wait_ge(w_hi, n + 1 + v * 12)
                s = n % RING
                eng.tensor_tensor(wlo[:, s, :], raw[:, s, :], whi[:, s, :].bitcast(F), ALU.subtract).then_inc(w_lo, 1)

            def splits_to(end):
                while done[0] < min(end, CHUNKS):
                    split(done[0])
                    done[0] += 1

            def ada_finish(a):
                li, c = a // 12, a % 12
                m, half = c // 2, c % 2
                splits_to(AT["ada", a] + 6)
                eng.wait_ge(ada_out, a + 1)
                if m in (2, 5):
                    gm = m // 3
                    eng.wait_ge(gate_landed[li + li * gm], 64 if li == 0 else 16)
                    for v in range(2 if li == 0 else 1):
                        g = gate[:, v, gm, half * HALF:(half + 1) * HALF]
                        ins = eng.tensor_tensor(g, ps[:, ada_banks(a)[1 - v], :], g, ALU.mult)
                    ins.then_inc(ada_done, 1)
                    return
                idx = m if m < 2 else m - 1
                for v in range(2):
                    src = ps[:, ada_banks(a)[1], 0:8].rearrange("p (t v) -> p v t", v=2)[:, v, :]
                    dst = mod[:, li, idx, 4 * half:4 * half + 4, v]
                    if idx % 2 == 0:
                        ins = eng.tensor_copy(dst, src)
                    else:
                        g0 = C_G + 8 * (2 * li + idx // 2) + 4 * half
                        ins = eng.scalar_tensor_tensor(dst, src, 1.0, cols[:, g0:g0 + 4], ALU.add, ALU.mult)
                ins.then_inc(ada_done, 1)

            def mean(t, src, ssq, number, signal):
                eng.wait_ge(ssq, number + 1)
                eng.tensor_scalar(src[:, 1, t:t + 1], src[:, 0, t:t + 1], 1.0 / D, EPS, ALU.mult, ALU.add).then_inc(signal, 1)

            def update_scale(k, i):
                li, m, tiles = UPDATES[k]
                t = tiles[i]
                eng.wait_ge(u_rstd, UPD0[k] + i + 1)
                eng.scalar_tensor_tensor(y[:, t, :], y[:, t, :], ustat[:, 2, t:t + 1],
                                         gate[:, 1 if t < CT else 0, m, :], ALU.mult, ALU.mult).then_inc(u_scaled, 1)

            def update_norm(ku, kn, adds=lambda i: None):
                li, m, tiles = UPDATES[ku]
                n = len(tiles)
                eng.wait_ge(ada_done, 12 * li + (6 if m == 0 else 12))
                for i in range(n + 4):
                    if i < n:
                        adds(i)
                        mean(tiles[i], ustat, u_ssq, UPD0[ku] + i, u_mean)
                    if 0 <= i - 1 < n:
                        update_scale(ku, i - 1)
                    if kn is not None and 0 <= i - 2 < n:
                        mean(tiles[i - 2], stat, n_ssq, NORM_ROW0[kn] + i - 2, n_mean)
                    if 0 <= i - 1 < n and (i - 1) % 2 == 0:
                        t = tiles[i - 1]
                        eng.wait_ge(u_scaled, UPD0[ku] + i)
                        eng.tensor_tensor(x[:, t, :], x[:, t, :], y[:, t, :], ALU.add).then_inc(x_even, 1)

            def norm_split(k):
                seq = NORM_TR0[k]
                todo = [(t0, t1, ct) for t0, t1 in NORM_GRP[k] for ct in range(KT)]

                def lo_part(s, t0, t1, ct):
                    eng.wait_ge(n_hi, s + 1)
                    eng.tensor_tensor(lo[:, ct, t0 * P:t1 * P], ntmp[:, s % 4, 0:(t1 - t0) * P],
                                      hi[:, ct, t0 * P:t1 * P].bitcast(F), ALU.subtract).then_inc(n_lo, 1)

                for i, (t0, t1, ct) in enumerate(todo):
                    eng.wait_ge(n_tmp, seq + i + 1)
                    eng.tensor_copy(hi[:, ct, t0 * P:t1 * P], ntmp[:, (seq + i) % 4, 0:(t1 - t0) * P]).then_inc(n_hi, 1)
                    if i:
                        lo_part(seq + i - 1, *todo[i - 1])
                lo_part(seq + len(todo) - 1, *todo[-1])

            def ffn(li):
                b = AT["ffn", li]
                hw = 384 if li == 0 else HALF
                w = TOK if li == 0 else SEQ
                tiles = UPDATES[2 * li + 1][2]
                nd = 2 * len(tiles)

                def product(q, t, par):
                    eng.wait_ge(silu_r[li], q + 1)
                    if li == 0:
                        s, up = sg[:, t, 0:w].rearrange("p (h w) -> p h w", h=2), ps[:, 4 * t + 2:4 * t + 4, 0:hw]
                    else:
                        s, up = sg[:, t, 0:w], ps[:, 4 * t + 2, 0:hw]
                    eng.tensor_tensor(s, s, up, ALU.mult).then_inc(prod_r[li], 1)
                    eng.wait_ge(ahi_r[li], q + 1)
                    eng.tensor_tensor(alo[:, par, t, 0:w], sg[:, t, 0:w], ahi[:, par, t, 0:w].bitcast(F),
                                      ALU.subtract).then_inc(alo_r[li], 1)

                def down_adds(j, last_chunk, v, outputs=range(nd)):
                    for o in outputs:
                        if o < nd - 1:
                            eng.wait_ge(down_mm[li], (nd - 1) * j + o + 1)
                        else:
                            eng.wait_ge(w_used, last_chunk + 1 + v * 12)
                        to = y[:, tiles[o // 2], (o % 2) * HALF:(o % 2 + 1) * HALF]
                        eng.tensor_tensor(to, ps[:, o % 4, :], to, ALU.add).then_inc(down_add[li], 1)

                def step(n0, i, par, v):
                    for k in range(1, 5):
                        split(n0 + k, v)
                    product(2 * i, 0, par)
                    split(n0 + 5, v)
                    split(n0 + 6, v)
                    product(2 * i + 1, 1, par)
                    down_adds(i - 1, n0 + 5, v)

                splits_to(b + 5)
                product(0, 0, 0)
                product(1, 1, 0)
                eng.wait_ge(down_add[li], ZEROED)
                with eng.Fori(0, 5) as v:
                    for s in range(2):
                        step(b + 4 + 6 * s, 1 + s + 2 * v, (1 + s) % 2, v)
                done[0] = b + 65
                splits_to(b + 66)
                return lambda i: down_adds(HT // 2 - 1, b + 65, 0, (2 * i, 2 * i + 1))

            eng.wait_ge(silu_done, 1)
            eng.wait_ge(zeroed, 1)
            sv = silu_c[:, :, :].rearrange("p v k -> p k v")
            eng.tensor_copy(s4[:, :, 0:4:2], sv).then_inc(s4_done, 1)
            eng.wait_ge(s4_done, 1)
            eng.tensor_tensor(s4[:, :, 1:4:2], sv, s4[:, :, 0:4:2].bitcast(F), ALU.subtract).then_inc(s4_done, 1)
            splits_to(3)
            eng.wait_ge(start_tr, 2)
            eng.tensor_copy(cols[:, :], ps[:, 4, 0:NCOL]).then_inc(cols_done, 1)
            eng.wait_ge(cols_done, 1)
            for a in range(4):
                splits_to(AT["ada", a] + 6)
                if a < 3:
                    mean(2 * a, stat, n_ssq, 2 * a, n_mean)
                    mean(2 * a + 1, stat, n_ssq, 2 * a + 1, n_mean)
                if a:
                    ada_finish(a - 1)
            ada_finish(3)
            norm_split(0)

            def rope(cc):
                nh = 4 if cc < 2 else 2
                w = nh * P
                eng.wait_ge(rope_landed, 32)
                for i in range(TT - CT):
                    r = 4 * cc + i
                    eng.wait_ge(qkv_moved, (6 * cc + CT + i + 1) if cc < 2 else 12 + 2 * (CT + i) + 1)
                    if cc:
                        eng.wait_ge(qk_tr, 6 * cc)
                    if r >= 2:
                        eng.wait_ge(rope_done, r - 1)
                    src = qraw[:, CT + i, 0:w]
                    c = rc[:, i, :].rearrange("p (o w) -> p o w", o=1).to_broadcast((P, nh, P))
                    eng.tensor_tensor(qrot[:, i, 0:w].rearrange("p (h w) -> p h w", h=nh),
                                      src.rearrange("p (h w) -> p h w", h=nh), c, ALU.mult).then_inc(rope_mul, 1)
                    sv5 = src.rearrange("p (h a s w) -> p s h a w", h=nh, a=2, s=2)
                    tv5 = rtmp[:, r % 2, 0:w].rearrange("p (h a s w) -> p s h a w", h=nh, a=2, s=2)
                    rv = rs[:, i, :].rearrange("p (a s w) -> p s a w", a=2, s=2)
                    for s in range(2):
                        sn = rv[:, s].rearrange("p (o a) w -> p o a w", o=1).to_broadcast((P, nh, 2, 32))
                        eng.tensor_tensor(tv5[:, s], sv5[:, 1 - s], sn, ALU.mult).then_inc(rope_mul, 1)

            for j in range(12):
                splits_to(AT["qkv", j] + 3)
                if j % 4 == 3:
                    rope(j // 4)
                for a in QKV_ADA.get(j, ()):
                    ada_finish(a)
            splits_to(AT["qkv", 11] + 4)

            step_no = [0]

            def chain(ins):
                step_no[0] += 1
                ins.then_inc(sp_dve, 1)
                eng.wait_ge(sp_dve, step_no[0])

            lamc = cols[:, C_LAM:C_LAM + 16]
            chain(eng.tensor_scalar(sp[:, 0, :], lamc, -1.0, None, ALU.mult))
            chain(eng.tensor_tensor(sp[:, 0, :], sp[:, 0, :], lamc, ALU.max))
            eng.wait_ge(sp_act, 1)
            chain(eng.tensor_scalar(sp[:, 2, :], sp[:, 1, :], 2.0, None, ALU.add))
            chain(eng.reciprocal(sp[:, 2, :], sp[:, 2, :]))
            chain(eng.tensor_tensor(sp[:, 1, :], sp[:, 1, :], sp[:, 2, :], ALU.mult))
            chain(eng.tensor_tensor(sp[:, 2, :], sp[:, 1, :], sp[:, 1, :], ALU.mult))
            chain(eng.tensor_scalar(sp[:, 3, :], sp[:, 2, :], 2.0 / 17, 2.0 / 15, ALU.mult, ALU.add))
            for k in range(13, 0, -2):
                chain(eng.tensor_tensor(sp[:, 3, :], sp[:, 3, :], sp[:, 2, :], ALU.mult))
                chain(eng.tensor_scalar(sp[:, 3, :], sp[:, 3, :], 2.0 / k, None, ALU.add))
            chain(eng.tensor_tensor(sp[:, 3, :], sp[:, 3, :], sp[:, 1, :], ALU.mult))
            chain(eng.tensor_scalar(sp[:, 4, :], lamc, -1.0, 0.0, ALU.mult, ALU.max))
            chain(eng.tensor_tensor(sp[:, 4, :], sp[:, 4, :], sp[:, 3, :], ALU.add))
            chain(eng.tensor_scalar(dec[:, 0, :], sp[:, 4, :], -8.0, None, ALU.mult))
            chain(eng.tensor_scalar(dec[:, 1, :], sp[:, 4, :], 8.0, None, ALU.mult))


            eng.wait_ge(att_landed, 32)
            eng.tensor_scalar(nsink[:, :], snk[:, :], -1.0, None, ALU.mult).then_inc(s_den, 1)
            eng.wait_ge(s_den, 1)

            def maxima(u):
                t, g, h0, w0, nw = UNITS[u]
                b = u % SR
                eng.wait_ge(s_mm, u + 1)
                if nw:
                    if u >= SR:
                        eng.wait_ge(p_tr, GR0[u - SR + 1])
                    off, w = (w0 - t + 1) * P, nw * P
                    mk = mask[:, off:off + w].rearrange("p (o w) -> p o w", o=1).to_broadcast((P, 2, w))
                    k = 3 * (u % 2) + 1
                    eng.tensor_tensor(S[:, b, :, CTX:CTX + w], ps[:, k:k + 2, 0:w], mk, ALU.add).then_inc(s_win, 1)
                    eng.wait_ge(s_win, u - NCU + 1)
                eng.wait_ge(s_ctx, u + 1)
                eng.tensor_reduce(smx[:, b, :], S[:, b, :, 0:CTX + nw * P], AX, ALU.max).then_inc(s_max, 1)
                eng.wait_ge(s_max, u + 1)
                eng.scalar_tensor_tensor(snm[:, b, :], smx[:, b, :], -SCALE, nsink[:, h0:h0 + 2],
                                         ALU.mult, ALU.min).then_inc(s_neg, 1)
                eng.wait_ge(s_neg, 2 * u + 1)
                eng.tensor_tensor(ses[:, b, :], snk[:, h0:h0 + 2], snm[:, b, :], ALU.add).then_inc(s_neg, 1)

            def normalise(u):
                t, g, h0, w0, nw = UNITS[u]
                b, nk = u % SR, CTX + nw * P
                eng.wait_ge(s_exp, 3 * (u + 1))
                eng.tensor_tensor(ssum[:, b, :], ssum[:, b, :], ses[:, b, :], ALU.add).then_inc(s_den, 1)
                eng.wait_ge(s_den, u + 2)
                eng.reciprocal(sri[:, b, :], ssum[:, b, :]).then_inc(s_inv, 1)
                eng.wait_ge(s_inv, u + 1)
                for h in range(2):
                    eng.tensor_scalar(S[:, b, h, 0:nk], S[:, b, h, 0:nk], sri[:, b, h:h + 1], None, ALU.mult).then_inc(s_prob, 1)

            maxima(0)
            maxima(1)
            normalise(0)
            for un, (t, g, h0, w0, nw) in enumerate(UNITS):
                if un + 1 < NU:
                    normalise(un + 1)
                if un + 2 < NU:
                    maxima(un + 2)
                eng.wait_ge(o_hi, un + 1)
                eng.tensor_tensor(lo[:, h0:h0 + 2, t * P:(t + 1) * P], ps[:, 7, 0:2 * P].rearrange("p (h q) -> p h q", h=2),
                                  hi[:, h0:h0 + 2, t * P:(t + 1) * P].bitcast(F), ALU.subtract).then_inc(o_lo, 1)
                if un in UNIT_ADA:
                    splits_to(AT["ada", UNIT_ADA[un]] + 6)
                if un - 1 in UNIT_ADA:
                    ada_finish(UNIT_ADA[un - 1])

            for j in range(8):
                splits_to(AT["o", j] + 3)
                for a in O_ADA.get(j, ()):
                    ada_finish(a)
            update_norm(0, 1)
            splits_to(AT["ffn", 0] + 3)
            norm_split(1)
            update_norm(1, 2, ffn(0))
            splits_to(AT["in", 0, 0] + 3)
            norm_split(2)

            def z_lo_parts(tiles):
                for ct in tiles:
                    eng.wait_ge(z_hi, ct + 1)
                    eng.tensor_tensor(lo[:, ct, CTX:TOK], z[:, ct, :], hi[:, ct, CTX:TOK].bitcast(F),
                                      ALU.subtract).then_inc(z_lo, 1)

            def taps(n, j):
                q = 2 * n + j
                k0 = 12 * n + 6 * j
                step = 0
                for k, dt in ((0, -1), (2, 1), (3, 2)):
                    wk = cols[:, C_CW + 8 * k + q:C_CW + 8 * k + q + 1]
                    for s, (t0, t1, src) in enumerate(((0, CTX, ps[:, 2 - 2 * j, 0:CTX]), (CTX, TOK, ps[:, 3 - 2 * j, :]))):
                        w = t1 - t0
                        a, e = max(0, -dt), w - max(0, dt)
                        if step < 2:
                            eng.wait_ge(in_act, 6 * n + 2 * j + s + 1)
                        else:
                            eng.wait_ge(conv, k0 + step - 1)
                        eng.scalar_tensor_tensor(u[:, j, t0 + a:t0 + e], src[:, a + dt:e + dt], wk,
                                                 u[:, j, t0 + a:t0 + e], ALU.mult, ALU.add).then_inc(conv, 1)
                        step += 1

            for n in range(NBLK):
                nxt = AT["in", n + 1, 0] if n + 1 < NBLK else AT["out", 0]
                for j in range(2):
                    splits_to(AT["in", n, j] + 3)
                    taps(n, j)
                splits_to(AT["ada", 16 + 2 * n] + 6)
                for j in range(2):
                    eng.wait_ge(u_hi, 2 * n + j + 1)
                    eng.tensor_tensor(ulo[:, j, :], u[:, j, :], uhi[:, j, :].bitcast(F), ALU.subtract).then_inc(u_lo, 1)
                    splits_to(AT["in", n, 2 + j] + 3)
                    if j == 0:
                        ada_finish(16 + 2 * n)
                if n == NBLK - 1:
                    z_lo_parts(range(KT - 2))
                splits_to(AT["bd", n, 0] + 3)
                ada_finish(17 + 2 * n)
                for e in (2 * n, 2 * n + 1):
                    for m in range(2):
                        s = 2 * e + m
                        eng.wait_ge(a_sq, s + 1)
                        eng.wait_ge(tanh_r, s + 1)
                        eng.scalar_tensor_tensor(rr[e % 2][:, m, :], a2[m][:, :], 1.0, rr[e % 2][:, m, :],
                                                 ALU.add, ALU.mult).then_inc(v_r, 1)
                    splits_to(nxt + 2 + e % 2)
                for e in (2 * n, 2 * n + 1):
                    d = e % 2
                    for m in range(2):
                        s = 2 * e + m
                        eng.wait_ge(sqrt_r, s + 1)
                        eng.wait_ge(iu_r, s + 1)
                        a, b, h = aa[d], rr[d], ii[d]
                        eng.tensor_tensor(b[:, m, :], b[:, m, :], h[:, m, :], ALU.mult).then_inc(b_r, 1)
                        eng.wait_ge(b_r, s + 1)
                        if d == 0:
                            eng.tensor_tensor_scan(h[:, m, 0:CTX], a[:, m, 0:CTX], b[:, m, 0:CTX], 0.0,
                                                   ALU.mult, ALU.add).then_inc(scan_r, 1)
                            eng.wait_ge(scan_r, 2 * s + 1)
                            if n:
                                eng.wait_ge(z_r, 2 * n)
                            eng.tensor_tensor_scan(hsum[:, m, :], a[:, m, CTX:TOK], b[:, m, CTX:TOK],
                                                   h[:, m, CTX - 1:CTX], ALU.mult, ALU.add).then_inc(scan_r, 1)
                        else:
                            eng.tensor_tensor_scan(h[:, m, 0:CTX][:, ::-1], a[:, m, 0:CTX][:, ::-1],
                                                   b[:, m, 0:CTX][:, ::-1], 0.0, ALU.mult, ALU.add).then_inc(scan_r, 1)
                            eng.wait_ge(scan_r, 2 * s + 1)
                            eng.tensor_tensor_scan(h[:, m, CTX:TOK][:, ::-1], a[:, m, CTX:TOK][:, ::-1],
                                                   b[:, m, CTX:TOK][:, ::-1], h[:, m, 0:1],
                                                   ALU.mult, ALU.add).then_inc(scan_r, 1)
                    splits_to(nxt + 4)
            for j in range(8):
                splits_to(AT["out", j] + 3)
                if j == 3:
                    z_lo_parts(range(KT - 2, KT))
            update_norm(2, 3)
            splits_to(AT["ffn", 1] + 3)
            norm_split(3)
            update_norm(3, None, ffn(1))

        @block.gpsimd
        def _(eng):
            def rstd(src, t, means, number, signal):
                eng.wait_ge(means, number + 1)
                eng.tensor_tensor(src[:, 2, t:t + 1], src[:, 1, t:t + 1], mhalf[:, :], ALU.pow).then_inc(signal, 1)

            def update_norm(ku, kn):
                li, m, tiles = UPDATES[ku]
                n = len(tiles)
                for i in range(n + 4):
                    if i < n:
                        rstd(ustat, tiles[i], u_mean, UPD0[ku] + i, u_rstd)
                    if 0 <= i - 1 < n and (i - 1) % 2:
                        t = tiles[i - 1]
                        eng.wait_ge(u_scaled, UPD0[ku] + i)
                        eng.tensor_tensor(x[:, t, :], x[:, t, :], y[:, t, :], ALU.add).then_inc(x_odd, 1)
                    if kn is not None and 0 <= i - 2 < n:
                        rstd(stat, tiles[i - 2], n_mean, NORM_ROW0[kn] + i - 2, n_rstd)

            eng.memset(s4[:, :, :].bitcast(F), 0.0).then_inc(zeroed, 1)
            eng.memset(mhalf[:, :], -0.5).then_inc(zeroed, 1)
            eng.wait_ge(zeroed, 2)
            for i in range(TT):
                rstd(stat, i, n_mean, i, n_rstd)
            for cc in range(3):
                w = HALF if cc < 2 else 2 * P
                for i in range(TT - CT):
                    r = 4 * cc + i
                    eng.wait_ge(rope_mul, 3 * (r + 1))
                    eng.tensor_tensor(qrot[:, i, 0:w], qrot[:, i, 0:w], rtmp[:, r % 2, 0:w], ALU.add).then_inc(rope_done, 1)
            update_norm(0, 1)
            wait_x(eng, 0, 4)
            wait_x(eng, 0, 5)
            eng.memset(y[:, :, :], 0.0).then_inc(down_add[0], ZEROED)
            update_norm(1, 2)
            for n in range(NBLK):
                for e in (2 * n, 2 * n + 1):
                    for m in range(2):
                        s, d = 2 * e + m, e % 2
                        eng.wait_ge(decay_exp, s + 1)
                        if s >= 2:
                            eng.wait_ge(v_r, s - 1)
                        eng.tensor_tensor(a2[m][:, :], aa[d][:, m, :], aa[d][:, m, :], ALU.mult).then_inc(a_sq, 1)
                        eng.wait_ge(sig, 4 * e + 2 * m + 2)
                        eng.tensor_tensor(ii[d][:, m, :], ii[d][:, m, :], u[:, m, :], ALU.mult).then_inc(iu_r, 1)
                for m in range(2):
                    eng.wait_ge(scan_r, 8 * n + 4 + 2 * m + 2)
                    eng.tensor_tensor(hsum[:, m, :], hsum[:, m, :], ii[1][:, m, CTX:TOK], ALU.add).then_inc(h_r, 1)
                    eng.wait_ge(h_r, 2 * n + m + 1)
                    eng.wait_ge(in_act, 6 * n + 5 + m)
                    eng.tensor_tensor(z[:, 2 * n + m, :], hsum[:, m, :], z[:, 2 * n + m, :], ALU.mult).then_inc(z_r, 1)
            update_norm(2, 3)
            wait_x(eng, 2, 2)
            wait_x(eng, 2, 3)
            eng.memset(y[:, CT:TT, :], 0.0).then_inc(down_add[1], ZEROED)
            update_norm(3, None)

        @block.tensor
        def _(eng):
            def mm3(to, a_hi, a_lo, b_hi, b_lo, start, stop):
                eng.matmul(to, a_hi, b_hi, start=start, stop=False)
                eng.matmul(to, a_hi, b_lo, start=False, stop=False)
                return eng.matmul(to, a_lo, b_hi, start=False, stop=stop)

            def ready(n, v=0):
                eng.wait_ge(w_lo, n + 1 + v * 12)

            def ada_sums(a):
                acc, res = ada_banks(a)
                if a >= 4:
                    eng.wait_ge(ada_done, a)
                elif a >= 2:
                    eng.wait_ge(row_moved, a - 1)
                for j in range(4):
                    n = AT["ada", a] + j
                    ready(n)
                    for kk in range(2):
                        k = 2 * j + kk
                        for part in (whi, wlo):
                            ins = eng.matmul(ps[:, acc, :], s4[:, k, :], part[:, n % RING, kk * HALF:(kk + 1) * HALF],
                                             start=(k == 0 and part is whi), stop=(k == KT - 1 and part is wlo))
                    ins.then_inc(w_used, 1)

            def ada_result(a):
                li, c = a // 12, a % 12
                acc, res = ada_banks(a)
                if a:
                    eng.wait_ge(ada_done, a)
                eng.wait_ge(row_moved, a + 1)
                eng.wait_ge(bias_landed[a % 2], 16 * (a // 2 + 1))
                if c // 2 in (2, 5):
                    for v in range(2 if li == 0 else 1):
                        ins = eng.matmul(ps[:, res if v == 0 else acc, :], selb[:, v, :], modrow[:, a % 2, :], start=True, stop=True)
                else:
                    for t in range(4):
                        ins = eng.matmul(ps[:, res, 2 * t:2 * t + 2], modrow[:, a % 2, t * P:(t + 1) * P], selc[:, :],
                                         start=True, stop=True)
                ins.then_inc(ada_out, 1)

            def norm_transposes(k):
                rows, seq = NORM_ROW0[k], NORM_TR0[k]
                for t0, t1 in NORM_GRP[k]:
                    rows += t1 - t0
                    eng.wait_ge(n_row, rows)
                    if k == 2 and t0 == 0:
                        eng.wait_ge(down_add[0], 12 * (HT // 2) + ZEROED)
                    for ct in range(KT):
                        if seq >= NORM_TR0[k] + 8:
                            eng.wait_ge(n_tmp, seq - 7)
                        for t in range(t0, t1):
                            ins = eng.transpose(ps[:, seq % 8, (t - t0) * P:(t - t0 + 1) * P],
                                                hrow[:, t, ct * P:(ct + 1) * P], ident[:, :])
                        ins.then_inc(n_tr, 1)
                        seq += 1
                return seq - KT

            def token_major(name, tiles, acc, bank):
                for j in acc:
                    n = AT[name, j]
                    ready(n)
                    for kk in range(2):
                        k = 2 * (j % 4) + kk
                        for i, t in enumerate(tiles):
                            bank_no = bank(j, i)
                            h_hi, h_lo = hi[:, k, t * P:(t + 1) * P], lo[:, k, t * P:(t + 1) * P]
                            w = slice(kk * HALF, (kk + 1) * HALF)
                            if k == 0:
                                yield j, i
                            ins = mm3(ps[:, bank_no, :], h_hi, h_lo, whi[:, n % RING, w], wlo[:, n % RING, w],
                                      k == 0, k == KT - 1)
                    ins.then_inc(w_used, 1)

            def channel_major(n, parts, col0=0, v=0, kts=range(KT), src=None, norm_seq=None):
                src_hi, src_lo = src if src else (hi, lo)
                for i, k in enumerate(kts):
                    if norm_seq is not None:
                        eng.wait_ge(n_lo, norm_seq + k + 1)
                    w_h = whi[:, n % RING, col0 + i * P:col0 + (i + 1) * P]
                    w_l = wlo[:, n % RING, col0 + i * P:col0 + (i + 1) * P]
                    for to, tok in parts:
                        ins = mm3(to, w_h, w_l, src_hi[:, k, tok], src_lo[:, k, tok], i == 0, i == len(kts) - 1)
                return ins

            def ffn(li, norm_seq):
                b = AT["ffn", li]
                tiles = UPDATES[2 * li + 1][2]
                nd = 2 * len(tiles)
                cuts = [(0, 384), (384, 768)] if li == 0 else [(CTX, TOK)]

                def up(n0, i, t, v, first):
                    for s in range(2):
                        n = n0 + 2 * t + s
                        ready(n, v)
                        if s == 0 and not first:
                            if t == 0:
                                eng.wait_ge(down_add[li], nd * (i - 1) + ZEROED - (4 - len(cuts)))
                                eng.wait_ge(prod_r[li], 2 * i - 1)
                            else:
                                eng.wait_ge(prod_r[li], 2 * i)
                        if s == 1 and t == 0 and not first:
                            eng.wait_ge(down_add[li], nd * (i - 1) + ZEROED)
                        parts = [(ps[:, 4 * t + 2 * s + k, 0:c1 - c0], slice(c0, c1)) for k, (c0, c1) in enumerate(cuts)]
                        if first and t == 0 and s == 0:
                            eng.wait_ge(n_tmp, norm_seq + 2)
                        channel_major(n, parts, norm_seq=norm_seq if first and t == 0 and s == 0 else None).then_inc(w_used, 1)

                def down(n, j, par, v):
                    ready(n + 1, v)
                    eng.wait_ge(alo_r[li], 2 * j + 2)
                    if not isinstance(j, int) or j < HT // 2 - 1:
                        eng.wait_ge(prod_r[li], 2 * j + 3)
                    for o in range(nd):
                        if o >= 4:
                            eng.wait_ge(down_add[li], nd * j + o - 3 + ZEROED)
                        tk = slice((o // 2) * P, (o // 2 + 1) * P)
                        w = slice((o % 2) * HALF, (o % 2 + 1) * HALF)
                        for t in range(2):
                            s = (n + t) % RING
                            ins = mm3(ps[:, o % 4, :], ahi[:, par, t, tk], alo[:, par, t, tk], whi[:, s, w], wlo[:, s, w],
                                      t == 0, t == 1)
                            if o == nd - 1:
                                ins.then_inc(w_used, 1)
                        if o < nd - 1:
                            ins.then_inc(down_mm[li], 1)

                for t in range(2):
                    up(b, 0, t, 0, True)
                with eng.Fori(0, 5) as v:
                    for s in range(2):
                        n0, i = b + 4 + 6 * s, 1 + s + 2 * v
                        for t in range(2):
                            up(n0, i, t, v, False)
                        down(n0 + 4, s + 2 * v, s, v)
                eng.wait_ge(down_add[li], nd * (HT // 2 - 1) + ZEROED)
                down(b + 64, HT // 2 - 1, 0, 0)

            eng.wait_ge(c_landed, 48)
            eng.transpose(ps[:, 7, 0:16], stage_c[:, :], ident[0:16, 0:16]).then_inc(start_tr, 1)
            eng.wait_ge(cols_landed, 16 * 9)
            eng.transpose(ps[:, 4, 0:NCOL], stage[:, :], ident[0:NCOL, 0:NCOL]).then_inc(start_tr, 1)
            eng.wait_ge(s4_done, 2)
            eng.wait_ge(sel_landed, 32)
            eng.wait_ge(cols_done, 1)
            for a in range(4):
                ada_sums(a)
                if a:
                    ada_result(a - 1)
            ada_result(3)
            eng.wait_ge(ada_done, 4)
            seq = norm_transposes(0)
            eng.wait_ge(n_lo, seq + KT)

            def qk_transposes(cc):
                nh = 4 if cc < 2 else 2
                eng.wait_ge(ada_done, {0: 7, 1: 9, 2: 9}[cc])
                for t in range(TT):
                    s = 6 * cc + t
                    if t < CT:
                        eng.wait_ge(qkv_moved, 6 * cc + t + 1 if cc < 2 else 12 + 2 * t + 1)
                        src = qraw[:, t, :]
                    else:
                        eng.wait_ge(rope_done, 4 * cc + t - CT + 1)
                        src = qrot[:, t - CT, :]
                    if s >= 2:
                        eng.wait_ge(qk_moved, s - 1)
                    for h in range(nh):
                        ins = eng.transpose(ps[:, 6 + s % 2, h * P:(h + 1) * P], src[:, h * P:(h + 1) * P], ident[:, :])
                    ins.then_inc(qk_tr, 1)

            for j in range(12):
                for jj, i in token_major("qkv", range(TT), [j], lambda j, i: i):
                    if jj >= 4:
                        eng.wait_ge(qkv_moved, 6 * (jj // 4 - 1) + i + 1)
                for a in QKV_ADA.get(j - 1, ()):
                    ada_result(a)
                for a in QKV_ADA.get(j, ()):
                    if j >= 6:
                        eng.wait_ge(qk_moved, 6)
                    ada_sums(a)
                if j in (5, 9):
                    qk_transposes((j - 5) // 4)
            qk_transposes(2)

            eng.wait_ge(qkv_moved, 24)
            eng.wait_ge(qk_moved, 18)

            def scores(u):
                t, g, h0, w0, nw = UNITS[u]
                k = 3 * (u % 2)
                if u >= 2:
                    eng.wait_ge(s_ctx, u - 1)
                    if u - 2 >= NCU:
                        eng.wait_ge(s_win, u - 2 - NCU + 1)
                    elif nw:
                        eng.wait_ge(ada_done, 12)
                for h in range(2):
                    q = qT[:, h0 + h, t * P:(t + 1) * P]
                    ins = eng.matmul(ps[:, k, h * CTX:(h + 1) * CTX], q, kT[:, g, 0:CTX], start=True, stop=True)
                    if nw:
                        ins = eng.matmul(ps[:, k + 1 + h, 0:nw * P], q, kT[:, g, w0 * P:(w0 + nw) * P],
                                         start=True, stop=True)
                ins.then_inc(s_mm, 1)

            def turn(u, i):
                q = GR0[u] + i
                if q:
                    eng.wait_ge(p_moved, q)
                for k in range(len(GRPS[u][i])):
                    for h in range(2):
                        ins = eng.transpose(ps[:, 6, (2 * k + h) * P:(2 * k + h + 1) * P],
                                            S[:, u % SR, h, (2 * i + k) * P:(2 * i + k + 1) * P], ident[:, :])
                ins.then_inc(p_tr, 1)

            def values(u, i):
                q, g = GR0[u] + i, UNITS[u][1]
                eng.wait_ge(p_moved, q + 1)
                if i == 0 and u:
                    eng.wait_ge(o_hi, u)
                    eng.wait_ge(o_lo, u)
                for k, kt in enumerate(GRPS[u][i]):
                    ins = eng.matmul(ps[:, 7, 0:2 * P], V[:, kt, g * P:(g + 1) * P], PT[:, q % PR, 2 * k * P:2 * (k + 1) * P],
                                     start=(i == 0 and k == 0), stop=(i == len(GRPS[u]) - 1 and k == len(GRPS[u][i]) - 1))
                ins.then_inc(pv_mm, 1)

            scores(0)
            scores(1)
            for un in range(NU):
                eng.wait_ge(s_prob, 2 * (un + 1))
                for i in range(len(GRPS[un])):
                    turn(un, i)
                    if i == 0 and un + 2 < NU:
                        scores(un + 2)
                    if i:
                        values(un, i - 1)
                values(un, len(GRPS[un]) - 1)
                if un - 1 in UNIT_ADA:
                    ada_result(UNIT_ADA[un - 1])
                if un in UNIT_ADA:
                    ada_sums(UNIT_ADA[un])

            eng.wait_ge(o_hi, len(UNITS))
            eng.wait_ge(o_lo, len(UNITS))
            for j in range(8):
                for jj, i in token_major("o", range(TT), [j], lambda j, i: i):
                    if jj >= 4:
                        eng.wait_ge(y_moved, i + 1)
                for a in O_ADA.get(j - 1, ()):
                    ada_result(a)
                for a in O_ADA.get(j, ()):
                    ada_sums(a)
            eng.wait_ge(ada_done, 16)
            ffn(0, norm_transposes(1))
            norm_seq = norm_transposes(2)
            eng.wait_ge(n_tmp, norm_seq + 4)

            for n in range(NBLK):
                for j in range(4):
                    c = AT["in", n, j]
                    ready(c)
                    if j == 1 and n:
                        eng.wait_ge(sig, 8 * n)
                    if j == 2 and n == 0:
                        eng.wait_ge(n_tmp, norm_seq + 6)
                    if j < 2:
                        parts = [(ps[:, 2 - 2 * j, 0:CTX], slice(0, CTX)), (ps[:, 3 - 2 * j, :], slice(CTX, TOK))]
                    else:
                        parts = [(ps[:, 2 + j, :], slice(CTX, TOK))]
                    channel_major(c, parts, norm_seq=norm_seq if n == 0 and j == 0 else None).then_inc(w_used, 1)
                    if j == 2:
                        ada_result(16 + 2 * n)
                    if j in IN_ADA:
                        ada_sums(IN_ADA[j] + 2 * n)
                eng.wait_ge(u_lo, 2 * n + 2)
                for d in range(2):
                    c, e = AT["bd", n, d], 2 * n + d
                    ready(c)
                    for m in range(2):
                        for g in range(2):
                            s = 4 * e + 2 * m + g
                            if s >= 2:
                                eng.wait_ge(sig, s - 1)
                            for k in range(2):
                                at_w = (2 * g + k) * 2 * P + m * P
                                w_h, w_l = whi[:, c % RING, at_w:at_w + P], wlo[:, c % RING, at_w:at_w + P]
                                for to, tok in ((ps[:, 4 * g, 0:384], slice(0, 384)),
                                                (ps[:, 4 * g + 1, 0:384], slice(384, 768))):
                                    ins = mm3(to, w_h, w_l, uhi[:, k, tok], ulo[:, k, tok], k == 0, k == 1)
                            ins.then_inc(bd_mm if 2 * m + g < 3 else w_used, 1)
                    if d == 0:
                        ada_result(17 + 2 * n)
            eng.wait_ge(z_lo, KT - 2)
            eng.wait_ge(sig, 4 * 2 * NBLK)
            eng.wait_ge(ada_done, 24)
            for jj, (half, pair) in enumerate(OUT_ORDER):
                if pair == 3:
                    eng.wait_ge(z_lo, KT)
                n = AT["out", jj]
                ready(n)
                for kk in range(2):
                    k, w = 2 * pair + kk, slice(kk * HALF, (kk + 1) * HALF)
                    for i in range(4):
                        tok = slice((CT + i) * P, (CT + i + 1) * P)
                        ins = mm3(ps[:, 4 * half + i, :], hi[:, k, tok], lo[:, k, tok], whi[:, n % RING, w], wlo[:, n % RING, w],
                                  k == 0, k == KT - 1)
                ins.then_inc(w_used, 1)
            ffn(1, norm_transposes(3))


_TRUNK_INS = ["x", "c", "ctx", "c_ctx", "ada_w", "ada_b", "norm_g", "ffn_w_gu", "ffn_w_down", "a_w_qkv", "a_sinks",
              "a_w_o", "b_w_in", "b_conv_w", "b_conv_b", "b_lam", "b_w_a", "b_b_a", "b_w_x", "b_b_x", "b_w_out"]


def shape_constants():
    pos = np.arange(SEQ)
    inv = (1.0 / (np.float32(ROPE_BASE) ** (np.arange(0, 64, 2, dtype=np.float32) / np.float32(64)))).astype(np.float32)
    ang = np.stack([(pos // GRID_W).astype(np.float32)[:, None] * inv, (pos % GRID_W).astype(np.float32)[:, None] * inv], 1)
    cos, sin = np.cos(ang), np.sin(ang)
    c = np.stack([cos, cos], 2).reshape(SEQ // P, P, P).transpose(1, 0, 2)
    s = np.stack([-sin, sin], 2).reshape(SEQ // P, P, P).transpose(1, 0, 2)
    i, j = np.arange(P)[:, None], np.arange(3 * P)[None, :]
    mask = np.where(np.abs(j - P - i) <= P, 0.0, NEG)
    sel = np.zeros((5, 2, P))
    sel[[0, 1, 4], 0] = 1.0
    sel[[2, 3, 4], 1] = 1.0
    made = {"rope_c": c, "rope_s": s, "win_mask": mask, "eye": np.eye(P), "sel": sel, "sel_c": sel[:, :, 0]}
    return {k: np.ascontiguousarray(v, dtype=np.float32) for k, v in made.items()}


def kernel(**inputs):
    import concourse.bacc as bacc
    from concourse.bass_utils import run_bass_kernel_spmd

    nc = bacc.Bacc("TRN2", target_bir_lowering=False, num_devices=1)
    arrays, args = {}, []
    for name in _TRUNK_INS:
        arrays[f"in_{name}"] = np.ascontiguousarray(inputs[name])
    arrays.update({f"const_{k}": v for k, v in shape_constants().items()})
    for name, a in arrays.items():
        args.append(nc.dram_tensor(name, a.shape, mybir.dt.from_np(a.dtype), kind="ExternalInput").ap())
    args.append(nc.dram_tensor("out_latents", (1, SEQ, D), F, kind="ExternalOutput").ap())
    trunk(nc, *args)
    r = run_bass_kernel_spmd(nc, [arrays], core_ids=[0])
    return r.results[0]["out_latents"]
```

```python
from contextlib import ExitStack

import numpy as np

import concourse.bass as bass
from concourse import mybir

F = mybir.dt.float32
R = mybir.dt.float32r
ALU = mybir.AluOpType
ACT = mybir.ActivationFunctionType
AX = mybir.AxisListType.X

P = 128
D = 1024
KT = D // P
SEQ, CTX = 512, 256
TOK = CTX + SEQ
TT = TOK // P
CT = CTX // P
HID = 2816
HT = HID // P
HEADS, KVH, GROUP = 8, 2, 4
SCALE = float(P) ** -0.5
EPS = 1e-6
CH = 1024
RING = 3
HALF = 512
NEG = -1.0e30
GRID_W, ROPE_BASE = 64, 10000.0
NBLK = 4

C_G, C_CW, C_CB, C_LAM, C_BA, C_BX, NCOL = 0, 32, 64, 72, 88, 104, 120


QKV_PIECES = {j: [(4 + j // 2, 2 * (j % 2) + i) for i in range(2)] for j in range(6)}
QKV_PIECES.update({7: [(7, 0), (7, 1)], 8: [(7, 2), (7, 3)], 9: [(8, i) for i in range(4)]})
QKV_RESULT = {2: 4, 4: 5, 6: 6, 9: 7, 10: 8}
QK_TURNS = {6: 0, 10: 1}
UNIT_PIECES = {u: [(9 + u // 2, 2 * (u % 2) + i) for i in range(2)] for u in range(6)}
UNIT_RESULT = {2: 9, 4: 10, 6: 11}
O_PIECES = {j: [(12 + j // 2, 2 * (j % 2) + i) for i in range(2)] for j in range(8)}
O_RESULT = {2: 12, 4: 13, 6: 14}
X_AFTER = {(0, 2): (0, 1), (0, 3): (2,), (1, 0): (3,), (1, 1): (4,), (1, 2): (5,)}
RG_STREAM = (("in", 0), ("ada", 0, 0), ("ada", 0, 1), ("in", 1), ("ada", 0, 2), ("ada", 0, 3), ("in", 2), ("ada", 1, 0),
             ("in", 3), ("ada", 1, 1), ("bd", 0), ("ada", 1, 2), ("bd", 1), ("ada", 1, 3))
OUT_ORDER = [(0, 0), (0, 1), (0, 2), (1, 0), (1, 1), (1, 2), (0, 3), (1, 3)]


def plan():
    order = [(("ada", a, i), 1) for a in range(4) for i in range(4)]
    for j in range(12):
        order.append((("qkv", j), 1))
        order += [(("ada", a, i), 1) for a, i in QKV_PIECES.get(j, ())]
    order += [(("ada", a, i), 1) for u in range(6) for a, i in UNIT_PIECES[u]]
    for j in range(8):
        order.append((("o", j), 1))
        order += [(("ada", a, i), 1) for a, i in O_PIECES[j]]
    order.append((("ffn", 0), 3 * HT))
    for n in range(NBLK):
        for step in RG_STREAM:
            key = ("ada", 16 + 2 * n + step[1], step[2]) if step[0] == "ada" else (step[0], n, step[1])
            order.append((key, 1))
    order += [(("out", j), 1) for j in range(8)]
    order.append((("ffn", 1), 3 * HT))
    at, n = {}, 0
    for key, count in order:
        at[key] = n
        n += count
    return order, at, n


ORDER, AT, CHUNKS = plan()


def landed_table():
    count, got = [0] * RING, []
    for key, number in ORDER:
        for _ in range(number):
            n = len(got)
            count[n % RING] += 32 if key[0] == "bd" else 16
            got.append(count[n % RING])
    return got


LANDED = landed_table()

NORMS = [(0, 0, range(0, TT)), (0, 1, range(0, TT)), (1, 0, range(0, TT)), (1, 1, range(CT, TT))]
UPDATES = [(0, 0, range(0, TT)), (0, 1, range(0, TT)), (1, 0, range(CT, TT)), (1, 1, range(CT, TT))]
NORM_ROW0 = [0, 6, 12, 18]
NORM_GRP = [[(0, 2), (2, 6)], [(0, 2), (2, 6)], [(0, 2), (2, 6)], [(2, 6)]]
NORM_TR0 = [0, 16, 32, 48]
UPD0 = [0, 6, 12, 16]

UNITS = []
for t in range(TT):
    w0 = 0 if t < CT else max(t - 1, CT)
    nw = 0 if t < CT else min(t + 1, TT - 1) - w0 + 1
    UNITS += [(t, h // GROUP, h, w0, nw) for h in range(0, HEADS, 2)]
NU = len(UNITS)
NCU = CT * HEADS // 2
GRPS = []
for _, _, _, w0, nw in UNITS:
    kts = list(range(CT)) + list(range(w0, w0 + nw))
    GRPS.append([kts[k:k + 2] for k in range(0, len(kts), 2)])
GR0 = [sum(len(k) for k in GRPS[:u]) for u in range(NU + 1)]
SR, PR = 4, 5


def ada_banks(a):
    if a < 4:
        return 6 - a % 2, 7
    return (1, 2) if a in UNIT_RESULT.values() else (6, 7)


def norm_parts(grp, c0=0, c1=KT):
    return [(grp, ct) for ct in range(c0, c1)]


def lag(ku):
    return 3 if ku == 2 else 2


def norm_bank(k, grp, ct):
    return 4 + ct % 4 if k == 2 and grp == 0 else ct


ZEROED = 4


def trunk(nc, x_in, c_in, ctx_in, cctx_in, ada_w, ada_b, norm_g, w_gu, w_down, w_qkv, sinks, w_o,
          b_w_in, conv_w, conv_b, lam, w_a, b_a, w_x, b_x, b_w_out,
          rope_c, rope_s, win_mask, eye, sel, sel_c, out):
    with ExitStack() as st:
        def sem(name):
            return st.enter_context(nc.semaphore(name))

        def sb(name, shape, dt=F):
            return st.enter_context(nc.sbuf_tensor(name, shape, dt))

        hi = sb("hT_hi", [P, KT, TOK], R)
        lo = sb("hT_lo", [P, KT, TOK], R)
        raw = sb("w_raw", [P, RING, CH])
        whi = sb("w_hi", [P, RING, CH], R)
        wlo = sb("w_lo", [P, RING, CH], R)
        ident = sb("ident", [P, P])
        selb = sb("sel_rows", [5, 2, P])
        selc = sb("sel_cols", [5, 2])
        s4 = sb("silu_parts", [P, KT, P], R)
        silu_c = sb("silu_c", [P, 2, KT])
        stage = sb("stage_rows", [NCOL, P])
        stage_c = sb("stage_c", [16, P])
        cols = sb("cols", [P, NCOL])
        mod = sb("mod_cols", [P, 2, 4, KT, 2])
        modrow = sb("mod_rows", [5, 2, HALF])
        stat = sb("stat", [P, 3, TT])
        ustat = sb("ustat", [P, 4, TT])
        mhalf = sb("minus_half", [P, 1])
        dec = sb("decay", [P, 2, 16])
        sp = sb("sp_work", [P, 5, 16])
        nsink = sb("neg_sinks", [P, HEADS])
        snk = sb("sinks_bc", [P, HEADS])
        smx = sb("row_max", [P, SR, 2])
        snm = sb("neg_max", [P, SR, 2])
        ssum = sb("row_sum", [P, SR, 2])
        ses = sb("sink_exp", [P, SR, 2])
        sri = sb("row_inv", [P, SR, 2])

        K = 1024
        g0 = (nc.sbuf_base + 63) // 64 * 64
        a0 = g0 + 40 * K

        def ar(name, off, shape, dt=F):
            return nc.alloc_sbuf_tensor_at(name, shape, dt, offset=a0 + off)

        gate = ar("gate_rows", -40 * K, [P, 2, 2, D])
        x = ar("x", -24 * K, [P, TT, D])
        y = ar("y", 0, [P, TT, D])
        hrow = ar("h_rows", 24 * K, [P, TT, D])
        ntmp = ar("norm_tmp", 48 * K, [P, 4, HALF])
        junk = ar("square_out", 62 * K, [P, D])
        qT = ar("qT", 0, [P, HEADS, TOK])
        kT = ar("kT", 24 * K, [P, KVH, TOK])
        V = ar("V", 30 * K, [P, TT, 2 * P])
        qraw = ar("q_raw", 36 * K, [P, TT, HALF])
        qrot = ar("q_rot", 48 * K, [P, TT - CT, HALF])
        rc = ar("rope_cos", 56 * K, [P, TT - CT, P])
        rs = ar("rope_sin", 58 * K, [P, TT - CT, P])
        rtmp = ar("rope_tmp", 60 * K, [P, 2, HALF])
        S = ar("scores", 36 * K, [P, SR, 2, 5 * P])
        PT = ar("probsT", 56 * K, [P, PR, HALF])
        mask = ar("mask", 66 * K, [P, 3 * P])
        ahi = ar("act_hi", 24 * K, [P, 2, 2, TOK], R)
        alo = ar("act_lo", 36 * K, [P, 2, 2, TOK], R)
        sg = ar("act", 48 * K, [P, 2, TOK])
        u = ar("conv_out", 0, [P, 2, TOK])
        uhi = ar("conv_hi", 6 * K, [P, 2, TOK], R)
        ulo = ar("conv_lo", 12 * K, [P, 2, TOK], R)
        hsum = ar("h_sum", 18 * K, [P, 2, SEQ])
        z = ar("z", 24 * K, [P, KT, SEQ])
        rr = [ar("gate_r0", 40 * K, [P, 2, TOK]), ar("gate_r1", -32 * K, [P, 2, TOK])]
        ii = [ar("gate_i0", 46 * K, [P, 2, TOK]), ar("gate_i1", -26 * K, [P, 2, TOK])]
        aa = [ar("lru_a0", 52 * K, [P, 2, TOK]), ar("lru_a1", 58 * K, [P, 2, TOK])]
        a2 = [ar("lru_sq0", 64 * K, [P, TOK]), ar("lru_sq1", -20 * K, [P, TOK])]
        assert a0 + 68 * K <= nc.sbuf_usable_end

        ps = st.enter_context(nc.psum_tensor("ps", [P, 8, HALF], F))

        raw_landed = [sem(f"raw_landed{i}") for i in range(RING)]
        x_landed = [sem(f"x_landed{i}") for i in range(TT)]
        c_landed, cols_landed, rope_landed = sem("c_landed"), sem("cols_landed"), sem("rope_landed")
        gate_landed = [sem("gates0_landed"), sem("mixer_gate1_landed"), sem("ffn_gate1_landed")]
        sel_landed, att_landed = sem("sel_landed"), sem("att_landed")
        bias_landed = [sem("bias_landed0"), sem("bias_landed1")]
        w_hi, w_lo, w_used = sem("w_hi_ready"), sem("w_lo_ready"), sem("w_used")
        zeroed, start_tr, silu_done, s4_done, cols_done = (
            sem("zeroed"), sem("start_tr"), sem("silu_done"), sem("s4_done"), sem("cols_done"))
        sp_act, sp_dve = sem("sp_act"), sem("sp_dve")
        row_moved, ada_out, ada_done, ada_step = sem("row_moved"), sem("ada_out"), sem("ada_done"), sem("ada_step")
        n_ssq, n_mean, n_rstd, n_row = sem("n_ssq"), sem("n_mean"), sem("n_rstd"), sem("n_row")
        n_tr, n_hi, n_tmp, n_lo = sem("n_tr"), sem("n_hi"), sem("n_tmp"), sem("n_lo")
        u_ssq, u_mean, u_rstd, u_scaled, x_added = (
            sem("u_ssq"), sem("u_mean"), sem("u_rstd"), sem("u_scaled"), sem("x_added"))
        qkv_moved, rope_mul, rope_done, qk_tr, qk_moved = (
            sem("qkv_moved"), sem("rope_mul"), sem("rope_done"), sem("qk_tr"), sem("qk_moved"))
        s_mm, s_ctx, s_win, s_max, s_neg, s_exp, s_den, s_inv, s_prob = (
            sem("s_mm"), sem("s_ctx"), sem("s_win"), sem("s_max"), sem("s_neg"), sem("s_exp"),
            sem("s_den"), sem("s_inv"), sem("s_prob"))
        p_tr, p_moved, pv_mm, o_hi, o_lo = sem("p_tr"), sem("p_moved"), sem("pv_mm"), sem("o_hi"), sem("o_lo")
        y_moved, tile_done, half_ssq, half_mean = sem("y_moved"), sem("tile_done"), sem("half_ssq"), sem("half_mean")
        silu_r, prod_r, ahi_r, alo_r, down_mm, down_add = [], [], [], [], [], []
        for i in range(2):
            silu_r.append(sem(f"silu_ready{i}"))
            prod_r.append(sem(f"prod_ready{i}"))
            ahi_r.append(sem(f"act_hi_ready{i}"))
            alo_r.append(sem(f"act_lo_ready{i}"))
            down_mm.append(sem(f"down_mm{i}"))
            down_add.append(sem(f"down_added{i}"))
        in_act, conv, u_hi, u_lo = sem("in_act"), sem("conv"), sem("u_hi"), sem("u_lo")
        bd_mm, sig, decay_exp, tanh_r, a_sq, iu_r, v_r, sqrt_r, b_r, scan_r, h_r, z_r, z_hi, z_lo = (
            sem("bd_mm"), sem("sigmoid"), sem("decay_exp"), sem("tanh_r"), sem("a_sq"), sem("iu_r"),
            sem("v_r"), sem("sqrt_r"), sem("b_r"), sem("scan_r"), sem("h_r"), sem("z_r"),
            sem("z_hi"), sem("z_lo"))
        out_sent = sem("out_sent")

        def wait_x(eng, k, i):
            eng.wait_ge(x_added, UPD0[k] + i + 1)

        def out_banks(i):
            return ps[:, 2 * i:2 * i + 2, :]

        def landed_value(n, v=0):
            return LANDED[n] + v * (16 * 12 // RING)

        def gu_src(li, q, up):
            s = w_gu[li].rearrange("(k p) n -> p k n", p=P)
            return s[:, :, bass.ts(q + (HT if up else 0), P)]

        def down_src(li, q):
            return w_down[li][bass.ts(q, P), :]

        block = st.enter_context(nc.Block())

        @block.sync
        def _(eng):
            def load(n, src, dst=None, v=0):
                if n >= RING:
                    eng.wait_ge(w_lo, n - RING + 1 + v * 12)
                to = raw[:, n % RING, :] if dst is None else dst(raw[:, n % RING, :])
                eng.dma_start(to, src).then_inc(raw_landed[n % RING], 16)

            def two_by(dst):
                return dst.rearrange("p (k n) -> p k n", k=2)

            def load_cols512(n, w, j, cc):
                load(n, w[2 * j * P:(2 * j + 2) * P, cc * HALF:(cc + 1) * HALF].rearrange("(k p) n -> p k n", p=P), two_by)

            def eight_by(dst):
                return dst.rearrange("p (k n) -> p k n", k=KT)

            def load_ada(a, j):
                li, c = a // 12, a % 12
                load_cols512(AT["ada", a, j], ada_w[li], j, c)
                if j < 3:
                    return
                if a >= 2:
                    eng.wait_ge(ada_out, a - 1)
                eng.dma_start(modrow[4:5, a % 2, :], ada_b[li:li + 1, c * HALF:(c + 1) * HALF]).then_inc(bias_landed[a % 2], 16)

            def load_gate_gain(li, m, v):
                g = norm_g[li, 2 * m + 1:2 * m + 2, :].to_broadcast((P, D))
                eng.dma_start(gate[:, v, m, :], g).then_inc(gate_landed[li + li * m], 16)

            def load_ffn(li):
                b = AT["ffn", li]

                def gu(n, q, v=0):
                    for t in range(2):
                        load(n + 2 * t, gu_src(li, q + t, False), eight_by, v)
                        load(n + 2 * t + 1, gu_src(li, q + t, True), eight_by, v)

                def down(n, q, v=0):
                    for t in range(2):
                        load(n + t, down_src(li, q + t), None, v)

                gu(b, 0)
                with eng.Fori(0, 5) as v:
                    for s in range(2):
                        gu(b + 4 + 6 * s, 4 * v + 2 + 2 * s, v)
                        down(b + 8 + 6 * s, 4 * v + 2 * s, v)
                down(b + 64, HT - 2)

            eng.dma_start(stage_c[0:8, :], c_in.rearrange("a (t p) -> (a t) p", p=P)).then_inc(c_landed, 16)
            eng.dma_start(stage_c[8:16, :], cctx_in.rearrange("(t p) -> t p", p=P)).then_inc(c_landed, 16)
            eng.dma_start(ident[:, :], eye).then_inc(c_landed, 16)
            gate_loads = [(0, m, v) for m in range(2) for v in range(2)]
            for key, count in ORDER:
                n = AT[key]
                if key[0] == "ada":
                    a, j = key[1:]
                    if a == 4 and j == 0:
                        for g in gate_loads:
                            load_gate_gain(*g)
                    if a in (16, 22) and j == 0:
                        eng.wait_ge(x_added, UPD0[2])
                        load_gate_gain(1, (a - 16) // 6, 0)
                    load_ada(a, j)
                    for t in X_AFTER.get((a, j), ()):
                        src = ctx_in[0, t * P:(t + 1) * P, :] if t < CT else x_in[0, (t - CT) * P:(t - CT + 1) * P, :]
                        eng.dma_start(x[:, t, :], src).then_inc(x_landed[t], 16)
                    if a == 0 and j == 2:
                        eng.dma_start(selb[:, :, :], sel).then_inc(sel_landed, 16)
                        eng.dma_start(selc[:, :], sel_c).then_inc(sel_landed, 16)
                elif key[0] == "qkv":
                    load_cols512(n, w_qkv[0], key[1] % 4, key[1] // 4)
                    if key[1] == 0:
                        eng.dma_start(rc[:, :, :], rope_c).then_inc(rope_landed, 16)
                        eng.dma_start(rs[:, :, :], rope_s).then_inc(rope_landed, 16)
                        eng.dma_start(mask[:, :], win_mask).then_inc(att_landed, 16)
                        eng.dma_start(snk[:, :], sinks[0:1, :].to_broadcast((P, HEADS))).then_inc(att_landed, 16)
                elif key[0] == "o":
                    load_cols512(n, w_o[0], key[1] % 4, key[1] // 4)
                elif key[0] == "out":
                    load_cols512(n, b_w_out[0], OUT_ORDER[key[1]][1], OUT_ORDER[key[1]][0])
                elif key[0] == "in":
                    _, b, j = key
                    m = 2 * b + j if j < 2 else KT + 2 * b + j - 2
                    load(n, b_w_in[0].rearrange("(k p) n -> p k n", p=P)[:, :, m * P:(m + 1) * P], eight_by)
                elif key[0] == "bd":
                    _, b, d = key
                    eng.wait_ge(w_lo, n - RING + 1)
                    slot = raw[:, n % RING, :].rearrange("p (g k n) -> p g k n", g=2, k=2)
                    for g, w in enumerate((w_a, w_x)):
                        eng.dma_start(slot[:, g], w[0, d, b].rearrange("(k p) n -> p k n", p=P)).then_inc(raw_landed[n % RING], 16)
                else:
                    load_ffn(key[1])
            for i, t in enumerate(range(CT, TT)):
                wait_x(eng, 3, i)
                eng.dma_start(out[0, (t - CT) * P:(t - CT + 1) * P, :], x[:, t, :]).then_inc(out_sent, 16)
            eng.wait_ge(out_sent, 16 * (TT - CT))

        @block.scalar
        def _(eng):
            done = [0]
            last_square = []

            def split(n, v=0):
                eng.wait_ge(raw_landed[n % RING], landed_value(n, v))
                if n >= RING:
                    eng.wait_ge(w_used, n - RING + 1 + v * 12)
                eng.activation(whi[:, n % RING, :], raw[:, n % RING, :], ACT.Copy).then_inc(w_hi, 1)

            def splits_to(end):
                while done[0] < min(end, CHUNKS):
                    split(done[0])
                    done[0] += 1

            def ada_row(a):
                n = AT["ada", a, 3]
                splits_to(n + (2 if a == 3 else 3))
                eng.wait_ge(w_used, n + 1)
                if a >= 2:
                    eng.wait_ge(ada_out, a - 1)
                eng.activation(modrow[0:4, a % 2, :], ps[0:4, ada_banks(a)[0], :], ACT.Copy).then_inc(row_moved, 1)

            def square(src, dst, signal, number):
                if last_square:
                    eng.wait_ge(*last_square[-1])
                to = junk[:, 0:HALF] if src.shape[-1] == HALF and len(src.shape) == 2 else junk[:, :]
                if len(src.shape) == 3:
                    to = to.rearrange("p (h w) -> p h w", h=2)
                eng.activation(to, src, ACT.Square, accum_out=dst).then_inc(signal, 1)
                last_square.append((signal, number + 1))

            def norm_square(k, i):
                t = NORMS[k][2][i]
                if k == 0:
                    eng.wait_ge(x_landed[t], 16)
                else:
                    wait_x(eng, k - 1, i)
                square(x[:, t, :], stat[:, 0, t:t + 1], n_ssq, NORM_ROW0[k] + i)

            def norm_row(k, i):
                t = NORMS[k][2][i]
                eng.wait_ge(n_rstd, NORM_ROW0[k] + i + 1)
                if k == 2 and i == 0:
                    eng.wait_ge(w_used, AT["ffn", 0] + 3 * HT)
                eng.activation(hrow[:, t, :], x[:, t, :], ACT.Copy, scale=stat[:, 2, t:t + 1]).then_inc(n_row, 1)

            def update_square(k, i, ready):
                t = UPDATES[k][2][i]
                ready(i)
                if k == 2:
                    src = out_banks(i)
                else:
                    src = y[:, t, HALF:D] if k == 0 else y[:, t, :]
                square(src, ustat[:, 0, t:t + 1], u_ssq, UPD0[k] + i)

            def projection_rows(half, t):
                if t < TT - 1:
                    eng.wait_ge(tile_done, (3 + half) * (TT - 1) + t + 1)
                else:
                    eng.wait_ge(w_used, AT["o", 4 * half + 3] + 1)
                eng.activation(y[:, t, half * HALF:(half + 1) * HALF], ps[:, t, :], ACT.Copy).then_inc(y_moved, 1)
                eng.wait_ge(y_moved, half * TT + t + 1)

            def out_tile(i):
                if i < 3:
                    eng.wait_ge(tile_done, 5 * (TT - 1) + i + 1)
                else:
                    eng.wait_ge(w_used, AT["out", 7] + 1)

            def norm_affine(k, parts):
                li, which, _ = NORMS[k]
                eng.wait_ge(ada_done, 12 * li + (4 if which == 0 else 10))
                for grp, ct in parts:
                    t0, t1 = NORM_GRP[k][grp]
                    v, seq = 1 if t0 == 0 else 0, NORM_TR0[k] + KT * grp + ct
                    eng.wait_ge(n_tr, seq + 1)
                    if seq >= 4:
                        eng.wait_ge(n_lo, seq - 3)
                    eng.activation(ntmp[:, seq % 4, 0:(t1 - t0) * P], ps[:, norm_bank(k, grp, ct), 0:(t1 - t0) * P],
                                   ACT.Identity, bias=mod[:, li, 2 * which, ct, v:v + 1],
                                   scale=mod[:, li, 2 * which + 1, ct, v:v + 1]).then_inc(n_tmp, 1)

            def update_norm(ku, kn, ready, between=lambda i: None):
                n = len(UPDATES[ku][2])
                for i in range(n + lag(ku) + 2):
                    between(i)
                    if i < n:
                        update_square(ku, i, ready)
                    if kn is not None and 0 <= i - lag(ku) < n:
                        norm_square(kn, i - lag(ku))
                    if kn is not None and 0 <= i - lag(ku) - 1 < n:
                        norm_row(kn, i - lag(ku) - 1)

            def ffn(li):
                b = AT["ffn", li]
                hw = 384 if li == 0 else HALF
                w = TOK if li == 0 else SEQ

                def gated(n0, q, t, v):
                    eng.wait_ge(w_used, n0 + 2 + 2 * t + v * 12)
                    if not isinstance(q, int) or q >= 2:
                        eng.wait_ge(alo_r[li], q - 1)
                    if li == 0:
                        g, o = ps[:, 4 * t:4 * t + 2, 0:hw], sg[:, t, 0:w].rearrange("p (h w) -> p h w", h=2)
                    else:
                        g, o = ps[:, 4 * t, 0:hw], sg[:, t, 0:w]
                    eng.activation(o, g, ACT.Silu).then_inc(silu_r[li], 1)
                    eng.wait_ge(prod_r[li], q + 1)

                def gated_hi(q, t, par):
                    eng.activation(ahi[:, par, t, 0:w], sg[:, t, 0:w], ACT.Copy).then_inc(ahi_r[li], 1)

                def step(n0, i, par, v):
                    for k in range(1, 5):
                        split(n0 + k, v)
                    gated(n0, 2 * i, 0, v)
                    gated_hi(2 * i, 0, par)
                    split(n0 + 5, v)
                    split(n0 + 6, v)
                    gated(n0, 2 * i + 1, 1, v)
                    gated_hi(2 * i + 1, 1, par)

                splits_to(b + 5)
                gated(b, 0, 0, 0)
                gated_hi(0, 0, 0)
                gated(b, 1, 1, 0)
                gated_hi(1, 1, 0)
                with eng.Fori(0, 5) as v:
                    for s in range(2):
                        step(b + 4 + 6 * s, 1 + s + 2 * v, (1 + s) % 2, v)
                done[0] = b + 65
                splits_to(b + 66)

            pieces = [(C_G + 8 * (2 * li + wh), norm_g[li, 2 * wh:2 * wh + 1, :], 8) for li in range(2) for wh in range(2)]
            pieces += [(C_CW, conv_w[0], 32), (C_CB, conv_b, 8), (C_LAM, lam[0], 16), (C_BA, b_a[0], 16), (C_BX, b_x[0], 16)]
            for row, src, n in pieces:
                eng.dma_start(stage[row:row + n, :], src.rearrange("a (t p) -> (a t) p", p=P)).then_inc(cols_landed, 16)
            eng.wait_ge(start_tr, 1)
            eng.activation(silu_c[:, :, :], ps[:, 7, 0:16].rearrange("p (v k) -> p v k", v=2), ACT.Silu).then_inc(silu_done, 1)
            splits_to(3)
            for a in range(4):
                ada_row(a)
                if a < 3:
                    norm_square(0, 2 * a)
                    norm_square(0, 2 * a + 1)
            norm_affine(0, norm_parts(0) + norm_parts(1))

            def qkv_move(cc):
                n = AT["qkv", 4 * cc + 3]
                splits_to(n + 3)
                if cc:
                    eng.wait_ge(qk_tr, 6 * cc)
                    eng.wait_ge(rope_mul, 12 * cc)
                for t in range(TT):
                    w = HALF if cc < 2 else 2 * P
                    if t < TT - 1:
                        eng.wait_ge(tile_done, (TT - 1) * cc + t + 1)
                    else:
                        eng.wait_ge(w_used, n + 1)
                    eng.activation(qraw[:, t, 0:w], ps[:, t, 0:w], ACT.Copy).then_inc(qkv_moved, 1)
                    if cc == 2:
                        eng.activation(V[:, t, :], ps[:, t, w:HALF], ACT.Copy).then_inc(qkv_moved, 1)

            def qk_move(cc):
                nh = 4 if cc < 2 else 2
                for t in range(TT):
                    s = 6 * cc + t
                    eng.wait_ge(qk_tr, s + 1)
                    dst = qT[:, 4 * cc:4 * cc + 4, t * P:(t + 1) * P] if cc < 2 else kT[:, :, t * P:(t + 1) * P]
                    src = ps[:, 6 + s % 2, 0:nh * P].rearrange("p (h q) -> p h q", h=nh)
                    eng.activation(dst, src, ACT.Copy).then_inc(qk_moved, 1)

            for j in range(12):
                splits_to(AT["qkv", j] + 3)
                if j % 4 == 3:
                    qkv_move(j // 4)
                for a, i in QKV_PIECES.get(j, ()):
                    if i == 3:
                        ada_row(a)
                if j in QK_TURNS:
                    qk_move(QK_TURNS[j])
            splits_to(AT["qkv", 11] + 4)
            qk_move(2)
            eng.wait_ge(sp_dve, 2)
            eng.activation(sp[:, 1, :], sp[:, 0, :], ACT.Exp, scale=-1.0).then_inc(sp_act, 1)

            def ctx_move(u):
                eng.wait_ge(s_mm, u + 1)
                if u >= SR:
                    eng.wait_ge(p_tr, GR0[u - SR + 1])
                eng.activation(S[:, u % SR, :, 0:CTX], ps[:, 3 * (u % 2), :].rearrange("p (h k) -> p h k", h=2),
                               ACT.Copy).then_inc(s_ctx, 1)

            def exps(u):
                t, g, h0, w0, nw = UNITS[u]
                b, nk = u % SR, CTX + nw * P
                eng.wait_ge(s_neg, 2 * (u + 1))
                for h in range(2):
                    eng.activation(S[:, b, h, 0:nk], S[:, b, h, 0:nk], ACT.Exp, bias=snm[:, b, h:h + 1],
                                   scale=SCALE, accum_out=ssum[:, b, h:h + 1]).then_inc(s_exp, 1)
                eng.activation(ses[:, b, :], ses[:, b, :], ACT.Exp).then_inc(s_exp, 1)

            def probs_move(u, i):
                q, w = GR0[u] + i, 2 * P * len(GRPS[u][i])
                eng.wait_ge(p_tr, q + 1)
                if q >= PR:
                    eng.wait_ge(pv_mm, q - PR + 1)
                eng.activation(PT[:, q % PR, 0:w], ps[:, 6, 0:w], ACT.Copy).then_inc(p_moved, 1)

            ctx_move(0)
            ctx_move(1)
            exps(0)
            for un, (t, g, h0, w0, nw) in enumerate(UNITS):
                if un + 1 < NU:
                    exps(un + 1)
                probs_move(un, 0)
                if un + 2 < NU:
                    ctx_move(un + 2)
                for i in range(1, len(GRPS[un])):
                    probs_move(un, i)
                eng.wait_ge(pv_mm, GR0[un + 1])
                eng.activation(hi[:, h0:h0 + 2, t * P:(t + 1) * P],
                               ps[:, 7, 0:2 * P].rearrange("p (h q) -> p h q", h=2), ACT.Copy).then_inc(o_hi, 1)
                for a, i in UNIT_PIECES.get(un, ()):
                    splits_to(AT["ada", a, i] + 2)
                    if i == 3:
                        ada_row(a)
            splits_to(AT["o", 0] + 3)

            for j in range(8):
                n = AT["o", j]
                splits_to(n + 3)
                if j == 3:
                    for i in range(TT):
                        projection_rows(0, i)
                        splits_to(n + 3 + min(i, 2))
                if j == 5:
                    for i in range(TT):
                        square(y[:, i, 0:HALF], ustat[:, 3, i:i + 1], half_ssq, i)
                if j % 2 and j < 7:
                    ada_row(12 + j // 2)

            def between(i):
                if i == 3:
                    ada_row(15)
                if i == 5:
                    splits_to(AT["ffn", 0] + 3)
                if i in (6, 9):
                    norm_affine(1, norm_parts(0, 0 if i == 6 else 4, 4 if i == 6 else KT))

            update_norm(0, 1, lambda i: projection_rows(1, i), between)
            norm_affine(1, norm_parts(1))
            ffn(0)

            update_norm(1, 2, lambda i: eng.wait_ge(down_add[0], 12 * (HT // 2 - 1) + 2 * i + 2 + ZEROED),
                        lambda i: splits_to(AT["in", 0, 0] + 1) if i == 0 else
                        norm_affine(2, norm_parts(0, 0 if i == 6 else 4, 4 if i == 6 else KT)) if i in (6, 9) else None)
            norm_affine(2, norm_parts(1, 0, 3))
            splits_to(AT["in", 0, 0] + 3)
            norm_affine(2, norm_parts(1, 3))

            def z_hi_parts(tiles):
                for ct in tiles:
                    eng.wait_ge(z_r, ct + 1)
                    eng.activation(hi[:, ct, CTX:TOK], z[:, ct, :], ACT.Copy).then_inc(z_hi, 1)

            def conv_start(n, j):
                q, k = 2 * n + j, 2 - 2 * j
                eng.wait_ge(w_used, AT["in", n, j] + 1)
                if n:
                    eng.wait_ge(iu_r, 4 * n)
                    eng.wait_ge(u_lo, 2 * n)
                w1, cb = cols[:, C_CW + 8 + q:C_CW + 9 + q], cols[:, C_CB + q:C_CB + q + 1]
                eng.activation(u[:, j, 0:CTX], ps[:, k, 0:CTX], ACT.Identity, bias=cb, scale=w1).then_inc(in_act, 1)
                eng.activation(u[:, j, CTX:TOK], ps[:, k + 1, :], ACT.Identity, bias=cb, scale=w1).then_inc(in_act, 1)

            def conv_hi(n, j):
                eng.wait_ge(conv, 6 * (2 * n + j + 1))
                if n:
                    eng.wait_ge(w_used, AT["bd", n - 1, 1] + 1)
                eng.activation(uhi[:, j, :], u[:, j, :], ACT.Copy).then_inc(u_hi, 1)

            def gelu(n, j):
                eng.wait_ge(w_used, AT["in", n, 2 + j] + 1)
                eng.activation(z[:, 2 * n + j, :], ps[:, 4 + j, :], ACT.Gelu_apprx_tanh).then_inc(in_act, 1)

            def sigmoids(n, d):
                e = 2 * n + d
                if n:
                    eng.wait_ge(scan_r, 4 * (e - 1))
                    if d:
                        eng.wait_ge(h_r, 2 * n)
                for m in range(2):
                    for g, (dst, col) in enumerate(((rr, C_BA), (ii, C_BX))):
                        s = 2 * m + g
                        if s < 3:
                            eng.wait_ge(bd_mm, 3 * e + s + 1)
                        else:
                            eng.wait_ge(w_used, AT["bd", n, d] + 1)
                        bias = cols[:, col + 8 * d + 2 * n + m:col + 8 * d + 2 * n + m + 1]
                        eng.activation(dst[d][:, m, :].rearrange("p (h w) -> p h w", h=2),
                                       ps[:, 4 * g:4 * g + 2, 0:384], ACT.Sigmoid, bias=bias).then_inc(sig, 1)

            def decays(n, d):
                e = 2 * n + d
                for m in range(2):
                    k, s = 8 * d + 2 * n + m, 2 * e + m
                    eng.wait_ge(sig, 4 * e + 2 * m + 1)
                    eng.activation(aa[d][:, m, :], rr[d][:, m, :], ACT.Exp, scale=dec[:, 0, k:k + 1]).then_inc(decay_exp, 1)
                    eng.wait_ge(decay_exp, s + 1)
                    eng.activation(rr[d][:, m, :], rr[d][:, m, :], ACT.Tanh, scale=dec[:, 1, k:k + 1]).then_inc(tanh_r, 1)
                    if s >= 2:
                        eng.wait_ge(v_r, s - 1)
                    eng.activation(a2[m][:, :], aa[d][:, m, :], ACT.Square).then_inc(a_sq, 1)

            def roots(n):
                for e in (2 * n, 2 * n + 1):
                    for m in range(2):
                        eng.wait_ge(v_r, 2 * e + m + 1)
                        eng.activation(rr[e % 2][:, m, :], rr[e % 2][:, m, :], ACT.Sqrt).then_inc(sqrt_r, 1)

            for n in range(NBLK):
                b = AT["in", n, 0]
                splits_to(b + 4)
                conv_start(n, 0)
                splits_to(b + 6)
                if n:
                    decays(n - 1, 1)
                splits_to(b + 7)
                conv_start(n, 1)
                splits_to(b + 8)
                ada_row(16 + 2 * n)
                splits_to(b + 9)
                if n:
                    roots(n - 1)
                conv_hi(n, 0)
                conv_hi(n, 1)
                gelu(n, 0)
                splits_to(b + 11)
                gelu(n, 1)
                if n == NBLK - 1:
                    z_hi_parts(range(KT - 4))
                splits_to(b + 13)
                sigmoids(n, 0)
                splits_to(b + 15)
                if n == NBLK - 1:
                    z_hi_parts(range(KT - 4, KT - 2))
                sigmoids(n, 1)
                splits_to(b + 17)
                ada_row(17 + 2 * n)
                decays(n, 0)
            splits_to(AT["out", 0] + 4)
            decays(NBLK - 1, 1)
            splits_to(AT["out", 0] + 5)
            roots(NBLK - 1)
            for j in range(8):
                splits_to(min(AT["out", j] + 3, AT["ffn", 1] + 1))
                if j == 3:
                    z_hi_parts(range(KT - 2, KT))
            update_norm(2, 3, out_tile,
                        lambda i: splits_to(AT["ffn", 1] + 3) if i == 4 else None)
            splits_to(AT["ffn", 1] + 3)
            norm_affine(3, norm_parts(0))
            ffn(1)
            update_norm(3, None, lambda i: eng.wait_ge(down_add[1], 8 * (HT // 2 - 1) + 2 * i + 2 + ZEROED))

        @block.vector
        def _(eng):
            done = [0]

            def split(n, v=0):
                eng.wait_ge(w_hi, n + 1 + v * 12)
                s = n % RING
                eng.tensor_tensor(wlo[:, s, :], raw[:, s, :], whi[:, s, :].bitcast(F), ALU.subtract).then_inc(w_lo, 1)

            def splits_to(end):
                while done[0] < min(end, CHUNKS):
                    split(done[0])
                    done[0] += 1

            def ada_finish(a):
                li, c = a // 12, a % 12
                m, half = c // 2, c % 2
                eng.wait_ge(ada_out, a + 1)
                if m in (2, 5):
                    gm = m // 3
                    eng.wait_ge(gate_landed[li + li * gm], 64 if li == 0 else 16)
                    for v in range(2 if li == 0 else 1):
                        g = gate[:, v, gm, half * HALF:(half + 1) * HALF]
                        ins = eng.tensor_tensor(g, ps[:, ada_banks(a)[1 - v], :], g, ALU.mult)
                    ins.then_inc(ada_done, 1)
                    return
                idx = m if m < 2 else m - 1
                for v in range(2):
                    src = ps[:, ada_banks(a)[1], 0:8].rearrange("p (t v) -> p v t", v=2)[:, v, :]
                    dst = mod[:, li, idx, 4 * half:4 * half + 4, v]
                    if idx % 2 == 0:
                        ins = eng.tensor_copy(dst, src)
                    else:
                        g0 = C_G + 8 * (2 * li + idx // 2) + 4 * half
                        ins = eng.scalar_tensor_tensor(dst, src, 1.0, cols[:, g0:g0 + 4], ALU.add, ALU.mult)
                ins.then_inc(ada_done, 1)

            def mean(t, src, ssq, number, signal):
                eng.wait_ge(ssq, number + 1)
                eng.tensor_scalar(src[:, 1, t:t + 1], src[:, 0, t:t + 1], 1.0 / D, EPS, ALU.mult, ALU.add).then_inc(signal, 1)

            def update_scale(k, i):
                li, m, tiles = UPDATES[k]
                t = tiles[i]
                eng.wait_ge(u_rstd, UPD0[k] + i + 1)
                if k == 2:
                    def halves(rows):
                        return rows.rearrange("p (h w) -> p h w", h=2)
                    eng.scalar_tensor_tensor(halves(y[:, t, :]), out_banks(i), ustat[:, 2, t:t + 1],
                                             halves(gate[:, 0, m, :]), ALU.mult, ALU.mult).then_inc(u_scaled, 1)
                    return
                eng.scalar_tensor_tensor(y[:, t, :], y[:, t, :], ustat[:, 2, t:t + 1],
                                         gate[:, 1 if t < CT else 0, m, :], ALU.mult, ALU.mult).then_inc(u_scaled, 1)

            def update_norm(ku, kn, adds=lambda i: None, between=lambda i: None):
                li, m, tiles = UPDATES[ku]
                n = len(tiles)
                eng.wait_ge(ada_done, 12 * li + (6 if m == 0 else 12))
                if ku == 0:
                    eng.wait_ge(half_ssq, TT)
                    eng.tensor_scalar(ustat[:, 3, tiles[0]:TT], ustat[:, 3, tiles[0]:TT], 1.0 / D, EPS,
                                      ALU.mult, ALU.add).then_inc(half_mean, 1)
                    eng.wait_ge(half_mean, 1)
                for i in range(n + lag(ku) + 2):
                    between(i)
                    if i < n:
                        adds(i)
                        if ku == 0:
                            t = tiles[i]
                            eng.wait_ge(u_ssq, UPD0[ku] + i + 1)
                            eng.scalar_tensor_tensor(ustat[:, 1, t:t + 1], ustat[:, 0, t:t + 1], 1.0 / D,
                                                     ustat[:, 3, t:t + 1], ALU.mult, ALU.add).then_inc(u_mean, 1)
                        else:
                            mean(tiles[i], ustat, u_ssq, UPD0[ku] + i, u_mean)
                    if 0 <= i - 1 < n:
                        update_scale(ku, i - 1)
                    if kn is not None and 0 <= i - lag(ku) < n:
                        mean(tiles[i - lag(ku)], stat, n_ssq, NORM_ROW0[kn] + i - lag(ku), n_mean)
                    if 0 <= i - 1 < n:
                        t = tiles[i - 1]
                        eng.wait_ge(u_scaled, UPD0[ku] + i)
                        eng.tensor_tensor(x[:, t, :], x[:, t, :], y[:, t, :], ALU.add).then_inc(x_added, 1)

            def norm_split(k, parts):
                def lo_part(grp, ct):
                    (t0, t1), q = NORM_GRP[k][grp], NORM_TR0[k] + KT * grp + ct
                    eng.wait_ge(n_hi, q + 1)
                    eng.tensor_tensor(lo[:, ct, t0 * P:t1 * P], ntmp[:, q % 4, 0:(t1 - t0) * P],
                                      hi[:, ct, t0 * P:t1 * P].bitcast(F), ALU.subtract).then_inc(n_lo, 1)

                for i, (grp, ct) in enumerate(parts):
                    (t0, t1), q = NORM_GRP[k][grp], NORM_TR0[k] + KT * grp + ct
                    eng.wait_ge(n_tmp, q + 1)
                    eng.tensor_copy(hi[:, ct, t0 * P:t1 * P], ntmp[:, q % 4, 0:(t1 - t0) * P]).then_inc(n_hi, 1)
                    if i:
                        lo_part(*parts[i - 1])
                lo_part(*parts[-1])

            def ffn(li):
                b = AT["ffn", li]
                hw = 384 if li == 0 else HALF
                w = TOK if li == 0 else SEQ
                tiles = UPDATES[2 * li + 1][2]
                nd = 2 * len(tiles)

                def product(q, t, par):
                    eng.wait_ge(silu_r[li], q + 1)
                    if li == 0:
                        s, up = sg[:, t, 0:w].rearrange("p (h w) -> p h w", h=2), ps[:, 4 * t + 2:4 * t + 4, 0:hw]
                    else:
                        s, up = sg[:, t, 0:w], ps[:, 4 * t + 2, 0:hw]
                    eng.tensor_tensor(s, s, up, ALU.mult).then_inc(prod_r[li], 1)
                    eng.wait_ge(ahi_r[li], q + 1)
                    eng.tensor_tensor(alo[:, par, t, 0:w], sg[:, t, 0:w], ahi[:, par, t, 0:w].bitcast(F),
                                      ALU.subtract).then_inc(alo_r[li], 1)

                def down_adds(j, last_chunk, v, outputs=range(nd)):
                    for o in outputs:
                        if o < nd - 1:
                            eng.wait_ge(down_mm[li], (nd - 1) * j + o + 1)
                        else:
                            eng.wait_ge(w_used, last_chunk + 1 + v * 12)
                        to = y[:, tiles[o // 2], (o % 2) * HALF:(o % 2 + 1) * HALF]
                        eng.tensor_tensor(to, ps[:, o % 4, :], to, ALU.add).then_inc(down_add[li], 1)

                def step(n0, i, par, v):
                    for k in range(1, 5):
                        split(n0 + k, v)
                    product(2 * i, 0, par)
                    split(n0 + 5, v)
                    split(n0 + 6, v)
                    product(2 * i + 1, 1, par)
                    down_adds(i - 1, n0 + 5, v)

                splits_to(b + 5)
                product(0, 0, 0)
                product(1, 1, 0)
                eng.wait_ge(down_add[li], ZEROED)
                with eng.Fori(0, 5) as v:
                    for s in range(2):
                        step(b + 4 + 6 * s, 1 + s + 2 * v, (1 + s) % 2, v)
                done[0] = b + 65
                splits_to(b + 66)
                return lambda i: down_adds(HT // 2 - 1, b + 65, 0, (2 * i, 2 * i + 1))

            eng.wait_ge(silu_done, 1)
            eng.wait_ge(zeroed, 1)
            sv = silu_c[:, :, :].rearrange("p v k -> p k v")
            eng.tensor_copy(s4[:, :, 0:4:2], sv).then_inc(s4_done, 1)
            eng.wait_ge(s4_done, 1)
            eng.tensor_tensor(s4[:, :, 1:4:2], sv, s4[:, :, 0:4:2].bitcast(F), ALU.subtract).then_inc(s4_done, 1)
            splits_to(3)
            eng.wait_ge(start_tr, 2)
            eng.tensor_copy(cols[:, :], ps[:, 4, 0:NCOL]).then_inc(cols_done, 1)
            eng.wait_ge(cols_done, 1)
            for a in range(4):
                splits_to(AT["ada", a, 3] + (2 if a == 3 else 3))
                if a < 3:
                    mean(2 * a, stat, n_ssq, 2 * a, n_mean)
                    mean(2 * a + 1, stat, n_ssq, 2 * a + 1, n_mean)
                if a:
                    ada_finish(a - 1)
            ada_finish(3)
            norm_split(0, norm_parts(0) + norm_parts(1))

            def rope(cc, last):
                nh = 4 if cc < 2 else 2
                w = nh * P
                eng.wait_ge(rope_landed, 32)
                for i in range(TT - CT):
                    splits_to(min(AT["qkv", 4 * cc + 3] + 3 + i, last + 1))
                    r = 4 * cc + i
                    eng.wait_ge(qkv_moved, (6 * cc + CT + i + 1) if cc < 2 else 12 + 2 * (CT + i) + 1)
                    if cc:
                        eng.wait_ge(qk_tr, 6 * cc)
                    if r >= 2:
                        eng.wait_ge(rope_done, r - 1)
                    src = qraw[:, CT + i, 0:w]
                    c = rc[:, i, :].rearrange("p (o w) -> p o w", o=1).to_broadcast((P, nh, P))
                    eng.tensor_tensor(qrot[:, i, 0:w].rearrange("p (h w) -> p h w", h=nh),
                                      src.rearrange("p (h w) -> p h w", h=nh), c, ALU.mult).then_inc(rope_mul, 1)
                    sv5 = src.rearrange("p (h a s w) -> p s h a w", h=nh, a=2, s=2)
                    tv5 = rtmp[:, r % 2, 0:w].rearrange("p (h a s w) -> p s h a w", h=nh, a=2, s=2)
                    rv = rs[:, i, :].rearrange("p (a s w) -> p s a w", a=2, s=2)
                    for s in range(2):
                        sn = rv[:, s].rearrange("p (o a) w -> p o a w", o=1).to_broadcast((P, nh, 2, 32))
                        eng.tensor_tensor(tv5[:, s], sv5[:, 1 - s], sn, ALU.mult).then_inc(rope_mul, 1)

            for j in range(12):
                splits_to(AT["qkv", j] + 3)
                if j in QKV_RESULT:
                    ada_finish(QKV_RESULT[j])
                if j % 4 == 3:
                    rope(j // 4, AT["qkv", j] + (5 if j < 11 else 3))
            splits_to(AT["qkv", 11] + 4)

            step_no = [0]

            def chain(ins):
                step_no[0] += 1
                ins.then_inc(sp_dve, 1)
                eng.wait_ge(sp_dve, step_no[0])

            lamc = cols[:, C_LAM:C_LAM + 16]
            chain(eng.tensor_scalar(sp[:, 0, :], lamc, -1.0, None, ALU.mult))
            chain(eng.tensor_tensor(sp[:, 0, :], sp[:, 0, :], lamc, ALU.max))
            eng.wait_ge(sp_act, 1)
            chain(eng.tensor_scalar(sp[:, 2, :], sp[:, 1, :], 2.0, None, ALU.add))
            chain(eng.reciprocal(sp[:, 2, :], sp[:, 2, :]))
            chain(eng.tensor_tensor(sp[:, 1, :], sp[:, 1, :], sp[:, 2, :], ALU.mult))
            chain(eng.tensor_tensor(sp[:, 2, :], sp[:, 1, :], sp[:, 1, :], ALU.mult))
            chain(eng.tensor_scalar(sp[:, 3, :], sp[:, 2, :], 2.0 / 17, 2.0 / 15, ALU.mult, ALU.add))
            for k in range(13, 0, -2):
                chain(eng.tensor_tensor(sp[:, 3, :], sp[:, 3, :], sp[:, 2, :], ALU.mult))
                chain(eng.tensor_scalar(sp[:, 3, :], sp[:, 3, :], 2.0 / k, None, ALU.add))
            chain(eng.tensor_tensor(sp[:, 3, :], sp[:, 3, :], sp[:, 1, :], ALU.mult))
            chain(eng.tensor_scalar(sp[:, 4, :], lamc, -1.0, 0.0, ALU.mult, ALU.max))
            chain(eng.tensor_tensor(sp[:, 4, :], sp[:, 4, :], sp[:, 3, :], ALU.add))
            chain(eng.tensor_scalar(dec[:, 0, :], sp[:, 4, :], -8.0, None, ALU.mult))
            chain(eng.tensor_scalar(dec[:, 1, :], sp[:, 4, :], 8.0, None, ALU.mult))

            eng.wait_ge(att_landed, 32)
            eng.tensor_scalar(nsink[:, :], snk[:, :], -1.0, None, ALU.mult).then_inc(s_den, 1)
            eng.wait_ge(s_den, 1)

            def maxima(u):
                t, g, h0, w0, nw = UNITS[u]
                b = u % SR
                eng.wait_ge(s_mm, u + 1)
                if nw:
                    if u >= SR:
                        eng.wait_ge(p_tr, GR0[u - SR + 1])
                    off, w = (w0 - t + 1) * P, nw * P
                    mk = mask[:, off:off + w].rearrange("p (o w) -> p o w", o=1).to_broadcast((P, 2, w))
                    k = 3 * (u % 2) + 1
                    eng.tensor_tensor(S[:, b, :, CTX:CTX + w], ps[:, k:k + 2, 0:w], mk, ALU.add).then_inc(s_win, 1)
                    eng.wait_ge(s_win, u - NCU + 1)
                eng.wait_ge(s_ctx, u + 1)
                eng.tensor_reduce(smx[:, b, :], S[:, b, :, 0:CTX + nw * P], AX, ALU.max).then_inc(s_max, 1)
                eng.wait_ge(s_max, u + 1)
                eng.scalar_tensor_tensor(snm[:, b, :], smx[:, b, :], -SCALE, nsink[:, h0:h0 + 2],
                                         ALU.mult, ALU.min).then_inc(s_neg, 1)
                eng.wait_ge(s_neg, 2 * u + 1)
                eng.tensor_tensor(ses[:, b, :], snk[:, h0:h0 + 2], snm[:, b, :], ALU.add).then_inc(s_neg, 1)

            def normalise(u):
                t, g, h0, w0, nw = UNITS[u]
                b, nk = u % SR, CTX + nw * P
                eng.wait_ge(s_exp, 3 * (u + 1))
                eng.tensor_tensor(ssum[:, b, :], ssum[:, b, :], ses[:, b, :], ALU.add).then_inc(s_den, 1)
                eng.wait_ge(s_den, u + 2)
                eng.reciprocal(sri[:, b, :], ssum[:, b, :]).then_inc(s_inv, 1)
                eng.wait_ge(s_inv, u + 1)
                for h in range(2):
                    eng.tensor_scalar(S[:, b, h, 0:nk], S[:, b, h, 0:nk], sri[:, b, h:h + 1], None, ALU.mult).then_inc(s_prob, 1)

            maxima(0)
            maxima(1)
            normalise(0)
            for un, (t, g, h0, w0, nw) in enumerate(UNITS):
                if un + 1 < NU:
                    normalise(un + 1)
                if un in UNIT_RESULT:
                    ada_finish(UNIT_RESULT[un])
                if un + 2 < NU:
                    maxima(un + 2)
                eng.wait_ge(o_hi, un + 1)
                eng.tensor_tensor(lo[:, h0:h0 + 2, t * P:(t + 1) * P], ps[:, 7, 0:2 * P].rearrange("p (h q) -> p h q", h=2),
                                  hi[:, h0:h0 + 2, t * P:(t + 1) * P].bitcast(F), ALU.subtract).then_inc(o_lo, 1)
                for a, i in UNIT_PIECES.get(un, ()):
                    splits_to(AT["ada", a, i] + 2)

            for j in range(8):
                splits_to(AT["o", j] + 3)
                if j in O_RESULT:
                    ada_finish(O_RESULT[j])
            def between(i):
                if i == 3:
                    splits_to(AT["ada", 15, 3] + 3)
                if i == 4:
                    ada_finish(15)
                if i == 5:
                    splits_to(AT["ffn", 0] + 3)
                if i in (8, 9):
                    norm_split(1, norm_parts(0, 4 * (i - 8), 4 * (i - 7)))

            update_norm(0, 1, between=between)
            norm_split(1, norm_parts(1))
            update_norm(1, 2, ffn(0), lambda i: splits_to(AT["in", 0, 0] + 1) if i == 0 else
                        norm_split(2, norm_parts(0, 4 * (i - 8), 4 * (i - 7))) if i in (8, 9) else None)
            norm_split(2, norm_parts(1, 0, 3))
            splits_to(AT["in", 0, 0] + 3)
            norm_split(2, norm_parts(1, 3))

            def z_lo_parts(tiles):
                for ct in tiles:
                    eng.wait_ge(z_hi, ct + 1)
                    eng.tensor_tensor(lo[:, ct, CTX:TOK], z[:, ct, :], hi[:, ct, CTX:TOK].bitcast(F),
                                      ALU.subtract).then_inc(z_lo, 1)

            def taps(n, j):
                q = 2 * n + j
                k0 = 12 * n + 6 * j
                step = 0
                for k, dt in ((0, -1), (2, 1), (3, 2)):
                    wk = cols[:, C_CW + 8 * k + q:C_CW + 8 * k + q + 1]
                    for s, (t0, t1, src) in enumerate(((0, CTX, ps[:, 2 - 2 * j, 0:CTX]), (CTX, TOK, ps[:, 3 - 2 * j, :]))):
                        w = t1 - t0
                        a, e = max(0, -dt), w - max(0, dt)
                        if step < 2:
                            eng.wait_ge(in_act, 6 * n + 2 * j + s + 1)
                        else:
                            eng.wait_ge(conv, k0 + step - 1)
                        eng.scalar_tensor_tensor(u[:, j, t0 + a:t0 + e], src[:, a + dt:e + dt], wk,
                                                 u[:, j, t0 + a:t0 + e], ALU.mult, ALU.add).then_inc(conv, 1)
                        step += 1

            def inputs(n, d):
                for m in range(2):
                    s = 2 * (2 * n + d) + m
                    eng.wait_ge(a_sq, s + 1)
                    eng.wait_ge(tanh_r, s + 1)
                    eng.scalar_tensor_tensor(rr[d][:, m, :], a2[m][:, :], 1.0, rr[d][:, m, :],
                                             ALU.add, ALU.mult).then_inc(v_r, 1)

            def scans(n, d):
                a, b, h = aa[d], rr[d], ii[d]
                for m in range(2):
                    s = 2 * (2 * n + d) + m
                    eng.wait_ge(sqrt_r, s + 1)
                    eng.wait_ge(iu_r, s + 1)
                    eng.tensor_tensor(b[:, m, :], b[:, m, :], h[:, m, :], ALU.mult).then_inc(b_r, 1)
                    eng.wait_ge(b_r, s + 1)
                    if d == 0:
                        eng.tensor_tensor_scan(h[:, m, 0:CTX], a[:, m, 0:CTX], b[:, m, 0:CTX], 0.0,
                                               ALU.mult, ALU.add).then_inc(scan_r, 1)
                        eng.wait_ge(scan_r, 2 * s + 1)
                        if n:
                            eng.wait_ge(z_r, 2 * n)
                        eng.tensor_tensor_scan(hsum[:, m, :], a[:, m, CTX:TOK], b[:, m, CTX:TOK],
                                               h[:, m, CTX - 1:CTX], ALU.mult, ALU.add).then_inc(scan_r, 1)
                    else:
                        eng.tensor_tensor_scan(h[:, m, 0:CTX][:, ::-1], a[:, m, 0:CTX][:, ::-1],
                                               b[:, m, 0:CTX][:, ::-1], 0.0, ALU.mult, ALU.add).then_inc(scan_r, 1)
                        eng.wait_ge(scan_r, 2 * s + 1)
                        eng.tensor_tensor_scan(h[:, m, CTX:TOK][:, ::-1], a[:, m, CTX:TOK][:, ::-1],
                                               b[:, m, CTX:TOK][:, ::-1], h[:, m, 0:1],
                                               ALU.mult, ALU.add).then_inc(scan_r, 1)

            def conv_lo(n, j):
                eng.wait_ge(u_hi, 2 * n + j + 1)
                eng.tensor_tensor(ulo[:, j, :], u[:, j, :], uhi[:, j, :].bitcast(F), ALU.subtract).then_inc(u_lo, 1)

            for n in range(NBLK):
                b = AT["in", n, 0]
                splits_to(b + 4)
                taps(n, 0)
                splits_to(b + 6)
                if n:
                    ada_finish(15 + 2 * n)
                    inputs(n - 1, 1)
                splits_to(b + 8)
                taps(n, 1)
                splits_to(b + 9)
                conv_lo(n, 0)
                conv_lo(n, 1)
                splits_to(b + 11)
                if n:
                    scans(n - 1, 0)
                ada_finish(16 + 2 * n)
                if n == NBLK - 1:
                    z_lo_parts(range(KT - 4))
                splits_to(b + 13)
                if n:
                    scans(n - 1, 1)
                splits_to(b + 15)
                if n == NBLK - 1:
                    z_lo_parts(range(KT - 4, KT - 2))
                splits_to(b + 17)
                inputs(n, 0)
            splits_to(AT["out", 0] + 4)
            ada_finish(23)
            inputs(NBLK - 1, 1)
            splits_to(AT["out", 0] + 5)
            scans(NBLK - 1, 0)
            splits_to(AT["out", 0] + 6)
            scans(NBLK - 1, 1)
            for j in range(8):
                splits_to(min(AT["out", j] + 3, AT["ffn", 1] + 1))
                if j == 3:
                    z_lo_parts(range(KT - 2, KT))
            update_norm(2, 3, between=lambda i: splits_to(AT["ffn", 1] + 3) if i == 4 else None)
            splits_to(AT["ffn", 1] + 3)
            norm_split(3, norm_parts(0))
            update_norm(3, None, ffn(1))

        @block.gpsimd
        def _(eng):
            def rstd(src, t, means, number, signal):
                eng.wait_ge(means, number + 1)
                eng.tensor_tensor(src[:, 2, t:t + 1], src[:, 1, t:t + 1], mhalf[:, :], ALU.pow).then_inc(signal, 1)

            def update_norm(ku, kn):
                li, m, tiles = UPDATES[ku]
                n = len(tiles)
                for i in range(n + lag(ku) + 2):
                    if i < n:
                        rstd(ustat, tiles[i], u_mean, UPD0[ku] + i, u_rstd)
                    if kn is not None and 0 <= i - lag(ku) < n:
                        rstd(stat, tiles[i - lag(ku)], n_mean, NORM_ROW0[kn] + i - lag(ku), n_rstd)

            eng.memset(s4[:, :, :].bitcast(F), 0.0).then_inc(zeroed, 1)
            eng.memset(mhalf[:, :], -0.5).then_inc(zeroed, 1)
            eng.wait_ge(zeroed, 2)
            for i in range(TT):
                rstd(stat, i, n_mean, i, n_rstd)
                eng.wait_ge(n_rstd, i + 1)
                eng.tensor_scalar(hrow[:, i, :], x[:, i, :], stat[:, 2, i:i + 1], None, ALU.mult).then_inc(n_row, 1)
            for cc in range(3):
                w = HALF if cc < 2 else 2 * P
                for i in range(TT - CT):
                    r = 4 * cc + i
                    eng.wait_ge(rope_mul, 3 * (r + 1))
                    eng.tensor_tensor(qrot[:, i, 0:w], qrot[:, i, 0:w], rtmp[:, r % 2, 0:w], ALU.add).then_inc(rope_done, 1)
            update_norm(0, 1)
            wait_x(eng, 0, 5)
            eng.memset(y[:, :, :], 0.0).then_inc(down_add[0], ZEROED)
            update_norm(1, 2)
            for n in range(NBLK):
                for e in (2 * n, 2 * n + 1):
                    for m in range(2):
                        d = e % 2
                        eng.wait_ge(sig, 4 * e + 2 * m + 2)
                        eng.tensor_tensor(ii[d][:, m, :], ii[d][:, m, :], u[:, m, :], ALU.mult).then_inc(iu_r, 1)
                for m in range(2):
                    eng.wait_ge(scan_r, 8 * n + 4 + 2 * m + 2)
                    eng.tensor_tensor(hsum[:, m, :], hsum[:, m, :], ii[1][:, m, CTX:TOK], ALU.add).then_inc(h_r, 1)
                    eng.wait_ge(h_r, 2 * n + m + 1)
                    eng.wait_ge(in_act, 6 * n + 5 + m)
                    eng.tensor_tensor(z[:, 2 * n + m, :], hsum[:, m, :], z[:, 2 * n + m, :], ALU.mult).then_inc(z_r, 1)
            update_norm(2, 3)
            wait_x(eng, 2, 3)
            eng.memset(y[:, CT:TT, :], 0.0).then_inc(down_add[1], ZEROED)
            update_norm(3, None)

        @block.tensor
        def _(eng):
            def mm3(to, a_hi, a_lo, b_hi, b_lo, start, stop):
                eng.matmul(to, a_hi, b_hi, start=start, stop=False)
                eng.matmul(to, a_hi, b_lo, start=False, stop=False)
                return eng.matmul(to, a_lo, b_hi, start=False, stop=stop)

            def ready(n, v=0):
                eng.wait_ge(w_lo, n + 1 + v * 12)

            def ada_piece(a, j):
                acc, n = ada_banks(a)[0], AT["ada", a, j]
                if j == 0 and a in (5, 6, 11, 12):
                    eng.wait_ge(ada_done, a)
                elif j == 0 and a >= 2:
                    eng.wait_ge(row_moved, a if a >= 4 else a - 1)
                ready(n)
                for kk in range(2):
                    k = 2 * j + kk
                    for part in (whi, wlo):
                        ins = eng.matmul(ps[:, acc, :], s4[:, k, :], part[:, n % RING, kk * HALF:(kk + 1) * HALF],
                                         start=(k == 0 and part is whi), stop=(k == KT - 1 and part is wlo))
                ins.then_inc(w_used, 1)

            def ada_result(a):
                li, c = a // 12, a % 12
                acc, res = ada_banks(a)
                if a:
                    eng.wait_ge(ada_done, a)
                eng.wait_ge(row_moved, a + 1)
                eng.wait_ge(bias_landed[a % 2], 16 * (a // 2 + 1))
                if c // 2 in (2, 5):
                    for v in range(2 if li == 0 else 1):
                        ins = eng.matmul(ps[:, res if v == 0 else acc, :], selb[:, v, :], modrow[:, a % 2, :], start=True, stop=True)
                else:
                    for t in range(4):
                        ins = eng.matmul(ps[:, res, 2 * t:2 * t + 2], modrow[:, a % 2, t * P:(t + 1) * P], selc[:, :],
                                         start=True, stop=True)
                ins.then_inc(ada_out, 1)

            def norm_transposes(k):
                rows, seq = NORM_ROW0[k], NORM_TR0[k]
                for grp, (t0, t1) in enumerate(NORM_GRP[k]):
                    rows += t1 - t0
                    eng.wait_ge(n_row, rows)
                    for ct in range(KT):
                        if k == 2 and grp == 0:
                            if ct >= 4:
                                eng.wait_ge(n_tmp, seq - 3)
                        elif seq >= NORM_TR0[k] + 8:
                            eng.wait_ge(n_tmp, seq - 7)
                        elif k == 1 and ct < TT:
                            eng.wait_ge(y_moved, TT + ct + 1)
                        for t in range(t0, t1):
                            ins = eng.transpose(ps[:, norm_bank(k, grp, ct), (t - t0) * P:(t - t0 + 1) * P],
                                                hrow[:, t, ct * P:(ct + 1) * P], ident[:, :])
                        ins.then_inc(n_tr, 1)
                        seq += 1
                return seq - KT

            def last_chunk(n, tiles, bank, pair):
                for i, t in enumerate(tiles):
                    for kk in range(2):
                        k, w, tok = 2 * pair + kk, slice(kk * HALF, (kk + 1) * HALF), slice(t * P, (t + 1) * P)
                        ins = mm3(ps[:, bank(i), :], hi[:, k, tok], lo[:, k, tok], whi[:, n % RING, w], wlo[:, n % RING, w],
                                  k == 0, k == KT - 1)
                    ins.then_inc(tile_done if i < len(tiles) - 1 else w_used, 1)

            def token_major(name, tiles, acc, bank, mid=lambda: None):
                for j in acc:
                    n = AT[name, j]
                    ready(n)
                    if j % 4 == 3:
                        last_chunk(n, tiles, lambda i: i, 3)
                        return
                    for kk in range(2):
                        k = 2 * (j % 4) + kk
                        if kk:
                            mid()
                        for i, t in enumerate(tiles):
                            bank_no = bank(j, i)
                            h_hi, h_lo = hi[:, k, t * P:(t + 1) * P], lo[:, k, t * P:(t + 1) * P]
                            w = slice(kk * HALF, (kk + 1) * HALF)
                            if k == 0:
                                yield j, i
                            ins = mm3(ps[:, bank_no, :], h_hi, h_lo, whi[:, n % RING, w], wlo[:, n % RING, w],
                                      k == 0, k == KT - 1)
                    ins.then_inc(w_used, 1)

            def channel_major(n, parts, col0=0, v=0, kts=range(KT), src=None, norm_seq=None):
                src_hi, src_lo = src if src else (hi, lo)
                for i, k in enumerate(kts):
                    if norm_seq is not None:
                        eng.wait_ge(n_lo, norm_seq + k + 1)
                    w_h = whi[:, n % RING, col0 + i * P:col0 + (i + 1) * P]
                    w_l = wlo[:, n % RING, col0 + i * P:col0 + (i + 1) * P]
                    for to, tok in parts:
                        ins = mm3(to, w_h, w_l, src_hi[:, k, tok], src_lo[:, k, tok], i == 0, i == len(kts) - 1)
                return ins

            def ffn(li, norm_seq):
                b = AT["ffn", li]
                tiles = UPDATES[2 * li + 1][2]
                nd = 2 * len(tiles)
                cuts = [(0, 384), (384, 768)] if li == 0 else [(CTX, TOK)]

                def up(n0, i, t, v, first):
                    for s in range(2):
                        n = n0 + 2 * t + s
                        ready(n, v)
                        if s == 0 and not first:
                            if t == 0:
                                eng.wait_ge(down_add[li], nd * (i - 1) + ZEROED - (4 - len(cuts)))
                                eng.wait_ge(prod_r[li], 2 * i - 1)
                            else:
                                eng.wait_ge(prod_r[li], 2 * i)
                        if s == 1 and t == 0 and not first:
                            eng.wait_ge(down_add[li], nd * (i - 1) + ZEROED)
                        parts = [(ps[:, 4 * t + 2 * s + k, 0:c1 - c0], slice(c0, c1)) for k, (c0, c1) in enumerate(cuts)]
                        if first and t == 0 and s == 0:
                            eng.wait_ge(n_tmp, norm_seq + 2)
                        channel_major(n, parts, norm_seq=norm_seq if first and t == 0 and s == 0 else None).then_inc(w_used, 1)

                def down(n, j, par, v):
                    ready(n + 1, v)
                    eng.wait_ge(alo_r[li], 2 * j + 2)
                    if not isinstance(j, int) or j < HT // 2 - 1:
                        eng.wait_ge(prod_r[li], 2 * j + 3)
                    for o in range(nd):
                        if o >= 4:
                            eng.wait_ge(down_add[li], nd * j + o - 3 + ZEROED)
                        tk = slice((o // 2) * P, (o // 2 + 1) * P)
                        w = slice((o % 2) * HALF, (o % 2 + 1) * HALF)
                        for t in range(2):
                            s = (n + t) % RING
                            ins = mm3(ps[:, o % 4, :], ahi[:, par, t, tk], alo[:, par, t, tk], whi[:, s, w], wlo[:, s, w],
                                      t == 0, t == 1)
                            if o == nd - 1:
                                ins.then_inc(w_used, 1)
                        if o < nd - 1:
                            ins.then_inc(down_mm[li], 1)

                for t in range(2):
                    up(b, 0, t, 0, True)
                with eng.Fori(0, 5) as v:
                    for s in range(2):
                        n0, i = b + 4 + 6 * s, 1 + s + 2 * v
                        for t in range(2):
                            up(n0, i, t, v, False)
                        down(n0 + 4, s + 2 * v, s, v)
                eng.wait_ge(down_add[li], nd * (HT // 2 - 1) + ZEROED)
                down(b + 64, HT // 2 - 1, 0, 0)

            eng.wait_ge(c_landed, 48)
            eng.transpose(ps[:, 7, 0:16], stage_c[:, :], ident[0:16, 0:16]).then_inc(start_tr, 1)
            eng.wait_ge(s4_done, 2)
            for a in range(4):
                for j in range(4):
                    ada_piece(a, j)
                    if a == 0 and j == 0:
                        eng.wait_ge(cols_landed, 16 * 9)
                        eng.transpose(ps[:, 4, 0:NCOL], stage[:, :], ident[0:NCOL, 0:NCOL]).then_inc(start_tr, 1)
                        eng.wait_ge(sel_landed, 32)
                if a:
                    ada_result(a - 1)
            ada_result(3)
            eng.wait_ge(ada_done, 4)
            seq = norm_transposes(0)

            def qk_transposes(cc):
                nh = 4 if cc < 2 else 2
                eng.wait_ge(ada_done, {0: 7, 1: 9, 2: 9}[cc])
                for t in range(TT):
                    s = 6 * cc + t
                    if t < CT:
                        eng.wait_ge(qkv_moved, 6 * cc + t + 1 if cc < 2 else 12 + 2 * t + 1)
                        src = qraw[:, t, :]
                    else:
                        eng.wait_ge(rope_done, 4 * cc + t - CT + 1)
                        src = qrot[:, t - CT, :]
                    if s >= 2:
                        eng.wait_ge(qk_moved, s - 1)
                    for h in range(nh):
                        ins = eng.transpose(ps[:, 6 + s % 2, h * P:(h + 1) * P], src[:, h * P:(h + 1) * P], ident[:, :])
                    ins.then_inc(qk_tr, 1)

            def result_of(table, j):
                return (lambda: ada_result(table[j])) if j in table else (lambda: None)

            for j in range(12):
                if j < 4:
                    eng.wait_ge(n_lo, seq + 2 * j + 2)
                for jj, i in token_major("qkv", range(TT), [j], lambda j, i: i, result_of(QKV_RESULT, j)):
                    if jj == 0:
                        eng.wait_ge(n_tmp, seq + i + 1)
                    if jj >= 4:
                        eng.wait_ge(qkv_moved, 6 * (jj // 4 - 1) + i + 1)
                if j == 0:
                    eng.wait_ge(n_tmp, seq + KT)
                for a, i in QKV_PIECES.get(j, ()):
                    if (a, i) == (7, 0):
                        eng.wait_ge(qk_moved, 6)
                    ada_piece(a, i)
                if j in QK_TURNS:
                    qk_transposes(QK_TURNS[j])
            qk_transposes(2)

            eng.wait_ge(qkv_moved, 24)
            eng.wait_ge(qk_moved, 18)

            def scores(u):
                t, g, h0, w0, nw = UNITS[u]
                k = 3 * (u % 2)
                if u >= 2:
                    eng.wait_ge(s_ctx, u - 1)
                    if u - 2 >= NCU:
                        eng.wait_ge(s_win, u - 2 - NCU + 1)
                    elif nw:
                        eng.wait_ge(ada_done, 12)
                for h in range(2):
                    q = qT[:, h0 + h, t * P:(t + 1) * P]
                    ins = eng.matmul(ps[:, k, h * CTX:(h + 1) * CTX], q, kT[:, g, 0:CTX], start=True, stop=True)
                    if nw:
                        ins = eng.matmul(ps[:, k + 1 + h, 0:nw * P], q, kT[:, g, w0 * P:(w0 + nw) * P],
                                         start=True, stop=True)
                ins.then_inc(s_mm, 1)

            def turn(u, i):
                q = GR0[u] + i
                if q:
                    eng.wait_ge(p_moved, q)
                for k in range(len(GRPS[u][i])):
                    for h in range(2):
                        ins = eng.transpose(ps[:, 6, (2 * k + h) * P:(2 * k + h + 1) * P],
                                            S[:, u % SR, h, (2 * i + k) * P:(2 * i + k + 1) * P], ident[:, :])
                ins.then_inc(p_tr, 1)

            def values(u, i):
                q, g = GR0[u] + i, UNITS[u][1]
                eng.wait_ge(p_moved, q + 1)
                if i == 0 and u:
                    eng.wait_ge(o_hi, u)
                    eng.wait_ge(o_lo, u)
                for k, kt in enumerate(GRPS[u][i]):
                    ins = eng.matmul(ps[:, 7, 0:2 * P], V[:, kt, g * P:(g + 1) * P], PT[:, q % PR, 2 * k * P:2 * (k + 1) * P],
                                     start=(i == 0 and k == 0), stop=(i == len(GRPS[u]) - 1 and k == len(GRPS[u][i]) - 1))
                ins.then_inc(pv_mm, 1)

            scores(0)
            scores(1)
            for un in range(NU):
                if un in UNIT_RESULT:
                    ada_result(UNIT_RESULT[un])
                eng.wait_ge(s_prob, 2 * (un + 1))
                for i in range(len(GRPS[un])):
                    turn(un, i)
                    if i == 0 and un + 2 < NU:
                        scores(un + 2)
                    if i:
                        values(un, i - 1)
                values(un, len(GRPS[un]) - 1)
                for a, i in UNIT_PIECES.get(un, ()):
                    ada_piece(a, i)

            eng.wait_ge(o_hi, len(UNITS))
            eng.wait_ge(o_lo, len(UNITS))
            for j in range(8):
                for jj, i in token_major("o", range(TT), [j], lambda j, i: i, result_of(O_RESULT, j)):
                    if jj >= 4:
                        eng.wait_ge(y_moved, i + 1)
                for a, i in O_PIECES[j]:
                    ada_piece(a, i)
            ada_result(15)
            eng.wait_ge(ada_done, 16)
            ffn(0, norm_transposes(1))
            norm_seq = norm_transposes(2)
            eng.wait_ge(n_tmp, norm_seq + 4)

            def w_in_tile(n, j):
                c = AT["in", n, j]
                ready(c)
                if j == 1 and n:
                    eng.wait_ge(sig, 8 * n)
                if j == 2 and n == 0:
                    eng.wait_ge(n_tmp, norm_seq + 6)
                if j < 2:
                    parts = [(ps[:, 2 - 2 * j, 0:CTX], slice(0, CTX)), (ps[:, 3 - 2 * j, :], slice(CTX, TOK))]
                else:
                    parts = [(ps[:, 2 + j, :], slice(CTX, TOK))]
                channel_major(c, parts, norm_seq=norm_seq if n == 0 and j == 0 else None).then_inc(w_used, 1)

            def gates(n, d):
                c, e = AT["bd", n, d], 2 * n + d
                eng.wait_ge(u_lo, 2 * n + 2)
                ready(c)
                for m in range(2):
                    for g in range(2):
                        s = 4 * e + 2 * m + g
                        if s >= 2:
                            eng.wait_ge(sig, s - 1)
                        for k in range(2):
                            at_w = (2 * g + k) * 2 * P + m * P
                            w_h, w_l = whi[:, c % RING, at_w:at_w + P], wlo[:, c % RING, at_w:at_w + P]
                            for to, tok in ((ps[:, 4 * g, 0:384], slice(0, 384)),
                                            (ps[:, 4 * g + 1, 0:384], slice(384, 768))):
                                ins = mm3(to, w_h, w_l, uhi[:, k, tok], ulo[:, k, tok], k == 0, k == 1)
                        ins.then_inc(bd_mm if 2 * m + g < 3 else w_used, 1)

            for n in range(NBLK):
                for step in RG_STREAM:
                    if step[0] == "ada":
                        ada_piece(16 + 2 * n + step[1], step[2])
                    elif step[0] == "bd":
                        if step[1] == 0:
                            eng.wait_ge(in_act, 6 * n + 6)
                        gates(n, step[1])
                    else:
                        w_in_tile(n, step[1])
                        if step[1] == 0 and n:
                            ada_result(15 + 2 * n)
                        if step[1] == 2:
                            ada_result(16 + 2 * n)
            eng.wait_ge(sig, 4 * 2 * NBLK)
            for jj, (half, pair) in enumerate(OUT_ORDER):
                if jj == 1:
                    ada_result(23)
                if jj == 3:
                    eng.wait_ge(ada_done, 24)
                if half == 0 or pair == 3:
                    eng.wait_ge(z_lo, 2 * pair + 2)
                n = AT["out", jj]
                ready(n)
                if jj == 6:
                    ready(n + 1)
                    for i in range(4):
                        tok = slice((CT + i) * P, (CT + i + 1) * P)
                        for h in range(2):
                            c = n + h
                            for k in range(KT - 2, KT):
                                w = slice((k % 2) * HALF, (k % 2 + 1) * HALF)
                                ins = mm3(ps[:, 2 * i + h, :], hi[:, k, tok], lo[:, k, tok], whi[:, c % RING, w],
                                          wlo[:, c % RING, w], False, k == KT - 1)
                            if i == 3:
                                ins.then_inc(w_used, 1)
                        if i < 3:
                            ins.then_inc(tile_done, 1)
                    break
                for kk in range(2):
                    k, w = 2 * pair + kk, slice(kk * HALF, (kk + 1) * HALF)
                    for i in range(4):
                        tok = slice((CT + i) * P, (CT + i + 1) * P)
                        if jj == 0 and kk == 0 and i == 3:
                            eng.wait_ge(row_moved, 24)
                        ins = mm3(ps[:, 2 * i + half, :], hi[:, k, tok], lo[:, k, tok], whi[:, n % RING, w], wlo[:, n % RING, w],
                                  k == 0, k == KT - 1)
                ins.then_inc(w_used, 1)
            ffn(1, norm_transposes(3))


_TRUNK_INS = ["x", "c", "ctx", "c_ctx", "ada_w", "ada_b", "norm_g", "ffn_w_gu", "ffn_w_down", "a_w_qkv", "a_sinks",
              "a_w_o", "b_w_in", "b_conv_w", "b_conv_b", "b_lam", "b_w_a", "b_b_a", "b_w_x", "b_b_x", "b_w_out"]


def shape_constants():
    pos = np.arange(SEQ)
    inv = (1.0 / (np.float32(ROPE_BASE) ** (np.arange(0, 64, 2, dtype=np.float32) / np.float32(64)))).astype(np.float32)
    ang = np.stack([(pos // GRID_W).astype(np.float32)[:, None] * inv, (pos % GRID_W).astype(np.float32)[:, None] * inv], 1)
    cos, sin = np.cos(ang), np.sin(ang)
    c = np.stack([cos, cos], 2).reshape(SEQ // P, P, P).transpose(1, 0, 2)
    s = np.stack([-sin, sin], 2).reshape(SEQ // P, P, P).transpose(1, 0, 2)
    i, j = np.arange(P)[:, None], np.arange(3 * P)[None, :]
    mask = np.where(np.abs(j - P - i) <= P, 0.0, NEG)
    sel = np.zeros((5, 2, P))
    sel[[0, 1, 4], 0] = 1.0
    sel[[2, 3, 4], 1] = 1.0
    made = {"rope_c": c, "rope_s": s, "win_mask": mask, "eye": np.eye(P), "sel": sel, "sel_c": sel[:, :, 0]}
    return {k: np.ascontiguousarray(v, dtype=np.float32) for k, v in made.items()}


def kernel(**inputs):
    import concourse.bacc as bacc
    from concourse.bass_utils import run_bass_kernel_spmd

    nc = bacc.Bacc("TRN2", target_bir_lowering=False, num_devices=1)
    arrays, args = {}, []
    for name in _TRUNK_INS:
        arrays[f"in_{name}"] = np.ascontiguousarray(inputs[name])
    arrays.update({f"const_{k}": v for k, v in shape_constants().items()})
    for name, a in arrays.items():
        args.append(nc.dram_tensor(name, a.shape, mybir.dt.from_np(a.dtype), kind="ExternalInput").ap())
    args.append(nc.dram_tensor("out_latents", (1, SEQ, D), F, kind="ExternalOutput").ap())
    trunk(nc, *args)
    r = run_bass_kernel_spmd(nc, [arrays], core_ids=[0])
    return r.results[0]["out_latents"]
```
